# Optimizing a Trainium2 kernel written in Bass

```python
import math, functools
import jax, jax.numpy as jnp
from jax import lax
import numpy as np

D_MODEL = 1024
BATCH = 1
SEQ = 1024
DEPTH = 1
DEC_BATCH = 8
DEC_SEQ = 1
PAST_LEN = 512
PAGE_SIZE = 128

A_HEADS = 8
A_DH = 64
A_DV = 2 * A_DH
B_HEADS = 8
B_DK = 128
B_DV = 128
D_FF = 2816
CONV_W = 3
ROPE_THETA = 10000.0
Q_BLOCK = 128
B_CHUNK = 64
EPS = 1e-6

A_QK_W = A_HEADS * 2 * A_DH
A_V_W = A_HEADS * A_DV
B_K_W = B_HEADS * B_DK
B_V_W = B_HEADS * B_DV
IN_SIZES = (A_QK_W, A_QK_W, A_V_W, B_K_W, B_K_W, B_V_W, B_V_W, D_MODEL, D_MODEL)
IN_W = sum(IN_SIZES)

kernel_name = "hybrid_diffattn_hgrn2_convffn_step"

F32 = jnp.float32

def rmsnorm(x, g):
    xf = x.astype(F32)
    xf = xf * lax.rsqrt(jnp.mean(xf * xf, axis=-1, keepdims=True) + EPS)
    return xf.astype(x.dtype) * g

def rope(x, pos):
    half = A_DH // 2
    inv = ROPE_THETA ** (-jnp.arange(half, dtype=F32) / half)
    ang = pos.astype(F32)[:, None] * inv[None, :]
    cos = jnp.cos(ang)[:, None, None, :]
    sin = jnp.sin(ang)[:, None, None, :]
    xf = x.astype(F32)
    x1, x2 = xf[..., :half], xf[..., half:]
    return jnp.concatenate([x1 * cos - x2 * sin, x2 * cos + x1 * sin], axis=-1).astype(x.dtype)

def split_in(z):
    offs = [int(o) for o in np.cumsum(IN_SIZES)[:-1]]
    return jnp.split(z, offs, axis=-1)

def diff_probs(s, lam):
    p = jax.nn.softmax(s, axis=-1)
    return p[:, :, 0] - lam * p[:, :, 1]

def attend_prompt(q, k, v, lam):
    b, t = q.shape[:2]
    nblk = t // Q_BLOCK
    scale = A_DH ** -0.5
    qb = q.reshape(b, nblk, Q_BLOCK, A_HEADS, 2, A_DH).swapaxes(0, 1)
    kpos = jnp.arange(t)

    def blk(args):
        qi, i = args
        qpos = i * Q_BLOCK + jnp.arange(Q_BLOCK)
        s = jnp.einsum('bqhcd,bkhcd->bhcqk', qi, k).astype(F32) * scale
        s = jnp.where(kpos[None, :] <= qpos[:, None], s, -jnp.inf)
        p = diff_probs(s, lam)
        return jnp.einsum('bhqk,bkhv->bqhv', p.astype(v.dtype), v)

    o = lax.map(blk, (qb, jnp.arange(nblk)))
    return o.swapaxes(0, 1).reshape(b, t, A_HEADS, A_DV)

def attend_sample(q, k, v, lam, k_past, v_past):
    tn = q.shape[1]
    p_len = k_past.shape[1]
    scale = A_DH ** -0.5
    s_past = jnp.einsum('bqhcd,bkhcd->bhcqk', q, k_past).astype(F32) * scale
    s_new = jnp.einsum('bqhcd,bkhcd->bhcqk', q, k).astype(F32) * scale
    causal = jnp.tril(jnp.ones((tn, tn), bool))
    s_new = jnp.where(causal, s_new, -jnp.inf)
    p = diff_probs(jnp.concatenate([s_past, s_new], axis=-1), lam).astype(v.dtype)
    return (jnp.einsum('bhqk,bkhv->bqhv', p[..., :p_len], v_past)
            + jnp.einsum('bhqk,bkhv->bqhv', p[..., p_len:], v))

def hgrn_chunked(q, k, g, v, s0):
    b, t = q.shape[:2]
    n = t // B_CHUNK
    tri = jnp.tril(jnp.ones((B_CHUNK, B_CHUNK), bool))[None, :, :, None, None]

    def to_chunks(a):
        return a.reshape(b, n, B_CHUNK, *a.shape[2:]).swapaxes(0, 1)

    def step(S, inp):
        qc, kc, gc, vc = inp
        cum = jnp.cumsum(gc, axis=1)
        rel = cum[:, :, None] - cum[:, None, :]
        decay = jnp.exp(jnp.where(tri, rel, -jnp.inf))
        A = jnp.einsum('bthk,btshk,bshk->bhts', qc, decay, kc)
        o = (jnp.einsum('bhts,bshv->bthv', A, vc)
             + jnp.einsum('bthk,bhkv->bthv', qc * jnp.exp(cum), S))
        last = cum[:, -1]
        S_new = (jnp.exp(last)[..., None] * S
                 + jnp.einsum('bshk,bshv->bhkv', kc * jnp.exp(last[:, None] - cum), vc))
        return S_new, o

    S, o = lax.scan(step, s0, (to_chunks(q), to_chunks(k), to_chunks(g), to_chunks(v)))
    return o.swapaxes(0, 1).reshape(b, t, B_HEADS, B_DV), S

def hgrn_steps(q, k, g, v, s0):
    def step(S, inp):
        qt, kt, gt, vt = inp
        S = jnp.exp(gt)[..., None] * S + kt[..., None] * vt[..., None, :]
        return S, jnp.einsum('bhk,bhkv->bhv', qt, S)

    S, o = lax.scan(step, s0, (q.swapaxes(0, 1), k.swapaxes(0, 1), g.swapaxes(0, 1), v.swapaxes(0, 1)))
    return o.swapaxes(0, 1), S

def token_mixer(xn, pos, p, attend, recur):
    b, t = xn.shape[:2]
    qa, ka, va, qb, fb, ib, ogb, ga, gb = split_in(xn @ p['w_in'])
    qa = rope(rmsnorm(qa.reshape(b, t, A_HEADS, 2, A_DH), p['q_norm_g']), pos)
    ka = rope(rmsnorm(ka.reshape(b, t, A_HEADS, 2, A_DH), p['k_norm_g']), pos)
    va = va.reshape(b, t, A_HEADS, A_DV)
    oa = attend(qa, ka, va, p['lam'])
    oa = rmsnorm(oa, p['subln_g']) * (1.0 - p['lam_init'])
    qh = jax.nn.silu(qb.astype(F32)).reshape(b, t, B_HEADS, B_DK)
    lb = p['lb']
    f = lb + (1.0 - lb) * jax.nn.sigmoid(fb.astype(F32))
    kh = (1.0 - f).reshape(b, t, B_HEADS, B_DK)
    gh = jnp.log(f).reshape(b, t, B_HEADS, B_DK)
    vh = ib.astype(F32).reshape(b, t, B_HEADS, B_DV)
    ob, s_new = recur(qh, kh, gh, vh)
    ob = rmsnorm(ob, p['hgrn_norm_g']) * jax.nn.silu(ogb.astype(F32).reshape(b, t, B_HEADS, B_DV))
    ob = ob.astype(xn.dtype)
    ya = oa.reshape(b, t, A_V_W) @ p['w_branch_a']
    yb = ob.reshape(b, t, B_V_W) @ p['w_branch_b']
    merged = jax.nn.sigmoid(ga) * ya + jax.nn.sigmoid(gb) * yb
    return merged @ p['w_out'], ka, va, s_new

def conv_ffn(hn, buf, p):
    t = hn.shape[1]
    u = hn @ p['w_up']
    full = jnp.concatenate([buf.astype(u.dtype), u], axis=1)
    y = p['conv_b']
    for j in range(CONV_W):
        y = y + p['conv_w'][j] * full[:, j:j + t]
    a, g = jnp.split(y, 2, axis=-1)
    return (jax.nn.silu(a) * g) @ p['w_down'], full[:, -(CONV_W - 1):]

def layer_step(x, c, pos, p, attend, recur, conv_buf):
    mod = jax.nn.silu(c) @ p['w_ada'] + p['b_ada']
    sh_m, sc_m, g_m, sh_f, sc_f, g_f = [m[:, None, :] for m in jnp.split(mod, 6, axis=-1)]
    xn = rmsnorm(x, p['rms_mix_g']) * (1.0 + sc_m) + sh_m
    mix, k_rows, v_rows, s_new = token_mixer(xn, pos, p, attend, recur)
    x = x + g_m * mix
    hn = rmsnorm(x, p['rms_ffn_g']) * (1.0 + sc_f) + sh_f
    ffn, buf_new = conv_ffn(hn, conv_buf, p)
    x = x + g_f * ffn
    return x, k_rows, v_rows, s_new, buf_new

def setup_inputs(seed: int = 0) -> dict:
    key = jax.random.key(seed)
    keys = list(jax.random.split(key, 40))

    def nrm(shape, s):
        return s * jax.random.normal(keys.pop(), shape, F32)

    n_pages = PAST_LEN // PAGE_SIZE
    n_used = DEC_BATCH * n_pages
    n_pool = n_used + (n_used + 3) // 4
    page_table = jax.random.permutation(keys.pop(), n_pool)[:n_used].reshape(DEC_BATCH, n_pages).astype(jnp.int32)
    d = D_MODEL
    return {
        'x_prompt': nrm((BATCH, SEQ, d), 1.0),
        'x_sample': nrm((DEC_BATCH, DEC_SEQ, d), 1.0),
        'cache_k': nrm((DEPTH, n_pool, PAGE_SIZE, A_HEADS, 2, A_DH), 1.0),
        'cache_v': nrm((DEPTH, n_pool, PAGE_SIZE, A_HEADS, A_DV), 1.0),
        'state_hgrn': nrm((DEPTH, DEC_BATCH, B_HEADS, B_DK, B_DV), 0.5),
        'state_conv': nrm((DEPTH, DEC_BATCH, CONV_W - 1, 2 * D_FF), 1.0),
        'page_table': page_table,
        'c_prompt': nrm((BATCH, d), 1.0),
        'c_sample': nrm((DEC_BATCH, d), 1.0),
        'w_ada': nrm((DEPTH, d, 6 * d), 0.5 * d ** -0.5),
        'b_ada': nrm((DEPTH, 6 * d), 0.01),
        'rms_mix_g': 1.0 + nrm((DEPTH, d), 0.02),
        'w_in': nrm((DEPTH, d, IN_W), d ** -0.5),
        'q_norm_g': 1.0 + nrm((DEPTH, A_DH), 0.02),
        'k_norm_g': 1.0 + nrm((DEPTH, A_DH), 0.02),
        'lambda_q1': nrm((DEPTH, A_DH), 0.1),
        'lambda_k1': nrm((DEPTH, A_DH), 0.1),
        'lambda_q2': nrm((DEPTH, A_DH), 0.1),
        'lambda_k2': nrm((DEPTH, A_DH), 0.1),
        'subln_g': 1.0 + nrm((DEPTH, A_DV), 0.02),
        'lb_logits': nrm((DEPTH + 1, B_K_W), 0.1),
        'hgrn_norm_g': 1.0 + nrm((DEPTH, B_DV), 0.02),
        'w_branch_a': nrm((DEPTH, A_V_W, d), A_V_W ** -0.5),
        'w_branch_b': nrm((DEPTH, B_V_W, d), B_V_W ** -0.5),
        'w_out': nrm((DEPTH, d, d), d ** -0.5),
        'rms_ffn_g': 1.0 + nrm((DEPTH, d), 0.02),
        'w_up': nrm((DEPTH, d, 2 * D_FF), d ** -0.5),
        'conv_w': nrm((DEPTH, CONV_W, 2 * D_FF), CONV_W ** -0.5),
        'conv_b': nrm((DEPTH, 2 * D_FF), 0.01),
        'w_down': nrm((DEPTH, D_FF, d), D_FF ** -0.5),
    }

def reference(x_prompt, x_sample, cache_k, cache_v, state_hgrn, state_conv, page_table, c_prompt, c_sample,
              w_ada, b_ada, rms_mix_g, w_in, q_norm_g, k_norm_g, lambda_q1, lambda_k1, lambda_q2, lambda_k2,
              subln_g, lb_logits, hgrn_norm_g, w_branch_a, w_branch_b, w_out, rms_ffn_g, w_up, conv_w, conv_b,
              w_down):
    bp, tp = x_prompt.shape[:2]
    bs, ts = x_sample.shape[:2]
    past_len = page_table.shape[1] * cache_k.shape[2]
    pos_p = jnp.arange(tp)
    pos_s = past_len + jnp.arange(ts)
    lb_all = jnp.cumsum(jax.nn.softmax(lb_logits.astype(F32), axis=0), axis=0)

    xp, xs = x_prompt, x_sample
    nk_p, nv_p, ns_p, nc_p = [], [], [], []
    nk_s, nv_s, ns_s, nc_s = [], [], [], []
    for l in range(DEPTH):
        lam_init = 0.8 - 0.6 * math.exp(-0.3 * l)
        lam = (jnp.exp(jnp.sum(lambda_q1[l].astype(F32) * lambda_k1[l].astype(F32)))
               - jnp.exp(jnp.sum(lambda_q2[l].astype(F32) * lambda_k2[l].astype(F32))) + lam_init)
        p = {
            'w_ada': w_ada[l], 'b_ada': b_ada[l], 'rms_mix_g': rms_mix_g[l], 'w_in': w_in[l],
            'q_norm_g': q_norm_g[l], 'k_norm_g': k_norm_g[l], 'lam': lam, 'lam_init': lam_init,
            'subln_g': subln_g[l], 'lb': lb_all[l], 'hgrn_norm_g': hgrn_norm_g[l],
            'w_branch_a': w_branch_a[l], 'w_branch_b': w_branch_b[l], 'w_out': w_out[l],
            'rms_ffn_g': rms_ffn_g[l], 'w_up': w_up[l], 'conv_w': conv_w[l], 'conv_b': conv_b[l],
            'w_down': w_down[l],
        }
        s0 = jnp.zeros((bp, B_HEADS, B_DK, B_DV), F32)
        buf0 = jnp.zeros((bp, CONV_W - 1, 2 * D_FF), xp.dtype)
        xp, kp, vp, sp, cp = layer_step(xp, c_prompt, pos_p, p, attend_prompt,
                                        functools.partial(hgrn_chunked, s0=s0), buf0)
        k_past = cache_k[l][page_table].reshape(bs, past_len, A_HEADS, 2, A_DH)
        v_past = cache_v[l][page_table].reshape(bs, past_len, A_HEADS, A_DV)
        xs, ks, vs, ss, cs = layer_step(xs, c_sample, pos_s, p,
                                        functools.partial(attend_sample, k_past=k_past, v_past=v_past),
                                        functools.partial(hgrn_steps, s0=state_hgrn[l].astype(F32)),
                                        state_conv[l])
        nk_p.append(kp); nv_p.append(vp); ns_p.append(sp.astype(state_hgrn.dtype)); nc_p.append(cp)
        nk_s.append(ks); nv_s.append(vs); ns_s.append(ss.astype(state_hgrn.dtype)); nc_s.append(cs)

    return (xp, xs,
            jnp.stack(nk_p), jnp.stack(nv_p), jnp.stack(ns_p), jnp.stack(nc_p),
            jnp.stack(nk_s), jnp.stack(nv_s), jnp.stack(ns_s), jnp.stack(nc_s))


_drawn_inputs = setup_inputs


def setup_inputs(seed=0):
    import zlib

    import numpy as np

    out = dict(_drawn_inputs(seed))
    spreads = {}
    factors = {'b_ada': 2.749,
     'rms_mix_g': 2.771,
     'q_norm_g': 8.0,
     'k_norm_g': 2.874,
     'lambda_q1': 3.695,
     'lambda_k1': 5.452,
     'lambda_q2': 8.0,
     'lambda_k2': 8.0,
     'subln_g': 58.442,
     'hgrn_norm_g': 23.809,
     'rms_ffn_g': 8.817,
     'conv_b': 24.797}
    for name, (base, spread) in spreads.items():
        noise = np.random.default_rng([zlib.crc32(name.encode()), seed]).standard_normal(out[name].shape)
        drawn = base * np.exp(spread * noise) if base else spread * noise
        out[name] = __import__('jax').numpy.asarray(drawn.astype(out[name].dtype))
    for name, factor in factors.items():
        out[name] = (out[name] * factor).astype(out[name].dtype)
    return out
```

```python
from contextlib import ExitStack

import concourse.bass as bass
import numpy as np
from concourse import mybir

F32 = mybir.dt.float32
F32R = mybir.dt.float32r
U32 = mybir.dt.uint32
I32 = mybir.dt.int32
ALU = mybir.AluOpType
ACT = mybir.ActivationFunctionType
AX = mybir.AxisListType

P = 128
D = 1024
T = 1024
NS = 8
NT = T + NS
NP = 3
TH = NT // NP
KT = D // P
H = 8
DH = 64
NB = T // P
PAST = 512
PAGES = PAST // P
POOL_PAGES = 40
FF = 2816
FT = FF // P
GROUPS = ((0, 8), (8, 8), (16, 6))
LEVELS = 7
HALF = P // 2
EPS = 1e-6
SCALE = DH ** -0.5
LAM_INIT = 0.2
BIG = 1e18
TABLES = "natural_log_exp_and_others"
FIRST_SEM, STAGE_SEMS = 99, 78
CS = NS + 1

VEC, _at = {}, 0
for _n, _w in (("b_ada", 6 * KT), ("mix_g", KT), ("ffn_g", KT), ("q_g", 1), ("k_g", 1), ("sub_g", 1), ("hgrn_g", 1),
               ("lb", 2 * H), ("conv_w", 3 * 2 * FT), ("conv_b", 2 * FT), ("lam", 4 * DH)):
    VEC[_n] = (_at, _w)
    _at += _w
VEC_W = _at
BASE = 16512
KEEP_END = BASE + 9 * 1024
WIDE = KT * NT * 4
R1 = KEEP_END
R2 = R1 + 2 * WIDE
TOP = 229344
R3 = TOP - 2 * WIDE


def cols(j):
    return slice(j * TH, (j + 1) * TH)


class Stage(ExitStack):

    def __init__(self, c):
        super().__init__()
        self.last, c["stage"] = c.get("stage"), self
        self.first = FIRST_SEM if self.last is None or self.last.first != FIRST_SEM else FIRST_SEM + STAGE_SEMS
        self.n = 0

    def semaphore(self, nc, name):
        self.n += 1
        assert self.n <= STAGE_SEMS, name
        return self.enter_context(nc.semaphore(name, num=self.first + self.n - 1))

    def clear_last(self, eng):
        if self.last is not None:
            eng.sem_clear(range(self.last.first, self.last.first + self.last.n))


class Sig:

    def __init__(self, ctx, nc, name, per=0, pre=0, init=0, step=1):
        self.sem = ctx.semaphore(nc, name)
        self.per, self.pre, self.init, self.step, self.name = per, pre, init, step, name

    def start(self, eng):
        eng.sem_inc(self.sem, self.init * self.step)

    def at(self, turn, k):
        least = self.init + self.pre + k
        assert least + (self.per * turn if isinstance(turn, int) else 0) > 0, (self.name, turn, k)
        return turn * (self.per * self.step) + self.step * least

    def before(self, k):
        assert self.init + k > 0, (self.name, k)
        return self.step * (self.init + k)


class Chain:

    def __init__(self, ctx, nc, eng, name):
        self.sem, self.eng, self.n = ctx.semaphore(nc, name), eng, 0

    def __call__(self, ins):
        self.n += 1
        ins.then_inc(self.sem, 1)

    def sync(self):
        if self.n:
            self.eng.wait_ge(self.sem, self.n)

    def reset(self):
        if self.n:
            self.sync()
            self.eng.sem_clear(self.sem)
            self.n = 0


class Memory:

    def __init__(self, nc, name, at, end=TOP):
        self.nc, self.name, self.off, self.end = nc, name, at, end

    def __call__(self, name, shape, dt=F32):
        t = self.nc.alloc_sbuf_tensor_at(f"{self.name}_{name}", shape, dt, offset=self.off)
        self.off += -(-int(np.prod(shape[1:])) * 4 // 32) * 32
        assert self.off <= self.end, (self.name, name, self.off - self.end)
        return t


def product(eng, out, whi, wlo, xhi, xlo, n_k, columns):
    for k in range(n_k):
        for n, (w, x) in enumerate(((whi, xhi), (whi, xlo), (wlo, xhi))):
            ins = eng.matmul(out, w[:, k * P:(k + 1) * P], x[:, k, columns],
                             start=(k == 0 and n == 0), stop=(k == n_k - 1 and n == 2))
    return ins


class Stream:

    def __init__(self, ctx, nc, mem, name, n_k=KT):
        self.n_k, w = n_k, n_k * P
        self.raw = [mem(f"w_raw{s}", [P, w]) for s in range(2)]
        self.hi = [mem(f"w_hi{s}", [P, w], F32R) for s in range(2)]
        self.lo = [mem(f"w_lo{s}", [P, w], F32R) for s in range(2)]
        self.ps = ctx.enter_context(nc.psum_tensor(f"{name}_ps", [P, 6, 512], F32))
        self.loaded = [Sig(ctx, nc, f"{name}_w_loaded{s}", per=1, step=16) for s in range(2)]
        self.hi_done = Sig(ctx, nc, f"{name}_w_hi_done", per=2, init=2)
        self.lo_done = Sig(ctx, nc, f"{name}_w_lo_done", per=2, init=2)
        self.done = Sig(ctx, nc, f"{name}_piece_done", per=6, init=6)
        self.free = Sig(ctx, nc, f"{name}_piece_free", per=6, init=6)

    def load(self, sp, turn, s, src):
        sp.wait_ge(self.hi_done.sem, self.hi_done.at(turn, s - 1))
        sp.wait_ge(self.lo_done.sem, self.lo_done.at(turn, s - 1))
        sp.dma_start(self.raw[s][:, :], src).then_inc(self.loaded[s].sem, 16)

    def split_hi(self, act, turn, s):
        act.wait_ge(self.loaded[s].sem, self.loaded[s].at(turn, 1))
        act.wait_ge(self.done.sem, self.done.at(turn, 3 * s - 3))
        act.activation(self.hi[s][:, :], self.raw[s][:, :], ACT.Copy).then_inc(self.hi_done.sem, 1)

    def split_lo(self, pool, turn, s):
        pool.wait_ge(self.loaded[s].sem, self.loaded[s].at(turn, 1))
        pool.wait_ge(self.hi_done.sem, self.hi_done.at(turn, s + 1))
        pool.wait_ge(self.done.sem, self.done.at(turn, 3 * s - 3))
        pool.tensor_tensor(self.lo[s][:, :], self.raw[s][:, :], self.hi[s][:, :].bitcast(F32), ALU.subtract)\
            .then_inc(self.lo_done.sem, 1)

    def piece(self, pe, turn, s, j, xhi, xlo):
        if j == 0:
            pe.wait_ge(self.hi_done.sem, self.hi_done.at(turn, s + 1))
            pe.wait_ge(self.lo_done.sem, self.lo_done.at(turn, s + 1))
        pe.wait_ge(self.free.sem, self.free.at(turn, 3 * s + j - 5))
        product(pe, self.ps[:, 3 * s + j, 0:TH], self.hi[s], self.lo[s], xhi, xlo, self.n_k, cols(j))\
            .then_inc(self.done.sem, 1)

    def wait_piece(self, eng, turn, s, j):
        eng.wait_ge(self.done.sem, self.done.at(turn, 3 * s + j + 1))

    def out(self, s, j):
        return self.ps[:, 3 * s + j, 0:TH]

    def head_start(self, pe=None, act=None, pool=None, reader=None):
        for eng, sig in ((pe, self.done), (act, self.hi_done), (pool, self.lo_done), (reader, self.free)):
            if eng is not None:
                sig.start(eng)


def turns(eng, n, body):
    with eng.Fori(0, n - 1) as i:
        body(i, False)
    body(n - 1, True)


def copy(dve, out, src):
    return dve.tensor_scalar(out, src, 1.0, None, ALU.mult)


def flat(ap):
    return ap.rearrange("o p n -> p (o n)")


def norm_stage(nc, a, c, x, hi, lo, mem, first):
    name = "norm1" if first else "norm2"
    shift, scale, gain = (0, KT, VEC["mix_g"][0]) if first else (3 * KT, 4 * KT, VEC["ffn_g"][0])
    n_ada = 2 * KT if first else 0
    RING = 4
    with Stage(c) as ctx:
        sq = [mem(f"sq{i}", [P, NT]) for i in range(2)]
        rs = mem("rs", [P, NT])
        y = [mem(f"y{i}", [P, NT]) for i in range(2)]
        ps = ctx.enter_context(nc.psum_tensor(f"{name}_ms", [P, NP, 512], F32))
        S = lambda n, **k: Sig(ctx, nc, f"{name}_{n}", **k)
        x_in = [S(f"x_in{k}", step=16) for k in range(KT)]
        squared, used, summed, lnd, rstd = S("squared"), S("sq_used"), S("ms_summed"), S("ln"), S("rstd")
        normed, high, low, stored = S("normed"), S("hi_done"), S("lo_done"), S("x_stored", step=16)
        if first:
            aw = [mem(f"ada_w{i}", [P, KT * P]) for i in range(RING)]
            cx = mem("cx", [P, KT, CS])
            tmp = mem("tmp", [P, 2, DH])
            lw = mem("lw", [P, 6, H])
            pa = ctx.enter_context(nc.psum_tensor(f"{name}_ada", [P, RING, 512], F32))
            kept, cond, ada_in = S("kept_in", step=16), S("c_in", step=16), [S(f"ada_in{i}", step=16) for i in range(RING)]
            ada_done, ada_read, silu_e, csil = S("ada_done"), S("ada_read"), S("silu_e"), S("csil")
            lam_s, lam_e, lb_s, lb_e = S("lam_s"), S("lam_e"), S("lb_s"), S("lb_e")
            vec_in, N_KEPT = S("vec_in", step=16), 3
        mods, mean_in, mean = S("mods_ready"), S("mean_in", step=16), mem("mean", [P, P])
        block = ctx.enter_context(nc.Block())

        @block.sync
        def _(sp):
            sp.dma_start(mean[:, :], a["ones1024"]).then_inc(mean_in.sem, 16)
            if first:
                sp.dma_start(cx[:, :, :], a["cT"]).then_inc(cond.sem, 16)
                sp.dma_start(c["vec"][:, :], a["vec"]).then_inc(vec_in.sem, 16)
                for k in range(KT):
                    sp.dma_start(x[:, k, :], a["xT"][:, k, :]).then_inc(x_in[k].sem, 16)
                for t in range(n_ada):
                    if t >= RING:
                        sp.wait_ge(ada_done.sem, ada_done.before(t - RING + 1))
                    sp.dma_start(aw[t % RING][:, :], flat(a["w_ada"][t:t + 1])).then_inc(ada_in[t % RING].sem, 16)
                for n in ("ident", "ones128", "ones"):
                    sp.dma_start(c[n][:, :], a[n]).then_inc(kept.sem, 16)
            else:
                for k in range(KT):
                    sp.dma_start(flat(a["x1_store"][k:k + 1]), x[:, k, :]).then_inc(stored.sem, 16)
                sp.wait_ge(stored.sem, stored.before(KT))

        @block.scalar
        def _(act):
            act.preload_act_table_set(TABLES)
            if first:
                act.wait_ge(cond.sem, cond.before(1))
                act.activation(c["csil"][:, :, :], cx[:, :, :], ACT.Exp, scale=-1.0).then_inc(silu_e.sem, 1)
                act.wait_ge(lam_s.sem, 1)
                act.activation(c["lam"][:, 0:2], c["lam"][:, 4:6], ACT.Exp).then_inc(lam_e.sem, 1)
                act.wait_ge(lb_s.sem, 1)
                act.activation(lw[:, 3:5, :], lw[:, 1:3, :], ACT.Exp).then_inc(lb_e.sem, 1)
            for k in range(KT):
                if first:
                    act.wait_ge(x_in[k].sem, x_in[k].before(1))
                if k >= 2:
                    act.wait_ge(used.sem, used.before(k - 1))
                act.activation(sq[k % 2][:, :], x[:, k, :], ACT.Square).then_inc(squared.sem, 1)
            act.wait_ge(summed.sem, 1)
            act.wait_ge(mods.sem, 1)
            for j in range(NP):
                act.activation(rs[:, cols(j)], ps[:, j, 0:TH], ACT.Ln, bias=c["eps"][:, 0:1]).then_inc(lnd.sem, 1)
            act.wait_ge(lnd.sem, NP)
            act.activation(rs[:, :], rs[:, :], ACT.Exp, scale=-0.5).then_inc(rstd.sem, 1)
            for k in range(KT):
                act.wait_ge(normed.sem, k + 1)
                act.activation(hi[:, k, :], y[k % 2][:, :], ACT.Copy).then_inc(high.sem, 1)

        @block.tensor
        def _(pe):
            pe.wait_ge(mean_in.sem, 16)
            for k in range(KT):
                pe.wait_ge(squared.sem, k + 1)
                for j in range(NP):
                    ins = pe.matmul(ps[:, j, 0:TH], mean[:, :], sq[k % 2][:, cols(j)], start=(k == 0), stop=(k == KT - 1))
                ins.then_inc(used.sem if k < KT - 1 else summed.sem, 1)
            if first:
                pe.wait_ge(csil.sem, 1)
            for t in range(n_ada):
                pe.wait_ge(ada_in[t % RING].sem, ada_in[t % RING].before(t // RING + 1))
                if t >= RING:
                    pe.wait_ge(ada_read.sem, t - RING + 1)
                for k in range(KT):
                    ins = pe.matmul(pa[:, t % RING, 0:CS], aw[t % RING][:, k * P:(k + 1) * P], c["csil"][:, k, :],
                                    start=(k == 0), stop=(k == KT - 1))
                ins.then_inc(ada_done.sem, 1)

        @block.gpsimd
        def _(pool):
            ctx.clear_last(pool)
            for k in range(KT):
                pool.wait_ge(normed.sem, k + 1)
                pool.wait_ge(high.sem, k + 1)
                pool.tensor_tensor(lo[:, k, :], y[k % 2][:, :], hi[:, k, :].bitcast(F32), ALU.subtract).then_inc(low.sem, 1)

        @block.vector
        def _(dve):
            ch = Chain(ctx, nc, dve, f"{name}_dve_chain")
            mod, vec = c["mod"], c["vec"]
            if first:
                ch(dve.memset(c["eps"][:, :], EPS))
                dve.wait_ge(silu_e.sem, 1)
                cs = c["csil"][:, :, :]
                ch(dve.tensor_scalar(cs, cs, 1.0, None, ALU.add))
                ch.sync()
                ch(dve.reciprocal(cs, cs))
                ch.sync()
                dve.tensor_tensor(cs, cs, cx[:, :, :], ALU.mult).then_inc(csil.sem, 1)
                dve.wait_ge(vec_in.sem, 16)
                lv = vec[:, VEC["lam"][0]:VEC["lam"][0] + 4 * DH].rearrange("p (c s n) -> p c s n", c=2, s=2)
                ch(dve.tensor_tensor(tmp[:, :, :], lv[:, :, 0, :], lv[:, :, 1, :], ALU.mult))
                ch.sync()
                dve.tensor_reduce(c["lam"][:, 4:6], tmp[:, :, :], AX.X, ALU.add).then_inc(lam_s.sem, 1)
                lb0 = VEC["lb"][0]
                l0, l1 = vec[:, lb0:lb0 + H], vec[:, lb0 + H:lb0 + 2 * H]
                ch(dve.tensor_tensor(lw[:, 0, :], l0, l1, ALU.max))
                ch.sync()
                ch(dve.tensor_tensor(lw[:, 1, :], l0, lw[:, 0, :], ALU.subtract))
                dve.tensor_tensor(lw[:, 2, :], l1, lw[:, 0, :], ALU.subtract).then_inc(lb_s.sem, 1)
                dve.wait_ge(lam_e.sem, 1)
                ch(dve.tensor_tensor(c["lam"][:, 2:3], c["lam"][:, 0:1], c["lam"][:, 1:2], ALU.subtract))
                ch.sync()
                ch(dve.tensor_scalar(c["lam"][:, 2:3], c["lam"][:, 2:3], LAM_INIT, None, ALU.add))
                ch.sync()
                ch(dve.tensor_scalar(c["lam"][:, 3:4], c["lam"][:, 2:3], -1.0, None, ALU.mult))
                dve.wait_ge(lb_e.sem, 1)
                ch(dve.tensor_tensor(lw[:, 5, :], lw[:, 3, :], lw[:, 4, :], ALU.add))
                ch.sync()
                ch(dve.reciprocal(lw[:, 5, :], lw[:, 5, :]))
                ch.sync()
                ch(dve.tensor_tensor(c["lb"][:, 0, :], lw[:, 3, :], lw[:, 5, :], ALU.mult))
                ch.sync()
                ch(dve.tensor_scalar(c["lb"][:, 1, :], c["lb"][:, 0, :], -1.0, 1.0, ALU.mult, ALU.add))
                for t in range(n_ada):
                    dve.wait_ge(ada_done.sem, t + 1)
                    dve.tensor_scalar(mod[:, t, :], pa[:, t % RING, 0:CS], vec[:, t:t + 1], None, ALU.add).then_inc(ada_read.sem, 1)
                dve.wait_ge(ada_read.sem, n_ada)
            for k in range(KT):
                m = mod[:, scale + k, :]
                ch(dve.tensor_scalar(m, m, 1.0, vec[:, gain + k:gain + k + 1], ALU.add, ALU.mult))
            ch.sync()
            dve.sem_inc(mods.sem, 1)
            dve.wait_ge(rstd.sem, 1)
            for k in range(KT):
                if k >= 2:
                    dve.wait_ge(high.sem, k - 1)
                    dve.wait_ge(low.sem, k - 1)
                yk = y[k % 2]
                ch(dve.tensor_tensor(yk[:, :], x[:, k, :], rs[:, :], ALU.mult))
                ch.sync()
                ch(dve.tensor_tensor(yk[:, T:NT], yk[:, T:NT], mod[:, scale + k, 1:CS], ALU.mult))
                ch(dve.tensor_scalar(yk[:, 0:T], yk[:, 0:T], mod[:, scale + k, 0:1], mod[:, shift + k, 0:1], ALU.mult, ALU.add))
                ch.sync()
                dve.tensor_tensor(yk[:, T:NT], yk[:, T:NT], mod[:, shift + k, 1:CS], ALU.add).then_inc(normed.sem, 1)
            if first:
                dve.wait_ge(kept.sem, kept.before(N_KEPT))


TILES = ("f", "qh", "ib", "og", "q", "k", "v")
NTL = len(TILES)
SLOT = (0, 1, 0, 1, 0, 1, 2)
BACK = (3, 3, 2, 2, 2, 2, 7)
PIECES = [(t, j) for t in range(NTL) for j in range(NP)]
ATT_PIECES = ([0], [1], [2], [3], [4, 5], [6, 7], [8, 9], [10, 11])
REC_PIECES = ([12], [13], [14], [15], [16], [17], [18], [19, 20])
SIGMOID = [n for n, (t, j) in enumerate(PIECES) if TILES[t] in ("f", "qh", "og")]
SPLIT_AT = {1: 1, 4: 2, 7: 3, 10: 4, 13: 5, 16: 6, 19: 7}


def level_view(ap, lv):
    return ap.rearrange("p (n two b) -> p n two b", two=2, b=1 << lv)


def heads_stage(nc, a, o, c, d, xh, xl):
    with Stage(c) as ctx:
        mem = Memory(nc, "h", R2)
        raw = [mem(f"w_raw{s}", [P, KT * P]) for s in range(2)]
        whi = [mem(f"w_hi{s}", [P, KT * P], F32R) for s in range(3)]
        wlo = [mem(f"w_lo{s}", [P, KT * P], F32R) for s in range(3)]
        qT, kT, vT = (mem(n, [P, NT]) for n in ("qT", "kT", "vT"))
        vtok = mem("vtok", [P, T])
        kk, fc, qh, ib, og = (mem(n, [P, NT]) for n in ("kk", "fc", "qh", "ib", "og"))
        ibtok = mem("ibtok", [P, T])
        E = mem("E", [P, 2, T])
        PT = mem("PT", [P, T])
        LV = [mem(f"LV{i}", [P, LEVELS + 2, P]) for i in range(2)]
        QL = [mem(f"QL{i}", [P, LEVELS * HALF + P]) for i in range(2)]
        AT = mem("AT", [P, P])
        kht = mem("kht", [P, P])
        St = mem("St", [P, P])
        oraw, braw = mem("oraw", [P, T]), mem("braw", [P, T])
        ex = [mem(f"ex{i}", [P, TH]) for i in range(2)]
        sq = [mem(f"sq{i}", [P, TH]) for i in range(2)]
        rg = [mem(f"rg{i}", [P, TH]) for i in range(2)]
        rb, rr = mem("rb", [P, TH]), mem("rr", [P, TH])
        ohi, olo = mem("ohi", [P, 512], F32R), mem("olo", [P, 512], F32R)
        cos, sin = mem("cos", [P, NT]), mem("sin", [P, NT])
        rot, blk, causal = (mem(n, [P, P]) for n in ("rot", "blk", "causal"))
        lmask = mem("lmask", [P, LEVELS * HALF], U32)
        sm = mem("sm", [P, 16])
        dec = mem("dec", [P, NB])
        subg = mem("subg", [P, 1])
        G = ctx.enter_context(nc.psum_tensor("h_G", [P, 2, 512], F32))
        SP_ = ctx.enter_context(nc.psum_tensor("h_S", [P, 4, 512], F32))
        X = ctx.enter_context(nc.psum_tensor("h_X", [P, 2, 512], F32))
        dest = {"f": fc, "qh": qh, "ib": ib, "og": og, "v": vT, "q": qT, "k": kT}
        Xf = X[:, :, :].rearrange("p a b -> p (a b)")

        def S(n, per, **k):
            return Sig(ctx, nc, f"h_{n}", per=per, **k)

        consts = S("consts_in", 0, step=16)
        loaded = [S("w_loaded0", 4, pre=3, step=16), S("w_loaded1", 3, pre=1, step=16)]
        hi_done, lo_done = S("w_hi_done", 7, pre=4), S("w_lo_done", 7, pre=4)
        piece_done = S("piece_done", 21, pre=9)
        piece_read = S("piece_read", 21, pre=9)
        ex_ready, ex_cut, sig_ready = (S(n, 9) for n in ("ex_ready", "ex_cut", "sig_ready"))
        sig_used = S("sig_used", 9, init=2)
        qk_squared = S("qk_squared", 6, pre=6)
        qk_summed = S("qk_summed", 6, pre=6)
        qk_rstd = S("qk_rstd", 6, pre=6)
        qk_ready = S("qk_ready", 6, pre=6)
        kv_stored = S("kv_stored", 2, step=16)
        sample_qkv, sample_rec = S("sample_qkv_kept", 1), S("sample_rec_kept", 1, init=1)
        scores, row_max, exped, weighed = S("scores", 8), S("row_max", 8), S("exped", 8), S("weighed", 8)
        turned, pt_ready, pv_done, pv_read = S("turned", 8), S("pt_ready", 8), S("pv_done", 8), S("pv_read", 8)
        v_turned, v_tok = S("v_turned", 1), S("v_tok", 1)
        ib_turned, ib_tok = S("ib_turned", 1, init=1), S("ib_tok", 1)
        log_f, cum_ready, dec_ready = S("log_f", 1), S("cum_ready", 1), S("chunk_decay", 1)
        lv_diff, lv_exp, lv_k = S("lv_diff", 8), S("lv_exp", 8), S("lv_ready", 8, init=2)
        rec_done, at_ready, kht_ready = S("rec_products", 8, init=1), S("at_ready", 8), S("kht_ready", 8)
        os_done, o_read, st_ready = S("rec_out_done", 8, init=1), S("rec_out_read", 8, init=1), S("state_ready", 8, init=1)
        st_stored = S("state_stored", 1, step=16, init=1)
        o_squared, o_summed, o_rstd, o_normed = S("o_squared", 4), S("o_summed", 4), S("o_rstd", 4, init=1), S("o_normed", 4, init=1)
        o_hi, o_lo = S("o_hi", 4), S("o_lo", 4, init=1)
        o_stored = S("o_stored", 8, step=16, init=2)
        block = ctx.enter_context(nc.Block())
        N_CONST = 6
        wt = a["w_in"]

        def slot(t):
            return SLOT[t] if t >= 0 else (0, 1, 2)[t + 3]

        @block.sync
        def _(sp):
            for t, n in ((cos, "cos"), (sin, "sin"), (rot, "rot"), (blk, "blk"), (causal, "causal"), (lmask, "lmask")):
                sp.dma_start(t[:, :], a[n]).then_inc(consts.sem, 16)
            for n in range(3):
                if n == 2:
                    sp.wait_ge(hi_done.sem, 1)
                    sp.wait_ge(lo_done.sem, 1)
                sp.dma_start(raw[n % 2][:, :], flat(wt[n:n + 1])).then_inc(loaded[n % 2].sem, 16)

            sp.wait_ge(hi_done.sem, hi_done.before(3))
            sp.wait_ge(lo_done.sem, lo_done.before(3))
            sp.dma_start(raw[0][:, :], flat(wt[3:4])).then_inc(loaded[0].sem, 16)
            sp.dma_start(raw[1][:, :], flat(wt[4:5])).then_inc(loaded[1].sem, 16)
            o_stored.start(sp)
            st_stored.start(sp)

            def store_branch(h, u):
                branch, s = "oa" if u < 2 else "ob", slice((u % 2) * 512, (u % 2) * 512 + 512)
                sp.wait_ge(o_lo.sem, o_lo.at(h, u + 1))
                sp.dma_start(flat(d[branch + "hi"][bass.ds(h, 1), :, s]), ohi[:, :].bitcast(F32)).then_inc(o_stored.sem, 16)
                sp.dma_start(flat(d[branch + "lo"][bass.ds(h, 1), :, s]), olo[:, :].bitcast(F32)).then_inc(o_stored.sem, 16)

            with sp.Fori(0, H) as h:
                sp.wait_ge(qk_ready.sem, qk_ready.at(h, 0))
                sp.dma_start(flat(o["k"][bass.ds(h, 1)]), kT[:, :]).then_inc(kv_stored.sem, 16)
                sp.wait_ge(piece_read.sem, piece_read.at(h, 0))
                sp.dma_start(flat(o["v"][bass.ds(h, 1)]), vT[:, :]).then_inc(kv_stored.sem, 16)
                for t in range(2, NTL + 2):
                    behind, r = {NTL: (1, 0), NTL + 1: (3, 1)}.get(t, (2, t % 2))
                    if t == NTL:
                        store_branch(h, 0)
                        store_branch(h, 1)
                    sp.wait_ge(hi_done.sem, hi_done.at(h, t - behind))
                    sp.wait_ge(lo_done.sem, lo_done.at(h, t - behind))
                    sp.dma_start(raw[r][:, :], flat(wt[bass.ds(h * NTL + (3 + t), 1)])).then_inc(loaded[r].sem, 16)
                sp.wait_ge(st_ready.sem, st_ready.at(h, NB))
                sp.dma_start(flat(o["state"][bass.ds(h, 1)]), St[:, :]).then_inc(st_stored.sem, 16)
                store_branch(h, 2)
                store_branch(h, 3)
            sp.wait_ge(kv_stored.sem, kv_stored.at(H, 0))
            sp.wait_ge(o_stored.sem, o_stored.at(H, 0))
            sp.wait_ge(st_stored.sem, st_stored.at(H, 0))
            for s in range(2):
                sp.wait_ge(loaded[s].sem, loaded[s].at(H, 1 if s else 0))

        def raw_loaded(eng, h, t):
            if t == NTL:
                eng.wait_ge(loaded[0].sem, loaded[0].at(h, 4))
            elif t % 2 == 0:
                eng.wait_ge(loaded[0].sem, loaded[0].at(h, t // 2))
            else:
                eng.wait_ge(loaded[1].sem, loaded[1].at(h, t // 2 + 1))

        def used_wait(eng, h, t):
            tile = t if t < NTL else 0
            back = BACK[tile]
            eng.wait_ge(piece_done.sem, piece_done.at(h, NP * (t - back + 1)))

        @block.scalar
        def _(act):
            act.preload_act_table_set(TABLES)
            ch = Chain(ctx, nc, act, "h_act_chain")
            act.wait_ge(consts.sem, consts.before(N_CONST))
            vec = c["vec"]
            gq, gk = (vec[:, VEC[n][0]:VEC[n][0] + 1] for n in ("q_g", "k_g"))

            def split(w, r):
                act.activation(whi[w][:, :], raw[r][:, :], ACT.Copy).then_inc(hi_done.sem, 1)

            def qk_piece(g, bank, u):
                act.activation(sq[u][:, :], G[:, bank, 0:TH], ACT.Square).then_inc(qk_squared.sem, 1)
                act.activation(rg[u][:, :], G[:, bank, 0:TH], ACT.Copy, scale=g).then_inc(piece_read.sem, 1)

            def qk_norm(value):
                act.wait_ge(qk_summed.sem, value)
                ch(act.activation(rr[:, :], X[:, 1, 0:TH], ACT.Ln, bias=c["eps"][:, 0:1]))
                ch.sync()
                act.activation(rr[:, :], rr[:, :], ACT.Exp, scale=-0.5).then_inc(qk_rstd.sem, 1)

            for n in range(9):
                for t in {0: (0, 1), 3: (2,)}.get(n, ()):
                    act.wait_ge(loaded[t % 2].sem, 16 * (t // 2 + 1))
                    split(t, t % 2)
                if n == 6:
                    act.wait_ge(loaded[0].sem, 16 * 3)
                    act.wait_ge(piece_done.sem, 3)
                    split(0, 0)
                act.wait_ge(piece_done.sem, n + 1)
                if n < 6:
                    if n >= 2:
                        act.wait_ge(qk_ready.sem, n - 1)
                    qk_piece(gq if n < 3 else gk, n % 2, n % 2)
                    if n >= 1:
                        qk_norm(n)
                else:
                    if n == 6:
                        qk_norm(6)
                    act.activation(vT[:, cols(n - 6)], G[:, n % 2, 0:TH], ACT.Copy).then_inc(piece_read.sem, 1)
            o_read.start(act)
            o_rstd.start(act)
            ch.reset()

            def piece(h, n):
                t, j = PIECES[n]
                kind = TILES[t]
                bank = G[:, n % 2, 0:TH]
                act.wait_ge(piece_done.sem, piece_done.at(h, n + 1))
                if kind in ("f", "qh", "og"):
                    s = SIGMOID.index(n)
                    if s >= 1:
                        sigmoid(h, s - 1)
                    act.wait_ge(sig_used.sem, sig_used.at(h, s - 1))
                    if j == 0 and kind != "f":
                        last = rec_done if kind == "qh" else o_normed
                        act.wait_ge(last.sem, last.at(h, 0))
                        act.wait_ge(sample_rec.sem, sample_rec.at(h, 0))
                    ins = act.activation(ex[s % 2][:, :], bank, ACT.Exp, scale=-1.0)
                    ins.then_inc(ex_ready.sem, 1)
                    if kind == "f":
                        act.wait_ge(ex_ready.sem, ex_ready.at(h, s + 1))
                        act.sem_inc(piece_read.sem, 1)
                    else:
                        act.activation(dest[kind][:, cols(j)], bank, ACT.Copy).then_inc(piece_read.sem, 1)
                elif kind in ("ib", "v"):
                    if kind == "v" and j == 0:
                        act.wait_ge(kv_stored.sem, kv_stored.at(h, 2))
                        act.wait_ge(sample_qkv.sem, sample_qkv.at(h, 1))
                    if kind == "ib" and j == 0:
                        act.wait_ge(ib_turned.sem, ib_turned.at(h, 0))
                        act.wait_ge(sample_rec.sem, sample_rec.at(h, 0))
                    act.activation(dest[kind][:, cols(j)], bank, ACT.Copy).then_inc(piece_read.sem, 1)
                else:
                    u = n - 12
                    act.wait_ge(qk_ready.sem, qk_ready.at(h, u - 1))
                    qk_piece(gq if kind == "q" else gk, n % 2, u % 2)

            def sigmoid(h, s):
                act.wait_ge(ex_cut.sem, ex_cut.at(h, s + 1))
                ch(act.activation(ex[s % 2][:, :], ex[s % 2][:, :], ACT.Ln))
                ch.sync()
                act.activation(ex[s % 2][:, :], ex[s % 2][:, :], ACT.Exp, scale=-1.0).then_inc(sig_ready.sem, 1)

            def split_next(h, n):
                if n in SPLIT_AT:
                    t = SPLIT_AT[n]
                    raw_loaded(act, h, t)
                    used_wait(act, h, t)
                    split(slot(t % NTL), 0 if t == NTL else t % 2)

            def levels(h, k):
                act.wait_ge(lv_diff.sem, lv_diff.at(h, k + 1))
                act.activation(LV[k % 2][:, :, :], LV[k % 2][:, :, :], ACT.Exp, scale=-1.0).then_inc(lv_exp.sem, 1)

            def o_norm(h, u):
                act.wait_ge(o_summed.sem, o_summed.at(h, u + 1))
                r = E[:, 0, (u % 2) * 512:(u % 2) * 512 + 512]
                if u >= 2:
                    act.wait_ge(o_lo.sem, o_lo.at(h, 2))
                ch(act.activation(r, X[:, u % 2, :], ACT.Ln, bias=c["eps"][:, 0:1]))
                ch.sync()
                act.activation(r, r, ACT.Exp, scale=-0.5).then_inc(o_rstd.sem, 1)

            def o_high(h, u):
                act.wait_ge(o_normed.sem, o_normed.at(h, u + 1))
                act.wait_ge(o_stored.sem, o_stored.at(h, 2 * u))
                act.activation(ohi[:, :], E[:, 1, (u % 2) * 512:(u % 2) * 512 + 512], ACT.Copy).then_inc(o_hi.sem, 1)

            with act.Fori(0, H) as h:
                for i in range(NB):
                    nk = (i + 1) * P
                    act.wait_ge(row_max.sem, row_max.at(h, i + 1))
                    if i == 0:
                        act.wait_ge(o_lo.sem, o_lo.at(h, 0))
                    for m in range(2):
                        ins = act.activation(E[:, m, 0:nk],
                                             SP_[:, 2 * m:2 * m + 2, :].rearrange("p a b -> p (a b)")[:, 0:nk],
                                             ACT.Exp, bias=sm[:, 2 + m:3 + m], scale=SCALE, accum_out=sm[:, 4 + m:5 + m])
                        if m == 0:
                            ch(ins)
                    ins.then_inc(exped.sem, 1)
                    if i == 0:
                        act.wait_ge(v_turned.sem, v_turned.at(h, 1))
                        act.activation(vtok[:, :], Xf, ACT.Copy).then_inc(v_tok.sem, 1)
                    for n in ATT_PIECES[i]:
                        split_next(h, n)
                        piece(h, n)
                    if i == 4:
                        act.wait_ge(sig_used.sem, sig_used.at(h, 3))
                        act.activation(fc[:, 0:T], fc[:, 0:T], ACT.Ln).then_inc(log_f.sem, 1)
                    act.wait_ge(turned.sem, turned.at(h, i + 1))
                    act.activation(PT[:, 0:nk], Xf[:, 0:nk], ACT.Copy).then_inc(pt_ready.sem, 1)
                    act.wait_ge(pv_done.sem, pv_done.at(h, i + 1))
                    act.activation(oraw[:, i * P:(i + 1) * P], X[:, 0, 0:P], ACT.Copy).then_inc(pv_read.sem, 1)
                sigmoid(h, len(SIGMOID) - 1)
                act.wait_ge(cum_ready.sem, cum_ready.at(h, 1))
                act.activation(dec[:, :], fc[:, P - 1:T:P], ACT.Exp).then_inc(dec_ready.sem, 1)
                act.wait_ge(ib_turned.sem, ib_turned.at(h, 1))
                act.activation(ibtok[:, :], Xf, ACT.Copy).then_inc(ib_tok.sem, 1)
                levels(h, 0)
                for k in range(NB):
                    if k + 1 < NB:
                        levels(h, k + 1)
                    act.wait_ge(rec_done.sem, rec_done.at(h, k + 1))
                    act.activation(kht[:, :], SP_[:, 2, 0:P], ACT.Copy).then_inc(kht_ready.sem, 1)
                    if k == 0:
                        o_norm(h, 0)
                        o_norm(h, 1)
                        o_high(h, 0)
                        o_high(h, 1)
                    for n in REC_PIECES[k]:
                        split_next(h, n)
                        piece(h, n)
                    if 1 <= k <= 6:
                        qk_norm(qk_summed.at(h, k))
                    act.wait_ge(os_done.sem, os_done.at(h, k + 1))
                    act.activation(braw[:, k * P:(k + 1) * P], SP_[:, 3, 0:P], ACT.Copy).then_inc(o_read.sem, 1)
                o_norm(h, 2)
                o_norm(h, 3)
                o_high(h, 2)
                o_high(h, 3)
                ch.reset()

        @block.tensor
        def _(pe):
            ident, ones = c["ident"], c["ones128"]
            pe.wait_ge(consts.sem, consts.before(N_CONST))
            for sig in (rec_done, os_done, ib_turned):
                sig.start(pe)

            def qk_sums(u):
                pe.matmul(X[:, 1, 0:TH], blk[:, :], sq[u][:, :], start=True, stop=True)
                pe.matmul(X[:, 0, 0:TH], rot[:, :], rg[u][:, :], start=True, stop=True).then_inc(qk_summed.sem, 1)

            for n in range(9):
                t = n // NP
                if n % NP == 0:
                    pe.wait_ge(hi_done.sem, t + 1)
                    pe.wait_ge(lo_done.sem, t + 1)
                if n >= 2:
                    pe.wait_ge(piece_read.sem, n - 1)
                product(pe, G[:, n % 2, 0:TH], whi[t], wlo[t], xh, xl, KT, cols(n % NP)).then_inc(piece_done.sem, 1)
                if n < 6:
                    pe.wait_ge(qk_squared.sem, n + 1)
                    pe.wait_ge(piece_read.sem, n + 1)
                    if n >= 1:
                        pe.wait_ge(qk_ready.sem, n)
                    qk_sums(n % 2)

            def piece(h, n):
                t, j = PIECES[n]
                if j == 0:
                    pe.wait_ge(hi_done.sem, hi_done.at(h, t))
                    pe.wait_ge(lo_done.sem, lo_done.at(h, t))
                pe.wait_ge(piece_read.sem, piece_read.at(h, n - 1 if n else 0))
                w = SLOT[t]
                product(pe, G[:, n % 2, 0:TH], whi[w], wlo[w], xh, xl, KT, cols(j)).then_inc(piece_done.sem, 1)

            def scores_of(h, i):
                nk = (i + 1) * P
                for m in range(2):
                    rows = slice(DH * m, DH * (m + 1))
                    for b in range(0, nk, 512):
                        w = min(512, nk - b)
                        ins = pe.matmul(SP_[:, 2 * m + b // 512, 0:w], qT[rows, i * P:(i + 1) * P], kT[rows, b:b + w],
                                        start=True, stop=True)
                ins.then_inc(scores.sem, 1)

            def turn8(src):
                for b in range(NB):
                    ins = pe.transpose(Xf[:, b * P:(b + 1) * P], src[:, b * P:(b + 1) * P], ident[:, :])
                return ins

            def o_sum(h, u):
                pe.wait_ge(o_squared.sem, o_squared.at(h, u + 1))
                pe.matmul(X[:, u % 2, :], ones[:, :], PT[:, (u % 2) * 512:(u % 2) * 512 + 512],
                          start=True, stop=True).then_inc(o_summed.sem, 1)

            with pe.Fori(0, H) as h:
                pe.wait_ge(qk_ready.sem, qk_ready.at(h, 0))
                pe.wait_ge(o_read.sem, o_read.at(h, 0))
                pe.wait_ge(st_ready.sem, st_ready.at(h, 0))
                scores_of(h, 0)
                pe.wait_ge(piece_read.sem, piece_read.at(h, 0))
                pe.wait_ge(o_rstd.sem, o_rstd.at(h, 0))
                turn8(vT).then_inc(v_turned.sem, 1)
                for i in range(NB):
                    for n in ATT_PIECES[i]:
                        piece(h, n)
                    pe.wait_ge(weighed.sem, weighed.at(h, i + 1))
                    if i == 0:
                        pe.wait_ge(v_tok.sem, v_tok.at(h, 1))
                    else:
                        pe.wait_ge(pv_read.sem, pv_read.at(h, i))
                    for b in range(i + 1):
                        ins = pe.transpose(Xf[:, b * P:(b + 1) * P], E[:, 0, b * P:(b + 1) * P], ident[:, :])
                    ins.then_inc(turned.sem, 1)
                    if i + 1 < NB:
                        scores_of(h, i + 1)
                    pe.wait_ge(pt_ready.sem, pt_ready.at(h, i + 1))
                    for b in range(i + 1):
                        ins = pe.matmul(X[:, 0, 0:P], vtok[:, b * P:(b + 1) * P], PT[:, b * P:(b + 1) * P],
                                        start=(b == 0), stop=(b == i))
                    ins.then_inc(pv_done.sem, 1)
                pe.wait_ge(piece_read.sem, piece_read.at(h, 9))
                pe.wait_ge(pv_read.sem, pv_read.at(h, NB))
                turn8(ib).then_inc(ib_turned.sem, 1)
                for k in range(NB):
                    ck = slice(k * P, (k + 1) * P)
                    pe.wait_ge(lv_k.sem, lv_k.at(h, k + 1))
                    if k:
                        pe.wait_ge(at_ready.sem, at_ready.at(h, k))
                        pe.wait_ge(kht_ready.sem, kht_ready.at(h, k))
                    pe.matmul(SP_[:, 0, 0:P], kk[:, ck], qh[:, ck], start=True, stop=True)
                    for lv in range(LEVELS):
                        pe.matmul(SP_[:, 1, lv * HALF:(lv + 1) * HALF], LV[k % 2][:, lv, :],
                                  QL[k % 2][:, lv * HALF:(lv + 1) * HALF], start=True, stop=True)
                    pe.transpose(SP_[:, 2, 0:P], LV[k % 2][:, LEVELS, :], ident[:, :]).then_inc(rec_done.sem, 1)
                    if k == 0:
                        pe.wait_ge(ib_tok.sem, ib_tok.at(h, 1))
                        o_sum(h, 0)
                        o_sum(h, 1)
                    for n in REC_PIECES[k]:
                        piece(h, n)
                    if 1 <= k <= 6:
                        u = k - 1
                        pe.wait_ge(qk_squared.sem, qk_squared.at(h, u + 1))
                        pe.wait_ge(piece_read.sem, piece_read.at(h, 12 + u + 1))
                        if u:
                            pe.wait_ge(qk_ready.sem, qk_ready.at(h, u))
                        else:
                            pe.wait_ge(o_rstd.sem, o_rstd.at(h, 2))
                        qk_sums(u % 2)
                    pe.wait_ge(at_ready.sem, at_ready.at(h, k + 1))
                    if k:
                        pe.wait_ge(o_read.sem, o_read.at(h, k))
                        pe.wait_ge(st_ready.sem, st_ready.at(h, k))
                    pe.matmul(SP_[:, 3, 0:P], ibtok[:, ck], AT[:, :], start=True, stop=(k == 0))
                    if k:
                        pe.matmul(SP_[:, 3, 0:P], St[:, :], QL[k % 2][:, LEVELS * HALF:], start=False, stop=True)
                    pe.wait_ge(kht_ready.sem, kht_ready.at(h, k + 1))
                    pe.matmul(SP_[:, 3, P:2 * P], kht[:, :], ibtok[:, ck], start=True, stop=True).then_inc(os_done.sem, 1)
                pe.wait_ge(qk_ready.sem, qk_ready.at(h, 6))
                o_sum(h, 2)
                o_sum(h, 3)

        @block.gpsimd
        def _(pool):
            ctx.clear_last(pool)
            ch = Chain(ctx, nc, pool, "h_pool_chain")

            def lo_of(w, r):
                pool.tensor_tensor(wlo[w][:, :], raw[r][:, :], whi[w][:, :].bitcast(F32), ALU.subtract).then_inc(lo_done.sem, 1)

            for t in range(4):
                pool.wait_ge(loaded[t % 2].sem, 16 * (t // 2 + 1)) if t < 3 else pool.wait_ge(loaded[0].sem, 48)
                pool.wait_ge(hi_done.sem, t + 1)
                if t == 3:
                    pool.wait_ge(piece_done.sem, 3)
                lo_of((0, 1, 2, 0)[t], (0, 1, 0, 0)[t])
            o_lo.start(pool)
            sample_rec.start(pool)

            def split_next(h, n):
                if n in SPLIT_AT:
                    t = SPLIT_AT[n]
                    raw_loaded(pool, h, t)
                    pool.wait_ge(hi_done.sem, hi_done.at(h, t))
                    used_wait(pool, h, t)
                    lo_of(slot(t % NTL), 0 if t == NTL else t % 2)

            def kept(name, src, h):
                return pool.tensor_copy(c["s_" + name][:, bass.ds(h, 1), :].rearrange("p o n -> p (o n)"), src[:, T:NT])

            def differences(h, k):
                if k == 0:
                    pool.wait_ge(cum_ready.sem, cum_ready.at(h, 1))
                pool.wait_ge(rec_done.sem, rec_done.at(h, max(k - 1, 0)))
                pool.wait_ge(lv_k.sem, lv_k.at(h, k - 1))
                cu, L = fc[:, k * P:(k + 1) * P], LV[k % 2]
                for lv in range(LEVELS):
                    b = 1 << lv
                    v, w = level_view(cu, lv), level_view(L[:, lv, :], lv)
                    mid = v[:, :, 0, b - 1:b].broadcast_to([P, HALF // b, b])
                    ch(pool.tensor_tensor(w[:, :, 0, :], v[:, :, 0, :], mid, ALU.subtract))
                    ch(pool.tensor_tensor(w[:, :, 1, :], mid, v[:, :, 1, :], ALU.subtract))
                ch(pool.tensor_tensor(L[:, LEVELS, :], cu, cu[:, P - 1:P].broadcast_to([P, P]), ALU.subtract))
                ch(pool.tensor_scalar(L[:, LEVELS + 1, :], cu, -1.0, 0.0, ALU.mult, ALU.add))
                ch.sync()
                pool.sem_inc(lv_diff.sem, 1)

            def squares(h, src, u):
                if u == 2:
                    pool.wait_ge(o_summed.sem, o_summed.at(h, 2))
                s = slice((u % 2) * 512, (u % 2) * 512 + 512)
                pool.tensor_tensor(PT[:, s], src[:, s], src[:, s], ALU.mult).then_inc(o_squared.sem, 1)

            def o_low(h, u):
                pool.wait_ge(o_hi.sem, o_hi.at(h, u + 1))
                s = slice((u % 2) * 512, (u % 2) * 512 + 512)
                pool.tensor_tensor(olo[:, :], E[:, 1, s], ohi[:, :].bitcast(F32), ALU.subtract).then_inc(o_lo.sem, 1)

            with pool.Fori(0, H) as h:
                pool.wait_ge(qk_ready.sem, qk_ready.at(h, 0))
                pool.wait_ge(piece_read.sem, piece_read.at(h, 0))
                ch(kept("q", qT, h))
                ch(kept("k", kT, h))
                ch(kept("v", vT, h))
                ch.sync()
                pool.sem_inc(sample_qkv.sem, 1)
                for i in range(NB):
                    for n in ATT_PIECES[i]:
                        split_next(h, n)
                pool.wait_ge(sig_used.sem, sig_used.at(h, 9))
                pool.wait_ge(piece_read.sem, piece_read.at(h, 9))
                for n, src in (("f", fc), ("kk", kk), ("qh", qh), ("ib", ib), ("og", og)):
                    ch(kept(n, src, h))
                ch.sync()
                pool.sem_inc(sample_rec.sem, 1)
                differences(h, 0)
                pool.wait_ge(pv_read.sem, pv_read.at(h, NB))
                squares(h, oraw, 0)
                squares(h, oraw, 1)
                for k in range(NB):
                    if k + 1 < NB:
                        differences(h, k + 1)
                    for n in REC_PIECES[k]:
                        split_next(h, n)
                    if k == 0:
                        o_low(h, 0)
                        o_low(h, 1)
                pool.wait_ge(o_read.sem, o_read.at(h, NB))
                squares(h, braw, 2)
                squares(h, braw, 3)
                o_low(h, 2)
                o_low(h, 3)
                ch.reset()

        @block.vector
        def _(dve):
            ch = Chain(ctx, nc, dve, "h_dve_chain")
            vec, lam, lb = c["vec"], c["lam"], c["lb"]
            dve.wait_ge(consts.sem, consts.before(N_CONST))
            ones_row = c["ones"]
            ch(dve.tensor_scalar(subg[:, :], vec[:, VEC["sub_g"][0]:VEC["sub_g"][0] + 1], 1.0 - LAM_INIT, None, ALU.mult))
            for sig in (lv_k, st_ready, sig_used, o_normed):
                sig.start(dve)

            def rope(j, u):
                ch(dve.tensor_tensor(rb[:, :], X[:, 0, 0:TH], sin[:, cols(j)], ALU.mult))
                ch(dve.tensor_tensor(rg[u][:, :], rg[u][:, :], cos[:, cols(j)], ALU.mult))
                ch.sync()
                ch(dve.tensor_tensor(rb[:, :], rb[:, :], rg[u][:, :], ALU.add))
                ch.sync()

            def rope_end(j, dst):
                dve.tensor_tensor(dst[:, cols(j)], rb[:, :], rr[:, :], ALU.mult).then_inc(qk_ready.sem, 1)

            for n in range(6):
                dve.wait_ge(qk_summed.sem, n + 1)
                rope(n % NP, n % 2)
                dve.wait_ge(qk_rstd.sem, n + 1)
                rope_end(n % NP, qT if n < 3 else kT)
            ch.reset()

            def maxima(h, i):
                nk = (i + 1) * P
                dve.wait_ge(scores.sem, scores.at(h, i + 1))
                both = SP_[:, :, :].rearrange("p (m a) b -> p m (a b)", m=2)
                diag = both[:, :, i * P:nk]
                ch(dve.tensor_tensor(diag, diag, causal[:, :].unsqueeze(1).broadcast_to([P, 2, P]), ALU.add))
                ch.sync()
                ch(dve.tensor_reduce(sm[:, 0:2], both[:, :, 0:nk], AX.X, ALU.max))
                ch.sync()
                dve.tensor_scalar(sm[:, 2:4], sm[:, 0:2], -SCALE, None, ALU.mult).then_inc(row_max.sem, 1)

            def weigh(h, i):
                nk = (i + 1) * P
                dve.wait_ge(exped.sem, exped.at(h, i + 1))
                ch(dve.reciprocal(sm[:, 6:8], sm[:, 4:6]))
                ch.sync()
                ch(dve.tensor_tensor(sm[:, 7:8], sm[:, 7:8], lam[:, 3:4], ALU.mult))
                ch(dve.tensor_scalar(E[:, 0, 0:nk], E[:, 0, 0:nk], sm[:, 6:7], None, ALU.mult))
                ch.sync()
                dve.scalar_tensor_tensor(out=E[:, 0, 0:nk], in0=E[:, 1, 0:nk], scalar=sm[:, 7:8], in1=E[:, 0, 0:nk],
                                         op0=ALU.mult, op1=ALU.add).then_inc(weighed.sem, 1)

            def cut(h, s):
                dve.wait_ge(ex_ready.sem, ex_ready.at(h, s + 1))
                dve.tensor_scalar(ex[s % 2][:, :], ex[s % 2][:, :], BIG, 1.0, ALU.min, ALU.add).then_inc(ex_cut.sem, 1)

            def use_sigmoid(h, s):
                t, j = PIECES[SIGMOID[s]]
                kind = TILES[t]
                dve.wait_ge(sig_ready.sem, sig_ready.at(h, s + 1))
                e = ex[s % 2][:, :]
                if kind == "f":
                    one_lb, low = (lb[:, n, bass.ds(h, 1)] for n in (1, 0))
                    ch(dve.tensor_scalar(fc[:, cols(j)], e, one_lb, low, ALU.mult, ALU.add))
                    ch.sync()
                    dve.tensor_scalar(kk[:, cols(j)], fc[:, cols(j)], -1.0, 1.0, ALU.mult, ALU.add).then_inc(sig_used.sem, 1)
                else:
                    dve.wait_ge(piece_read.sem, piece_read.at(h, SIGMOID[s] + 1))
                    dve.tensor_tensor(dest[kind][:, cols(j)], dest[kind][:, cols(j)], e, ALU.mult).then_inc(sig_used.sem, 1)

            def cumulate(h):
                dve.wait_ge(log_f.sem, log_f.at(h, 1))
                for k in range(NB):
                    g = fc[:, k * P:(k + 1) * P]
                    ch(dve.tensor_tensor_scan(g, ones_row[:, :], g, 0.0, ALU.mult, ALU.add))
                ch.sync()
                dve.sem_inc(cum_ready.sem, 1)

            def operands(h, k):
                L, Q, ck = LV[k % 2], QL[k % 2], slice(k * P, (k + 1) * P)
                dve.wait_ge(lv_exp.sem, lv_exp.at(h, k + 1))
                dve.wait_ge(os_done.sem, os_done.at(h, k - 1 if k >= 2 else 0))
                for lv in range(LEVELS):
                    b = 1 << lv
                    q2 = level_view(qh[:, ck], lv)[:, :, 1, :]
                    e2 = level_view(L[:, lv, :], lv)[:, :, 1, :]
                    ch(dve.tensor_tensor(Q[:, lv * HALF:(lv + 1) * HALF].rearrange("p (n b) -> p n b", b=b), q2, e2, ALU.mult))
                ch(dve.tensor_tensor(Q[:, LEVELS * HALF:], qh[:, ck], L[:, LEVELS + 1, :], ALU.mult))
                ch.sync()
                kl = L[:, 0:LEVELS + 1, :]
                dve.tensor_tensor(kl, kl, kk[:, ck].unsqueeze(1).broadcast_to([P, LEVELS + 1, P]), ALU.mult).then_inc(lv_k.sem, 1)

            def assemble(h, k):
                dve.wait_ge(rec_done.sem, rec_done.at(h, k + 1))
                dve.wait_ge(os_done.sem, os_done.at(h, k))
                ch(dve.tensor_tensor(AT[:, :], SP_[:, 0, 0:P], c["ident"][:, :], ALU.mult))
                ch.sync()
                for lv in range(LEVELS):
                    b = 1 << lv
                    s = slice(lv * HALF, (lv + 1) * HALF)
                    ins = dve.copy_predicated(level_view(AT[:, :], lv)[:, :, 1, :],
                                              lmask[:, s].rearrange("p (n b) -> p n b", b=b),
                                              SP_[:, 1, s].rearrange("p (n b) -> p n b", b=b))
                    if lv < LEVELS - 1:
                        ch(ins)
                        ch.sync()
                ins.then_inc(at_ready.sem, 1)

            def state(h, k):
                dve.wait_ge(os_done.sem, os_done.at(h, k + 1))
                dve.wait_ge(o_read.sem, o_read.at(h, k + 1))
                if k == 0:
                    dve.wait_ge(dec_ready.sem, dec_ready.at(h, 1))
                    dve.wait_ge(st_stored.sem, st_stored.at(h, 0))
                    dve.tensor_copy(St[:, :], SP_[:, 3, P:2 * P]).then_inc(st_ready.sem, 1)
                else:
                    dve.wait_ge(st_ready.sem, st_ready.at(h, k))
                    dve.scalar_tensor_tensor(out=St[:, :], in0=St[:, :], scalar=dec[:, k:k + 1], in1=SP_[:, 3, P:2 * P],
                                             op0=ALU.mult, op1=ALU.add).then_inc(st_ready.sem, 1)

            def o_norm(h, u):
                src, g = (oraw, subg[:, 0:1]) if u < 2 else (braw, vec[:, VEC["hgrn_g"][0]:VEC["hgrn_g"][0] + 1])
                s = slice((u % 2) * 512, (u % 2) * 512 + 512)
                dve.wait_ge(o_rstd.sem, o_rstd.at(h, u + 1))
                if u >= 2:
                    dve.wait_ge(o_lo.sem, o_lo.at(h, 2))
                if u < 2:
                    dve.scalar_tensor_tensor(out=E[:, 1, s], in0=src[:, s], scalar=g, in1=E[:, 0, s], op0=ALU.mult,
                                             op1=ALU.mult).then_inc(o_normed.sem, 1)
                else:
                    ch(dve.scalar_tensor_tensor(out=E[:, 1, s], in0=src[:, s], scalar=g, in1=E[:, 0, s], op0=ALU.mult, op1=ALU.mult))
                    ch.sync()
                    dve.tensor_tensor(E[:, 1, s], E[:, 1, s], og[:, s], ALU.mult).then_inc(o_normed.sem, 1)

            with dve.Fori(0, H) as h:
                done = 0
                for i in range(NB):
                    maxima(h, i)
                    weigh(h, i)
                    if i == 5:
                        cumulate(h)
                    for n in ATT_PIECES[i]:
                        if n in SIGMOID:
                            s = SIGMOID.index(n)
                            if s == 0:
                                dve.wait_ge(rec_done.sem, rec_done.at(h, 0))
                                dve.wait_ge(sample_rec.sem, sample_rec.at(h, 0))
                            cut(h, s)
                            if s:
                                use_sigmoid(h, s - 1)
                use_sigmoid(h, len(SIGMOID) - 1)
                operands(h, 0)
                for k in range(NB):
                    assemble(h, k)
                    if k + 1 < NB:
                        operands(h, k + 1)
                    if k == 0:
                        o_norm(h, 0)
                        o_norm(h, 1)
                    if 1 <= k <= 6:
                        u = k - 1
                        j = u % NP
                        dve.wait_ge(qk_summed.sem, qk_summed.at(h, u + 1))
                        rope(j, u % 2)
                        dve.wait_ge(qk_rstd.sem, qk_rstd.at(h, u + 1))
                        if u == 0:
                            dve.wait_ge(sample_qkv.sem, sample_qkv.at(h, 1))
                            dve.wait_ge(kv_stored.sem, kv_stored.at(h, 2))
                        rope_end(j, qT if u < 3 else kT)
                    state(h, k)
                o_norm(h, 2)
                o_norm(h, 3)
                ch.reset()


def gates_stage(nc, a, o, c, d, xh, xl, gate):
    with Stage(c) as ctx:
        mem = Memory(nc, "g", R2, R3)
        W = Stream(ctx, nc, mem, "g")
        kp = [mem(f"kp{i}", [P, D]) for i in range(2)]
        vp = mem("vp", [P, PAGES, D])
        qB, DG, st = mem("qB", [P, D]), mem("DG", [P, D]), mem("st", [P, D])
        s_tok = mem("s_tok", [P, PAGES, 2 * H])
        pd = mem("pd", [P, 2 * H])
        sc = mem("sc", [2 * H, PAST + 1])
        sv = mem("sv", [2 * H, 8])
        ge = mem("ge", [P, NT])
        pn = mem("pn", [2 * H, P])
        pt = mem("pt", [P, (PAGES + 1) * H])
        vn = mem("vn", [P, H])
        comb, coef = mem("comb", [2 * H, H]), mem("coef", [2 * H, 3])
        blk2 = mem("blk2", [P, 2])
        pages = mem("pages", [1, NS * PAGES], I32)
        subg = mem("subg", [P, 1])
        nsq, nrs = mem("nsq", [P, 2, H * NS]), mem("nrs", [P, 2, H * NS])
        nhi, nlo = mem("nhi", [P, 2, H * NS], F32R), mem("nlo", [P, 2, H * NS], F32R)
        Y = ctx.enter_context(nc.psum_tensor("g_Y", [P, 2, 512], F32))
        Yf = Y[:, :, :].rearrange("p a b -> p (a b)")

        def S(n, per=1, **k):
            return Sig(ctx, nc, f"g_{n}", per=per, **k)

        consts, page_in = S("consts_in", 0, step=16), S("pages_in", 0, step=16)
        k_in = [S(f"k_in{i}", 2, step=16) for i in range(2)]
        v_in, st_in, st_out = S("v_in", 4, step=16), S("st_in", step=16), S("st_out", step=16, init=1)
        diag_q, q_spread, q_copied = S("diag_q"), S("q_spread"), S("q_copied")
        k_scaled, k_summed = S("k_scaled", 2), S("k_summed", 4, init=2)
        diag_v, v_spread = S("diag_v"), S("v_spread")
        st_new, rec_out, rec_read = S("st_new"), S("rec_out"), S("rec_read")
        s_turned, s_max, s_exp, s_norm = S("s_turned"), S("s_max"), S("s_exp"), S("s_norm")
        p_turned, p_read, pv, pv_read = S("p_turned"), S("p_read"), S("pv", init=1), S("pv_read", init=1)
        gate_e, gate_cut = S("gate_e", 2), S("gate_cut", 2)
        n_sq, n_sum, n_rs, n_norm, n_hi, n_lo, n_st = (S("n_" + n) for n in ("sq", "sum", "rs", "norm", "hi", "lo", "st"))
        block = ctx.enter_context(nc.Block())
        wt = a["w_in"]
        N_CONST = 3

        def pair(ap, i):
            return ap[:, :, bass.ds(i, 1)]

        @block.sync
        def _(sp):
            for t, n in ((comb, "comb"), (blk2, "blk2"), (coef, "coef")):
                sp.dma_start(t[:, :], a[n]).then_inc(consts.sem, 16)
            sp.dma_start(pages[:, :], a["pages"]).then_inc(page_in.sem, 16)
            sp.wait_ge(page_in.sem, 16)

            def body(i, last):
                for s in range(2):
                    W.load(sp, i, s, flat(wt[bass.ds(i * 2 + (s + NTL * H), 1)]))
                sp.wait_ge(st_out.sem, st_out.at(i, 0))
                sp.dma_start(st[:, :], flat(a["state"][bass.ds(i, 1)])).then_inc(st_in.sem, 16)
                sp.wait_ge(pv.sem, pv.at(i, 0))
                for j in range(PAGES):
                    page = sp.value_load(pages[0:1, bass.ds(i * PAGES + j, 1)], min_val=0, max_val=POOL_PAGES - 1)
                    sp.wait_ge(k_summed.sem, k_summed.at(i, j - 1))
                    sp.dma_start(kp[j % 2][:, :], flat(a["cache_k"][bass.ds(page, 1)])).then_inc(k_in[j % 2].sem, 16)
                    sp.dma_start(vp[:, j, :], flat(a["cache_v"][bass.ds(page, 1)])).then_inc(v_in.sem, 16)
            turns(sp, NS, body)

        @block.scalar
        def _(act):
            act.preload_act_table_set(TABLES)
            W.head_start(act=act)
            W.free.start(act)
            st_out.start(act)
            ch = Chain(ctx, nc, act, "g_act_chain")
            W.split_hi(act, 0, 0)

            def body(i, last):
                for s in range(2):
                    if s == 0:
                        W.split_hi(act, i, 1)
                    elif not last:
                        W.split_hi(act, i + 1, 0)
                    for j in range(NP):
                        ch.sync()
                        W.wait_piece(act, i, s, j)
                        act.activation(ge[:, cols(j)], W.out(s, j), ACT.Exp, scale=-1.0).then_inc(W.free.sem, 1)
                        if (s, j) == (0, 0):
                            act.wait_ge(q_spread.sem, q_spread.at(i, 1))
                            act.activation(qB[:, :], Yf, ACT.Copy).then_inc(q_copied.sem, 1)
                        if (s, j) == (1, 0):
                            act.wait_ge(s_max.sem, s_max.at(i, 1))
                            act.activation(sc[:, :], sc[:, :], ACT.Exp, bias=sv[:, 1:2], scale=SCALE,
                                           accum_out=sv[:, 2:3]).then_inc(s_exp.sem, 1)
                    act.wait_ge(gate_cut.sem, gate_cut.at(i, s + 1))
                    ch(act.activation(ge[:, :], ge[:, :], ACT.Ln))
                    ch.sync()
                    ch(act.activation(gate[s][:, bass.ds(i, 1), :].rearrange("p o n -> p (o n)"), ge[:, :], ACT.Exp, scale=-1.0))
                    if s == 0:
                        act.wait_ge(st_new.sem, st_new.at(i, 1))
                        act.dma_start(flat(o["s_state"][bass.ds(i, 1)]), st[:, :]).then_inc(st_out.sem, 16)
                ch.reset()
            turns(act, NS, body)
            act.wait_ge(n_sum.sem, 1)
            ch(act.activation(nrs[:, :, :], Y[:, 0, 0:2 * H * NS].rearrange("p (a b) -> p a b", a=2), ACT.Ln, bias=c["eps"][:, 0:1]))
            ch.sync()
            act.activation(nrs[:, :, :], nrs[:, :, :], ACT.Exp, scale=-0.5).then_inc(n_rs.sem, 1)
            act.wait_ge(n_norm.sem, 1)
            act.activation(nhi[:, :, :], nsq[:, :, :], ACT.Copy).then_inc(n_hi.sem, 1)
            act.wait_ge(n_lo.sem, 1)
            act.wait_ge(n_hi.sem, 1)
            for b, name in enumerate(("oa", "ob")):
                for part, t in (("hi", nhi), ("lo", nlo)):
                    act.dma_start(d[name + part][:, :, T:NT].rearrange("h p n -> p h n"),
                                  t[:, b, :].bitcast(F32).rearrange("p (h n) -> p h n", h=H)).then_inc(n_st.sem, 16)
            act.wait_ge(n_st.sem, 64)
            act.wait_ge(st_out.sem, st_out.at(NS, 0))

        @block.tensor
        def _(pe):
            W.head_start(pe=pe)
            pv.start(pe)
            ones, ident = c["ones"], c["ident"]
            pe.wait_ge(consts.sem, 16 * N_CONST)

            def spread():
                for b in range(2):
                    ins = pe.matmul(Y[:, b, :], ones[:, :], DG[:, b * 512:(b + 1) * 512], start=True, stop=True)
                return ins

            def body(i, last):
                for s in range(2):
                    for j in range(NP):
                        W.piece(pe, i, s, j, xh, xl)
                        if (s, j) == (0, 0):
                            pe.wait_ge(diag_q.sem, diag_q.at(i, 1))
                            pe.wait_ge(pv_read.sem, pv_read.at(i, 0))
                            spread().then_inc(q_spread.sem, 1)
                        if (s, j) == (0, 1):
                            pe.wait_ge(diag_v.sem, diag_v.at(i, 1))
                            pe.wait_ge(q_copied.sem, q_copied.at(i, 1))
                            spread().then_inc(v_spread.sem, 1)
                        if (s, j) == (0, 2):
                            pe.wait_ge(st_new.sem, st_new.at(i, 1))
                            for b in range(NS):
                                ins = pe.matmul(Y[:, 1, b:b + 1], st[:, b * P:(b + 1) * P],
                                                c["s_qh"][:, bass.ds(i, 1), b:b + 1].rearrange("p o n -> p (o n)"),
                                                start=True, stop=True)
                            ins.then_inc(rec_out.sem, 1)
                        if (s, j) == (1, 0):
                            pe.wait_ge(k_summed.sem, k_summed.at(i, PAGES))
                            pe.wait_ge(rec_read.sem, rec_read.at(i, 1))
                            for b in range(PAGES):
                                pe.transpose(Y[0:2 * H, 0, b * P:(b + 1) * P], s_tok[:, b, :], ident[:, :])
                            pe.matmul(Y[0:2 * H, 1, 0:1], pd[:, :], ones[:, 0:1], start=True, stop=True).then_inc(s_turned.sem, 1)
                        if (s, j) == (1, 1):
                            pe.wait_ge(s_norm.sem, s_norm.at(i, 1))
                            for b in range(PAGES):
                                pe.matmul(Y[:, 0, b * H:(b + 1) * H], sc[:, b * P:(b + 1) * P], comb[:, :], start=True, stop=True)
                            pe.matmul(Y[:, 0, PAGES * H:(PAGES + 1) * H], pn[:, :], comb[:, :], start=True, stop=True)\
                              .then_inc(p_turned.sem, 1)
                        if (s, j) == (1, 2):
                            pe.wait_ge(p_read.sem, p_read.at(i, 1))
                            pe.wait_ge(v_in.sem, v_in.at(i, PAGES))
                            for h in range(H):
                                for b in range(PAGES):
                                    ins = pe.matmul(Y[:, 1, h:h + 1], vp[:, b, h * P:(h + 1) * P], pt[:, b * H + h:b * H + h + 1],
                                                    start=(b == 0), stop=(b == PAGES - 1))
                            ins.then_inc(pv.sem, 1)
            turns(pe, NS, body)
            pe.wait_ge(n_sq.sem, 1)
            pe.matmul(Y[:, 0, 0:2 * H * NS], c["ones128"][:, :], nsq[:, :, :].rearrange("p a b -> p (a b)"),
                      start=True, stop=True).then_inc(n_sum.sem, 1)

        @block.gpsimd
        def _(pool):
            ctx.clear_last(pool)
            W.head_start(pool=pool)

            W.split_lo(pool, 0, 0)

            def body(i, last):
                W.split_lo(pool, i, 1)
                for j in (2, 3):
                    pool.wait_ge(q_copied.sem, q_copied.at(i, 1))
                    pool.wait_ge(k_in[j % 2].sem, k_in[j % 2].at(i, 2))
                    pool.tensor_tensor(kp[j % 2][:, :], kp[j % 2][:, :], qB[:, :], ALU.mult).then_inc(k_scaled.sem, 1)
                if not last:
                    W.split_lo(pool, i + 1, 0)
            turns(pool, NS, body)
            pool.wait_ge(n_hi.sem, 1)
            pool.tensor_tensor(nlo[:, :, :], nsq[:, :, :], nhi[:, :, :].bitcast(F32), ALU.subtract).then_inc(n_lo.sem, 1)

        @block.vector
        def _(dve):
            k_summed.start(dve)
            pv_read.start(dve)
            ch = Chain(ctx, nc, dve, "g_dve_chain")
            ident = c["ident"]
            dve.wait_ge(consts.sem, 16 * N_CONST)
            ch(dve.tensor_scalar(subg[:, :], c["vec"][:, VEC["sub_g"][0]:VEC["sub_g"][0] + 1], 1.0 - LAM_INIT, None, ALU.mult))
            ch(dve.tensor_tensor(coef[:, 2:3], coef[:, 1:2], c["lam"][0:2 * H, 3:4], ALU.mult))
            ch.sync()
            ch(dve.tensor_tensor(coef[:, 2:3], coef[:, 2:3], coef[:, 0:1], ALU.add))
            ch.sync()
            ch.reset()
            per_head = DG[:, :].rearrange("p (h m) -> p h m", h=H)

            def sum_page(i, j):
                ch(dve.tensor_reduce(s_tok[:, j, :], kp[j % 2][:, :].rearrange("p (h n) -> p h n", n=DH), AX.X, ALU.add))
                ch.sync()
                dve.sem_inc(k_summed.sem, 1)

            def diagonal(vals):
                return dve.tensor_tensor(per_head, ident[:, :].unsqueeze(1).broadcast_to([P, H, P]), vals.broadcast_to([P, H, P]), ALU.mult)

            def cut(i, s):
                W.wait_piece(dve, i, s, 2)
                dve.wait_ge(W.free.sem, W.free.at(i, 3 * s + 3))
                dve.tensor_scalar(ge[:, :], ge[:, :], BIG, 1.0, ALU.min, ALU.add).then_inc(gate_cut.sem, 1)

            def body(i, last):
                sq, sk, sv_, skk, sf, sib, sob, soa = (c["s_" + n] for n in ("q", "k", "v", "kk", "f", "ib", "ob", "oa"))

                def head(t):
                    return t[:, bass.ds(i, 1), :].rearrange("p o n -> p (o n)").unsqueeze(2)
                dve.wait_ge(pv_read.sem, pv_read.at(i, 0))
                diagonal(pair(sq, i)).then_inc(diag_q.sem, 1)
                ch(dve.tensor_tensor(vn[:, :].unsqueeze(2), pair(sq, i), pair(sk, i), ALU.mult))
                ch.sync()
                ch(dve.tensor_tensor(pd[:, :].rearrange("p (h n) -> p h n", n=2), vn[:, :].unsqueeze(2).broadcast_to([P, H, 2]),
                                     blk2[:, :].unsqueeze(1).broadcast_to([P, H, 2]), ALU.mult))
                for j in range(2):
                    dve.wait_ge(k_in[j].sem, k_in[j].at(i, 1))
                    dve.wait_ge(q_copied.sem, q_copied.at(i, 1))
                    if j == 0:
                        diagonal(head(sib)).then_inc(diag_v.sem, 1)
                    ch(dve.tensor_tensor(kp[j][:, :], kp[j][:, :], qB[:, :], ALU.mult))
                    ch.sync()
                    sum_page(i, j)
                st3 = st[:, :].rearrange("p (b v) -> p b v", b=NS)
                dve.wait_ge(st_in.sem, st_in.at(i, 1))
                ch(dve.tensor_tensor(st3, st3, head(sf).broadcast_to([P, NS, P]), ALU.mult))
                dve.wait_ge(v_spread.sem, v_spread.at(i, 1))
                ch(dve.tensor_tensor(DG[:, :].rearrange("p (b v) -> p b v", b=NS), Yf.rearrange("p (b v) -> p b v", b=NS),
                                     head(skk).broadcast_to([P, NS, P]), ALU.mult))
                ch.sync()
                dve.tensor_tensor(st[:, :], st[:, :], DG[:, :], ALU.add).then_inc(st_new.sem, 1)
                for j in (2, 3):
                    dve.wait_ge(k_scaled.sem, k_scaled.at(i, j - 1))
                    sum_page(i, j)
                dve.wait_ge(rec_out.sem, rec_out.at(i, 1))
                copy(dve, head(sob).rearrange("p n o -> p (n o)"), Y[:, 1, 0:NS]).then_inc(rec_read.sem, 1)
                cut(i, 0)
                dve.wait_ge(s_turned.sem, s_turned.at(i, 1))
                ch(dve.tensor_copy(sc[:, 0:PAST], Y[0:2 * H, 0, :]))
                ch(dve.tensor_copy(sc[:, PAST:PAST + 1], Y[0:2 * H, 1, 0:1]))
                ch.sync()
                ch(dve.tensor_reduce(sv[:, 0:1], sc[:, :], AX.X, ALU.max))
                ch.sync()
                dve.tensor_scalar(sv[:, 1:2], sv[:, 0:1], -SCALE, None, ALU.mult).then_inc(s_max.sem, 1)
                dve.wait_ge(s_exp.sem, s_exp.at(i, 1))
                ch(dve.reciprocal(sv[:, 3:4], sv[:, 2:3]))
                ch.sync()
                ch(dve.tensor_tensor(sv[:, 3:4], sv[:, 3:4], coef[:, 2:3], ALU.mult))
                ch.sync()
                ch(dve.tensor_scalar(sc[:, :], sc[:, :], sv[:, 3:4], None, ALU.mult))
                ch.sync()
                dve.tensor_scalar(pn[:, :], c["ones"][0:2 * H, :], sc[:, PAST:PAST + 1], None, ALU.mult).then_inc(s_norm.sem, 1)
                dve.wait_ge(p_turned.sem, p_turned.at(i, 1))
                dve.tensor_copy(pt[:, :], Y[:, 0, 0:(PAGES + 1) * H]).then_inc(p_read.sem, 1)
                dve.wait_ge(p_read.sem, p_read.at(i, 1))
                ch(dve.tensor_tensor(vn[:, :].unsqueeze(2), pair(sv_, i), pt[:, PAGES * H:].unsqueeze(2), ALU.mult))
                ch.sync()
                dve.wait_ge(pv.sem, pv.at(i, 1))
                dve.tensor_tensor(pair(soa, i), Y[:, 1, 0:H].unsqueeze(2), vn[:, :].unsqueeze(2), ALU.add).then_inc(pv_read.sem, 1)
                cut(i, 1)
                ch.reset()
            turns(dve, NS, body)
            dve.wait_ge(rec_read.sem, rec_read.at(NS, 0))
            srcs = [c["s_oa"][:, :, :].rearrange("p a b -> p (a b)"), c["s_ob"][:, :, :].rearrange("p a b -> p (a b)")]
            dve.wait_ge(pv_read.sem, pv_read.at(NS, 0))
            ch(dve.tensor_tensor(nsq[:, 0, :], srcs[0], srcs[0], ALU.mult))
            dve.tensor_tensor(nsq[:, 1, :], srcs[1], srcs[1], ALU.mult).then_inc(n_sq.sem, 1)
            dve.wait_ge(n_rs.sem, 1)
            ch(dve.scalar_tensor_tensor(out=nsq[:, 0, :], in0=srcs[0], scalar=subg[:, 0:1], in1=nrs[:, 0, :], op0=ALU.mult, op1=ALU.mult))
            hg = c["vec"][:, VEC["hgrn_g"][0]:VEC["hgrn_g"][0] + 1]
            ch(dve.scalar_tensor_tensor(out=nsq[:, 1, :], in0=srcs[1], scalar=hg, in1=nrs[:, 1, :], op0=ALU.mult, op1=ALU.mult))
            ch.sync()
            dve.tensor_tensor(nsq[:, 1, :], nsq[:, 1, :], c["s_og"][:, :, :].rearrange("p a b -> p (a b)"), ALU.mult).then_inc(n_norm.sem, 1)


def branch_stage(nc, a, c, d, which, oh, ol, gate, mh, ml):
    NTURN, ADA = KT // 2, 4
    with Stage(c) as ctx:
        name = f"b{which}"
        mem = Memory(nc, name, R2, R3)
        W = Stream(ctx, nc, mem, name)
        aw = [mem(f"aw{i}", [P, KT * P]) for i in range(2)]
        m = [mem(f"m{i}", [P, TH]) for i in range(2)]
        pa = ctx.enter_context(nc.psum_tensor(f"{name}_ada", [P, 2, 512], F32))

        def S(n, per, **k):
            return Sig(ctx, nc, f"{name}_{n}", per=per, **k)

        x_in = [S(f"x_in{k}", 0, step=16) for k in range(KT)]
        ada_in = [S(f"ada_in{i}", ADA // 2, step=16) for i in range(2)]
        ada_done, ada_read = S("ada_done", ADA, init=2), S("ada_read", ADA, init=2)
        merged, m_hi, m_lo = S("merged", 6), S("m_hi", 6), S("m_lo", 6, init=2)
        block = ctx.enter_context(nc.Block())
        src = "oa" if which == 0 else "ob"
        wt = a["w_a"] if which == 0 else a["w_b"]

        @block.sync
        def _(sp):
            for s in range(2):
                W.load(sp, 0, s, flat(wt[s:s + 1]))
            for k in range(KT):
                sp.dma_start(oh[:, k, :].bitcast(F32), flat(d[src + "hi"][k:k + 1])).then_inc(x_in[k].sem, 16)
                sp.dma_start(ol[:, k, :].bitcast(F32), flat(d[src + "lo"][k:k + 1])).then_inc(x_in[k].sem, 16)

            def ada(i):
                for n in range(ADA):
                    sp.wait_ge(ada_done.sem, ada_done.at(i, n - 1))
                    sp.dma_start(aw[n % 2][:, :], flat(a["w_ada"][bass.ds(i * ADA + (n + 2 * KT + which * ADA * NTURN), 1)]))\
                      .then_inc(ada_in[n % 2].sem, 16)

            def body(i, last):
                ada(i)
                if not last:
                    for s in range(2):
                        W.load(sp, i + 1, s, flat(wt[bass.ds(i * 2 + (s + 2), 1)]))
            turns(sp, NTURN, body)

        @block.scalar
        def _(act):
            W.head_start(act=act)
            W.split_hi(act, 0, 0)

            def body(i, last):
                for s in range(2):
                    if s == 0:
                        W.split_hi(act, i, 1)
                    elif not last:
                        W.split_hi(act, i + 1, 0)
            turns(act, NTURN, body)

        @block.tensor
        def _(pe):
            W.head_start(pe=pe)
            ada_done.start(pe)
            for k in range(KT):
                pe.wait_ge(x_in[k].sem, 32)

            def ada(i, n):
                pe.wait_ge(ada_in[n % 2].sem, ada_in[n % 2].at(i, n // 2 + 1))
                pe.wait_ge(ada_read.sem, ada_read.at(i, n - 1))
                for k in range(KT):
                    ins = pe.matmul(pa[:, n % 2, 0:CS], aw[n % 2][:, k * P:(k + 1) * P], c["csil"][:, k, :], start=(k == 0), stop=(k == KT - 1))
                ins.then_inc(ada_done.sem, 1)

            def body(i, last):
                for s in range(2):
                    for j in range(NP):
                        W.piece(pe, i, s, j, oh, ol)
                        if j < 2:
                            ada(i, 2 * s + j)
            turns(pe, NTURN, body)

        @block.gpsimd
        def _(pool):
            ctx.clear_last(pool)
            W.head_start(pool=pool)
            if which:
                m_lo.start(pool)
            W.split_lo(pool, 0, 0)

            def body(i, last):
                for s in range(2):
                    if s == 0:
                        W.split_lo(pool, i, 1)
                    elif not last:
                        W.split_lo(pool, i + 1, 0)
                    if which:
                        for j in range(NP):
                            n = 3 * s + j
                            pool.wait_ge(m_hi.sem, m_hi.at(i, n + 1))
                            hi, lo = (t[:, bass.ds(i * 2 + s, 1), cols(j)].rearrange("p o n -> p (o n)") for t in (mh, ml))
                            pool.tensor_tensor(lo, m[n % 2][:, :], hi.bitcast(F32), ALU.subtract).then_inc(m_lo.sem, 1)
            turns(pool, NTURN, body)

        @block.vector
        def _(dve):
            W.free.start(dve)
            ada_read.start(dve)
            ch = Chain(ctx, nc, dve, f"{name}_dve_chain")

            def body(i, last):
                for s in range(2):
                    for j in range(NP):
                        n = 3 * s + j
                        g0, g1 = (g[:, bass.ds(i * 2 + s, 1), cols(j)].rearrange("p o n -> p (o n)") for g in gate)
                        W.wait_piece(dve, i, s, j)
                        if which == 0:
                            dve.tensor_tensor(g0, W.out(s, j), g0, ALU.mult).then_inc(W.free.sem, 1)
                        else:
                            dve.wait_ge(m_lo.sem, m_lo.at(i, n - 1))
                            dve.tensor_tensor(m[n % 2][:, :], W.out(s, j), g1, ALU.mult).then_inc(W.free.sem, 1)
                            dve.wait_ge(W.free.sem, W.free.at(i, n + 1))
                            dve.tensor_tensor(m[n % 2][:, :], m[n % 2][:, :], g0, ALU.add).then_inc(merged.sem, 1)
                            dve.wait_ge(merged.sem, merged.at(i, n + 1))
                            copy(dve, mh[:, bass.ds(i * 2 + s, 1), cols(j)].rearrange("p o n -> p (o n)"), m[n % 2][:, :])\
                               .then_inc(m_hi.sem, 1)
                        if j < 2:
                            t = 2 * s + j
                            dve.wait_ge(ada_done.sem, ada_done.at(i, t + 1))
                            tile = i * ADA + (t + 2 * KT + which * ADA * NTURN)
                            dve.tensor_scalar(c["mod"][:, bass.ds(tile, 1), :].rearrange("p o n -> p (o n)"), pa[:, t % 2, 0:CS],
                                              c["vec"][:, bass.ds(tile, 1)], None, ALU.add).then_inc(ada_read.sem, 1)
            turns(dve, NTURN, body)


def output_stage(nc, a, c, x, mh, ml):
    NTURN = KT // 2
    with Stage(c) as ctx:
        mem = Memory(nc, "o", R2, R3)
        mem.off = R2 + WIDE
        W = Stream(ctx, nc, mem, "o")
        t8 = mem("t8", [P, NS])
        x_in = Sig(ctx, nc, "o_x_in", step=16)
        block = ctx.enter_context(nc.Block())

        @block.sync
        def _(sp):
            W.load(sp, 0, 0, flat(a["w_out"][0:1]))
            W.load(sp, 0, 1, flat(a["w_out"][1:2]))
            sp.dma_start(x[:, :, :], a["xT"]).then_inc(x_in.sem, 16)

            def body(i, last):
                if not last:
                    for s in range(2):
                        W.load(sp, i + 1, s, flat(a["w_out"][bass.ds(i * 2 + (s + 2), 1)]))
            turns(sp, NTURN, body)

        @block.scalar
        def _(act):
            W.head_start(act=act)
            W.split_hi(act, 0, 0)

            def body(i, last):
                W.split_hi(act, i, 1)
                if not last:
                    W.split_hi(act, i + 1, 0)
            turns(act, NTURN, body)

        @block.tensor
        def _(pe):
            W.head_start(pe=pe)

            def body(i, last):
                for s in range(2):
                    for j in range(NP):
                        W.piece(pe, i, s, j, mh, ml)
            turns(pe, NTURN, body)

        @block.gpsimd
        def _(pool):
            ctx.clear_last(pool)
            W.head_start(pool=pool)
            W.split_lo(pool, 0, 0)

            def body(i, last):
                W.split_lo(pool, i, 1)
                if not last:
                    W.split_lo(pool, i + 1, 0)
            turns(pool, NTURN, body)

        @block.vector
        def _(dve):
            W.free.start(dve)
            ch = Chain(ctx, nc, dve, "o_dve_chain")
            dve.wait_ge(x_in.sem, 16)

            def body(i, last):
                for s in range(2):
                    xt = x[:, bass.ds(i * 2 + s, 1), :].rearrange("p o n -> p (o n)")
                    for j in range(NP):
                        W.wait_piece(dve, i, s, j)
                        add_residual(dve, ch, W, i, s, j, xt, c["mod"], i * 2 + (s + 2 * KT), t8)
                ch.reset()
            turns(dve, NTURN, body)


def add_residual(dve, ch, W, turn, s, j, x, mod, tile, t8):
    ps = W.out(s, j)
    a0, n = j * TH, (TH if j < NP - 1 else T - 2 * TH)
    f0 = mod[:, bass.ds(tile, 1), 0:1].rearrange("p o n -> p (o n)")
    ins = dve.scalar_tensor_tensor(out=x[:, a0:a0 + n], in0=ps[:, 0:n], scalar=f0, in1=x[:, a0:a0 + n], op0=ALU.mult, op1=ALU.add)
    if j == NP - 1:
        ch(ins)
        dve.wait_ge(W.free.sem, W.free.at(turn, 3 * s))
        ch(dve.tensor_tensor(t8[:, :], ps[:, n:TH], mod[:, bass.ds(tile, 1), 1:CS].rearrange("p o n -> p (o n)"), ALU.mult))
        ch.sync()
        ins = dve.tensor_tensor(x[:, T:NT], x[:, T:NT], t8[:, :], ALU.add)
    ins.then_inc(W.free.sem, 1)


def up_stage(nc, a, o, c, hh, hl, ah, al, g):
    f0, nf = GROUPS[g]
    with Stage(c) as ctx:
        name = f"u{g}"
        mem = Memory(nc, name, R2 + 2 * WIDE)
        W = Stream(ctx, nc, mem, name)
        u = [mem(f"u{s}", [P, 2 + NT]) for s in range(2)]
        y = [mem(f"y{s}", [P, NT]) for s in range(2)]
        e = mem("e", [P, NT])
        old = mem("old", [P, 2 * nf, 2, NS])
        new = mem("new", [P, 2 * nf, 2 + NS])
        cv = mem("cv", [P, 4 * 2 * FT])

        def S(n, per, **k):
            return Sig(ctx, nc, f"{name}_{n}", per=per, **k)

        old_in = S("old_in", 0, step=16)
        conved = S("conved", 2, init=2)
        e_raw, e_cut, e_sig, act_f, act_hi, act_lo = (S(n, 1, init=1) for n in ("e_raw", "e_cut", "e_sig", "act", "act_hi", "act_lo"))
        stored = S("stored", 0, step=16)
        block = ctx.enter_context(nc.Block())
        wt = a["w_up"]

        @block.sync
        def _(sp):
            for s in range(2):
                W.load(sp, 0, s, flat(wt[2 * f0 + s:2 * f0 + s + 1]))
            sp.dma_start(old[:, :, :, :], a["sconv"][:, 2 * f0:2 * (f0 + nf)]).then_inc(old_in.sem, 16)

            def body(i, last):
                if not last:
                    for s in range(2):
                        W.load(sp, i + 1, s, flat(wt[bass.ds(i * 2 + (2 * f0 + s + 2), 1)]))
            turns(sp, nf, body)
            sp.wait_ge(conved.sem, conved.at(nf, 0))
            sp.dma_start(o["conv"][:, 2 * f0:2 * (f0 + nf), :], new[:, :, :]).then_inc(stored.sem, 16)
            sp.wait_ge(old_in.sem, 16)
            sp.dma_start(o["conv_old"][:, 2 * f0:2 * (f0 + nf), :], old[:, :, 1, :]).then_inc(stored.sem, 16)
            sp.wait_ge(stored.sem, 32)

        @block.scalar
        def _(act):
            act.preload_act_table_set(TABLES)
            W.head_start(act=act)
            W.free.start(act)
            for sig in (e_raw, e_sig):
                sig.start(act)
            ch = Chain(ctx, nc, act, f"{name}_act_chain")
            W.split_hi(act, 0, 0)

            def read(i, s):
                act.wait_ge(conved.sem, conved.at(i, s - 1))
                for j in range(NP):
                    W.wait_piece(act, i, s, j)
                    act.activation(u[s][:, 2 + j * TH:2 + (j + 1) * TH], W.out(s, j), ACT.Copy).then_inc(W.free.sem, 1)

            def body(i, last):
                W.split_hi(act, i, 1)
                read(i, 0)
                if not last:
                    W.split_hi(act, i + 1, 0)
                act.wait_ge(conved.sem, conved.at(i, 1))
                act.wait_ge(act_f.sem, act_f.at(i, 0))
                act.activation(e[:, :], y[0][:, :], ACT.Exp, scale=-1.0).then_inc(e_raw.sem, 1)
                act.wait_ge(e_cut.sem, e_cut.at(i, 1))
                ch(act.activation(e[:, :], e[:, :], ACT.Ln))
                ch.sync()
                act.activation(e[:, :], e[:, :], ACT.Exp, scale=-1.0).then_inc(e_sig.sem, 1)
                read(i, 1)
                ch.reset()
            turns(act, nf, body)

        @block.tensor
        def _(pe):
            W.head_start(pe=pe)

            def body(i, last):
                for s in range(2):
                    for j in range(NP):
                        W.piece(pe, i, s, j, hh, hl)
            turns(pe, nf, body)

        @block.gpsimd
        def _(pool):
            ctx.clear_last(pool)
            W.head_start(pool=pool)
            act_lo.start(pool)
            W.split_lo(pool, 0, 0)

            def body(i, last):
                W.split_lo(pool, i, 1)
                if not last:
                    W.split_lo(pool, i + 1, 0)
                pool.wait_ge(act_hi.sem, act_hi.at(i, 1))
                hi, lo = (t[:, bass.ds(i, 1), :].rearrange("p o n -> p (o n)") for t in (ah, al))
                pool.tensor_tensor(lo, y[0][:, :], hi.bitcast(F32), ALU.subtract).then_inc(act_lo.sem, 1)
            turns(pool, nf, body)

        @block.vector
        def _(dve):
            conved.start(dve)
            e_cut.start(dve)
            act_f.start(dve)
            act_hi.start(dve)
            ch = Chain(ctx, nc, dve, f"{name}_dve_chain")
            for s in range(2):
                ch(dve.memset(u[s][:, 0:2], 0.0))
            n_cv, first = 2 * FT, VEC["conv_w"][0]
            ch(dve.tensor_copy(cv[:, :], c["vec"][:, first:first + 4 * n_cv]))
            dve.wait_ge(old_in.sem, 16)
            ch.sync()
            ch.reset()

            def conv(i, s):
                tile = i * 2 + (2 * f0 + s)
                own = i * 2 + s
                w = [cv[:, bass.ds(tile + r * n_cv, 1)] for r in range(4)]
                us, ys = u[s], y[s]
                st = [old[:, bass.ds(own, 1), r, :].rearrange("p o n -> p (o n)") for r in range(2)]
                W.wait_piece(dve, i, s, NP - 1)
                dve.wait_ge(W.free.sem, W.free.at(i, 3 * s + 3))
                if s == 0:
                    dve.wait_ge(act_hi.sem, act_hi.at(i, 0))
                    dve.wait_ge(act_lo.sem, act_lo.at(i, 0))
                ch(dve.tensor_scalar(ys[:, 0:T], us[:, 0:T], w[0], w[3], ALU.mult, ALU.add))
                ch(dve.tensor_scalar(ys[:, T:NT], st[0], w[0], w[3], ALU.mult, ALU.add))
                ch.sync()
                ch(dve.scalar_tensor_tensor(out=ys[:, 0:T], in0=us[:, 1:1 + T], scalar=w[1], in1=ys[:, 0:T], op0=ALU.mult, op1=ALU.add))
                ch(dve.scalar_tensor_tensor(out=ys[:, T:NT], in0=st[1], scalar=w[1], in1=ys[:, T:NT], op0=ALU.mult, op1=ALU.add))
                ch(copy(dve, new[:, bass.ds(own, 1), :].rearrange("p o n -> p (o n)"), us[:, T:T + 2 + NS]))
                ch.sync()
                dve.scalar_tensor_tensor(out=ys[:, :], in0=us[:, 2:2 + NT], scalar=w[2], in1=ys[:, :], op0=ALU.mult,
                                         op1=ALU.add).then_inc(conved.sem, 1)

            def body(i, last):
                conv(i, 0)
                dve.wait_ge(e_raw.sem, e_raw.at(i, 1))
                dve.tensor_scalar(e[:, :], e[:, :], BIG, 1.0, ALU.min, ALU.add).then_inc(e_cut.sem, 1)
                dve.wait_ge(e_sig.sem, e_sig.at(i, 1))
                ch(dve.tensor_tensor(y[0][:, :], y[0][:, :], e[:, :], ALU.mult))
                conv(i, 1)
                dve.wait_ge(conved.sem, conved.at(i, 2))
                dve.tensor_tensor(y[0][:, :], y[0][:, :], y[1][:, :], ALU.mult).then_inc(act_f.sem, 1)
                dve.wait_ge(act_f.sem, act_f.at(i, 1))
                copy(dve, ah[:, bass.ds(i, 1), :].rearrange("p o n -> p (o n)"), y[0][:, :]).then_inc(act_hi.sem, 1)
                ch.reset()
            turns(dve, nf, body)


def down_stage(nc, a, o, c, d, ah, al, g):
    f0, nf = GROUPS[g]
    NTURN = KT // 2
    src, dst = d["x1"][g], (d["x1"][g + 1] if g + 1 < len(GROUPS) else o["y"])
    with Stage(c) as ctx:
        name = f"d{g}"
        mem = Memory(nc, name, R2 + 2 * WIDE)
        W = Stream(ctx, nc, mem, name, nf)
        x = [mem(f"x{s}", [P, NT]) for s in range(2)]
        t8 = mem("t8", [P, NS])
        x_in = [Sig(ctx, nc, f"{name}_x_in{s}", per=1, step=16) for s in range(2)]
        x_out = [Sig(ctx, nc, f"{name}_x_out{s}", per=1, step=16, init=1) for s in range(2)]
        block = ctx.enter_context(nc.Block())
        wt = a["w_down"][:, :, f0 * P:(f0 + nf) * P]

        @block.sync
        def _(sp):
            def load(i, s, n):
                W.load(sp, i, s, flat(wt[n]))
                sp.wait_ge(x_out[s].sem, x_out[s].at(i, 0))
                sp.dma_start(x[s][:, :], flat(src[n])).then_inc(x_in[s].sem, 16)
            for s in range(2):
                load(0, s, slice(s, s + 1))

            def body(i, last):
                if not last:
                    for s in range(2):
                        load(i + 1, s, bass.ds(i * 2 + (s + 2), 1))
            turns(sp, NTURN, body)

        @block.scalar
        def _(act):
            W.head_start(act=act)
            for s in range(2):
                x_out[s].start(act)
            W.split_hi(act, 0, 0)

            def body(i, last):
                for s in range(2):
                    if s == 0:
                        W.split_hi(act, i, 1)
                    elif not last:
                        W.split_hi(act, i + 1, 0)
                    act.wait_ge(W.free.sem, W.free.at(i, 3 * s + 3))
                    act.dma_start(flat(dst[bass.ds(i * 2 + s, 1)]), x[s][:, :]).then_inc(x_out[s].sem, 16)
            turns(act, NTURN, body)
            for s in range(2):
                act.wait_ge(x_out[s].sem, x_out[s].at(NTURN, 0))

        @block.tensor
        def _(pe):
            W.head_start(pe=pe)

            def body(i, last):
                for s in range(2):
                    for j in range(NP):
                        W.piece(pe, i, s, j, ah, al)
            turns(pe, NTURN, body)

        @block.gpsimd
        def _(pool):
            ctx.clear_last(pool)
            W.head_start(pool=pool)
            W.split_lo(pool, 0, 0)

            def body(i, last):
                W.split_lo(pool, i, 1)
                if not last:
                    W.split_lo(pool, i + 1, 0)
            turns(pool, NTURN, body)

        @block.vector
        def _(dve):
            W.free.start(dve)
            ch = Chain(ctx, nc, dve, f"{name}_dve_chain")

            def body(i, last):
                for s in range(2):
                    dve.wait_ge(x_in[s].sem, x_in[s].at(i, 1))
                    for j in range(NP):
                        W.wait_piece(dve, i, s, j)
                        add_residual(dve, ch, W, i, s, j, x[s], c["mod"], i * 2 + (s + 5 * KT), t8)
                ch.reset()
            turns(dve, NTURN, body)


def program(nc, a, o):
    keep = Memory(nc, "keep", BASE, R1)
    c = {n: keep(n, [P, P]) for n in ("ident", "ones128", "ones")}
    c.update(vec=keep("vec", [P, VEC_W]), mod=keep("mod", [P, 6 * KT, CS]), csil=keep("csil", [P, KT, CS]),
             lam=keep("lam", [P, 8]), lb=keep("lb", [P, 2, H]), eps=keep("eps", [P, 1]))
    for n in ("q", "k", "v", "qh", "kk", "f", "ib", "og", "oa", "ob"):
        c["s_" + n] = keep("s_" + n, [P, H, NS])

    def scratch(name, dt):
        return nc.dram_tensor(name, (KT, P, NT), dt, kind="Internal").ap()

    d = {b + part: scratch(f"{b}_{part}", F32) for b in ("oa", "ob") for part in ("hi", "lo")}
    d["x1"] = [scratch(f"x_{g}", F32) for g in range(len(GROUPS))]

    def wide(name, at, dt=F32, n=KT):
        return nc.alloc_sbuf_tensor_at(name, [P, n, NT], dt, offset=at)

    xh, xl = wide("xn_hi", R1, F32R), wide("xn_lo", R1 + WIDE, F32R)
    x = wide("x", R2)
    norm_stage(nc, a, c, x, xh, xl, Memory(nc, "n1", R2 + WIDE), True)
    heads_stage(nc, a, o, c, d, xh, xl)
    gate = [wide("gate_a", R3), wide("gate_b", R3 + WIDE)]
    gates_stage(nc, a, o, c, d, xh, xl, gate)
    mh, ml = wide("merged_hi", R3, F32R), wide("merged_lo", R3 + WIDE, F32R)
    for which, b in enumerate(("oa", "ob")):
        oh, ol = wide(b + "_in_hi", R1, F32R), wide(b + "_in_lo", R1 + WIDE, F32R)
        branch_stage(nc, a, c, d, which, oh, ol, gate, mh, ml)
    x1 = wide("x1", R2)
    output_stage(nc, a, c, x1, mh, ml)
    hh, hl = wide("hn_hi", R1, F32R), wide("hn_lo", R1 + WIDE, F32R)
    norm_stage(nc, {**a, "x1_store": d["x1"][0]}, c, x1, hh, hl, Memory(nc, "n2", R2 + WIDE), False)
    for g, (f0, nf) in enumerate(GROUPS):
        ah, al = wide(f"act_hi{g}", R2, F32R, nf), wide(f"act_lo{g}", R2 + WIDE, F32R, nf)
        up_stage(nc, a, o, c, hh, hl, ah, al, g)
        down_stage(nc, a, o, c, d, ah, al, g)


def constants():
    f32 = np.float32
    k = {"ident": np.eye(P, dtype=f32), "ones": np.ones((P, P), f32), "ones128": np.full((P, P), 1 / P, f32),
         "ones1024": np.full((P, P), 1 / D, f32)}
    r = np.arange(P)
    k["blk"] = ((r[:, None] // DH) == (r[None, :] // DH)).astype(f32) / DH
    rot = np.zeros((P, P), f32)
    half = DH // 2
    for m in range(P):
        if m % DH < half:
            rot[m + half, m] = -1.0
        else:
            rot[m - half, m] = 1.0
    k["rot"] = rot
    inv = (f32(10000.0) ** (-np.arange(half, dtype=f32) / f32(half))).astype(f32)
    pos = np.concatenate([np.arange(T), np.full(NS, PAST)]).astype(f32)
    ang = (pos[:, None] * inv[None, :]).astype(f32).astype(np.float64)
    k["cos"] = np.ascontiguousarray(np.cos(ang).astype(f32).T[r % half])
    k["sin"] = np.ascontiguousarray(np.sin(ang).astype(f32).T[r % half])
    k["causal"] = np.where(r[None, :] <= r[:, None], 0.0, -1e30).astype(f32)
    m = np.zeros((P, LEVELS * HALF), np.uint32)
    for lv in range(LEVELS):
        b = 1 << lv
        for j in range(HALF):
            first = (j // b) * 2 * b
            m[first:first + b, lv * HALF + j] = 1
    k["lmask"] = m
    hc = np.arange(2 * H)
    k["comb"] = (hc[:, None] // 2 == np.arange(H)[None, :]).astype(f32)
    k["coef"] = np.stack([hc % 2 == 0, hc % 2 == 1, 0 * hc], 1).astype(f32)
    k["blk2"] = (r[:, None] // DH == np.arange(2)[None, :]).astype(f32)
    return k


def kernel(**inputs):
    import concourse.bacc as bacc
    from concourse.bass_utils import run_bass_kernel_spmd

    x = {n: np.asarray(v) for n, v in inputs.items()}
    f32 = np.float32

    def rows(v):
        return v.reshape(-1, P).T

    def tiles(w, order=None):
        kt, mt = w.shape[0] // P, w.shape[1] // P
        t = w.reshape(kt, P, mt, P).transpose(2, 1, 0, 3)
        return np.ascontiguousarray(t if order is None else t[order]).reshape(mt, P, kt * P)

    a = constants()
    tokens = np.concatenate([x["x_prompt"].reshape(T, D), x["x_sample"].reshape(NS, D)])
    a["xT"] = tokens.T.reshape(KT, P, NT).transpose(1, 0, 2)
    a["cT"] = np.concatenate([x["c_prompt"], x["c_sample"]]).T.reshape(KT, P, CS).transpose(1, 0, 2)
    a["w_ada"] = tiles(x["w_ada"][0])
    at = dict(zip(("q", "k", "v", "qh", "f", "ib", "og", "ga", "gb"), range(0, 9 * H, H)))
    order = [at[n] for n in ("q", "k", "v")]
    for h in range(H):
        order += [at[n] + h for n in ("f", "qh", "ib", "og")]
        if h + 1 < H:
            order += [at[n] + h + 1 for n in ("q", "k", "v")]
    gates = [at[n] + h for h in range(H) for n in ("ga", "gb")]
    a["w_in"] = tiles(x["w_in"][0], order + gates)
    a["w_a"], a["w_b"], a["w_out"] = tiles(x["w_branch_a"][0]), tiles(x["w_branch_b"][0]), tiles(x["w_out"][0])
    pairs = [s * FT + f for f in range(FT) for s in range(2)]
    a["w_up"] = tiles(x["w_up"][0], pairs)
    a["w_down"] = tiles(x["w_down"][0])
    conv_w = [rows(x["conv_w"][0, r])[:, pairs] for r in range(3)]
    lams = np.concatenate([x[n][0] for n in ("lambda_q1", "lambda_k1", "lambda_q2", "lambda_k2")])
    a["vec"] = np.concatenate(
        [rows(x["b_ada"][0]), rows(x["rms_mix_g"][0]), rows(x["rms_ffn_g"][0]), np.tile(x["q_norm_g"][0], 2)[:, None],
         np.tile(x["k_norm_g"][0], 2)[:, None], x["subln_g"][0][:, None], x["hgrn_norm_g"][0][:, None],
         rows(x["lb_logits"][0]), rows(x["lb_logits"][1])] + conv_w
        + [rows(x["conv_b"][0])[:, pairs], np.broadcast_to(lams, (P, 4 * DH))], axis=1)
    a["sconv"] = x["state_conv"][0].reshape(NS, 2, 2 * FT, P)[:, :, pairs].transpose(3, 2, 1, 0)
    a["state"] = x["state_hgrn"][0].transpose(1, 2, 0, 3).reshape(H, P, NS * P)
    a["cache_k"] = x["cache_k"][0].reshape(POOL_PAGES, P, D)
    a["cache_v"] = x["cache_v"][0].reshape(POOL_PAGES, P, D)
    a["pages"] = x["page_table"].reshape(1, NS * PAGES)
    outs = {"y": (KT, P, NT), "k": (H, P, NT), "v": (H, P, NT), "state": (H, P, P), "s_state": (H, P, NS * P),
            "conv": (P, 2 * FT, 2 + NS), "conv_old": (P, 2 * FT, NS)}

    nc = bacc.Bacc("TRN2", target_bir_lowering=False, num_devices=1)
    arrays, ins, res = {}, {}, {}
    for n, v in a.items():
        v = np.ascontiguousarray(v)
        arrays[f"in_{n}"] = v
        ins[n] = nc.dram_tensor(f"in_{n}", v.shape, mybir.dt.from_np(v.dtype), kind="ExternalInput").ap()
    for n, shape in outs.items():
        res[n] = nc.dram_tensor(f"out_{n}", shape, F32, kind="ExternalOutput").ap()
    program(nc, ins, res)
    r = run_bass_kernel_spmd(nc, [arrays], core_ids=[0]).results[0]
    r = {n: np.asarray(r[f"out_{n}"]) for n in outs}

    def per_token(v):
        return v.transpose(2, 0, 1).reshape(NT, -1)

    y, k, v = per_token(r["y"]), per_token(r["k"]), per_token(r["v"])
    back = np.argsort(pairs)
    conv = r["conv"][:, back].transpose(2, 1, 0).reshape(2 + NS, 2 * FF)
    old = r["conv_old"][:, back].transpose(2, 1, 0).reshape(NS, 2 * FF)
    C = np.ascontiguousarray
    return (C(y[:T].reshape(1, T, D)), C(y[T:].reshape(NS, 1, D)),
            C(k[:T].reshape(1, 1, T, H, 2, DH)), C(v[:T].reshape(1, 1, T, H, P)),
            C(r["state"].reshape(1, 1, H, P, P)), C(conv[:2].reshape(1, 1, 2, 2 * FF)),
            C(k[T:].reshape(1, NS, 1, H, 2, DH)), C(v[T:].reshape(1, NS, 1, H, P)),
            C(r["s_state"].reshape(H, P, NS, P).transpose(2, 0, 1, 3)[None]),
            C(np.stack([old, conv[2:]], 1)[None]))
```

```python
from contextlib import ExitStack

import concourse.bass as bass
import numpy as np
from concourse import mybir

F32 = mybir.dt.float32
F32R = mybir.dt.float32r
U32 = mybir.dt.uint32
I32 = mybir.dt.int32
ALU = mybir.AluOpType
ACT = mybir.ActivationFunctionType
AX = mybir.AxisListType

P = 128
D = 1024
T = 1024
NS = 8
NT = T + NS
NP = 3
TH = NT // NP
KT = D // P
H = 8
DH = 64
NB = T // P
PAST = 512
PAGES = PAST // P
POOL_PAGES = 40
FF = 2816
FT = FF // P
LEVELS = 7
HALF = P // 2
EPS = 1e-6
SCALE = DH ** -0.5
LAM_INIT = 0.2
BIG = 1e18
TABLES = "natural_log_exp_and_others"
FIRST_SEM, STAGE_SEMS = 99, 78
CS = NS + 1

VEC, _at = {}, 0
for _n, _w in (("b_ada", 6 * KT), ("mix_g", KT), ("ffn_g", KT), ("q_g", 1), ("k_g", 1), ("sub_g", 1), ("hgrn_g", 1),
               ("lb", 2 * H), ("conv_w", 3 * 2 * FT), ("conv_b", 2 * FT), ("lam", 4 * DH)):
    VEC[_n] = (_at, _w)
    _at += _w
VEC_W = _at
DMA_SCRATCH = 2048
BASE = DMA_SCRATCH + 128
KEEP_END = BASE + 9 * 1024
WIDE = KT * NT * 4
R1 = KEEP_END
R2 = R1 + 2 * WIDE
R_X = R2 + 6 * KT * P * 4
R_SQ = R_X + WIDE
TOP = 229344
R3 = TOP - 2 * WIDE


def cols(j):
    return slice(j * TH, (j + 1) * TH)


class Stage(ExitStack):

    def __init__(self, c):
        super().__init__()
        self.last, c["stage"] = c.get("stage"), self
        self.first = FIRST_SEM if self.last is None or self.last.first != FIRST_SEM else FIRST_SEM + STAGE_SEMS
        self.n = 0

    def semaphore(self, nc, name):
        self.n += 1
        assert self.n <= STAGE_SEMS, name
        return self.enter_context(nc.semaphore(name, num=self.first + self.n - 1))

    def clear_last(self, eng):
        if self.last is not None:
            eng.sem_clear(range(self.last.first, self.last.first + self.last.n))


class Sig:

    def __init__(self, ctx, nc, name, per=0, pre=0, init=0, step=1):
        self.sem = ctx.semaphore(nc, name)
        self.per, self.pre, self.init, self.step, self.name = per, pre, init, step, name

    def start(self, eng):
        eng.sem_inc(self.sem, self.init * self.step)

    def at(self, turn, k):
        least = self.init + self.pre + k
        assert least + (self.per * turn if isinstance(turn, int) else 0) > 0, (self.name, turn, k)
        return turn * (self.per * self.step) + self.step * least

    def before(self, k):
        assert self.init + k > 0, (self.name, k)
        return self.step * (self.init + k)


class Chain:

    def __init__(self, ctx, nc, eng, name):
        self.sem, self.eng, self.n = ctx.semaphore(nc, name), eng, 0

    def __call__(self, ins):
        self.n += 1
        ins.then_inc(self.sem, 1)

    def sync(self):
        if self.n:
            self.eng.wait_ge(self.sem, self.n)

    def reset(self):
        if self.n:
            self.sync()
            self.eng.sem_clear(self.sem)
            self.n = 0


class Memory:

    def __init__(self, nc, name, at, end=TOP):
        self.nc, self.name, self.off, self.end = nc, name, at, end

    def __call__(self, name, shape, dt=F32):
        t = self.nc.alloc_sbuf_tensor_at(f"{self.name}_{name}", shape, dt, offset=self.off)
        self.off += -(-int(np.prod(shape[1:])) * 4 // 32) * 32
        assert self.off <= self.end, (self.name, name, self.off - self.end)
        return t


def product(eng, out, whi, wlo, xhi, xlo, n_k, columns):
    for k in range(n_k):
        for n, (w, x) in enumerate(((whi, xhi), (whi, xlo), (wlo, xhi))):
            ins = eng.matmul(out, w[:, k * P:(k + 1) * P], x[:, k, columns],
                             start=(k == 0 and n == 0), stop=(k == n_k - 1 and n == 2))
    return ins


class Stream:

    def __init__(self, ctx, nc, slots, name):
        self.n_k, (self.raw, self.hi, self.lo) = KT, slots
        self.ps = ctx.enter_context(nc.psum_tensor(f"{name}_ps", [P, 6, 512], F32))
        self.loaded = [Sig(ctx, nc, f"{name}_w_loaded{s}", per=1, step=16) for s in range(2)]
        self.hi_done = Sig(ctx, nc, f"{name}_w_hi_done", per=2, init=2)
        self.lo_done = Sig(ctx, nc, f"{name}_w_lo_done", per=2, init=2)
        self.done = Sig(ctx, nc, f"{name}_piece_done", per=6, init=6)
        self.free = Sig(ctx, nc, f"{name}_piece_free", per=6, init=6)

    def load(self, sp, turn, s, src):
        sp.wait_ge(self.hi_done.sem, self.hi_done.at(turn, s - 1))
        sp.wait_ge(self.lo_done.sem, self.lo_done.at(turn, s - 1))
        sp.dma_start(self.raw[s][:, :], src).then_inc(self.loaded[s].sem, 16)

    def split_hi(self, act, turn, s):
        act.wait_ge(self.loaded[s].sem, self.loaded[s].at(turn, 1))
        act.wait_ge(self.done.sem, self.done.at(turn, 3 * s - 3))
        act.activation(self.hi[s][:, :], self.raw[s][:, :], ACT.Copy).then_inc(self.hi_done.sem, 1)

    def split_lo(self, pool, turn, s):
        pool.wait_ge(self.loaded[s].sem, self.loaded[s].at(turn, 1))
        pool.wait_ge(self.hi_done.sem, self.hi_done.at(turn, s + 1))
        pool.wait_ge(self.done.sem, self.done.at(turn, 3 * s - 3))
        pool.tensor_tensor(self.lo[s][:, :], self.raw[s][:, :], self.hi[s][:, :].bitcast(F32), ALU.subtract)\
            .then_inc(self.lo_done.sem, 1)

    def piece(self, pe, turn, s, j, xhi, xlo):
        if j == 0:
            pe.wait_ge(self.hi_done.sem, self.hi_done.at(turn, s + 1))
            pe.wait_ge(self.lo_done.sem, self.lo_done.at(turn, s + 1))
        pe.wait_ge(self.free.sem, self.free.at(turn, 3 * s + j - 5))
        product(pe, self.ps[:, 3 * s + j, 0:TH], self.hi[s], self.lo[s], xhi, xlo, self.n_k, cols(j))\
            .then_inc(self.done.sem, 1)

    def wait_piece(self, eng, turn, s, j):
        eng.wait_ge(self.done.sem, self.done.at(turn, 3 * s + j + 1))

    def out(self, s, j):
        return self.ps[:, 3 * s + j, 0:TH]

    def take_over(self, sp, act, pool):
        for eng, sigs in ((sp, self.loaded), (act, [self.hi_done]), (pool, [self.lo_done])):
            for sig in sigs if eng is not None else ():
                eng.sem_inc(sig.sem, sig.step)

    def head_start(self, pe=None, act=None, pool=None, reader=None):
        for eng, sig in ((pe, self.done), (act, self.hi_done), (pool, self.lo_done), (reader, self.free)):
            if eng is not None:
                sig.start(eng)


def turns(eng, n, body):
    with eng.Fori(0, n - 1) as i:
        body(i, False)
    body(n - 1, True)


def copy(dve, out, src):
    return dve.tensor_scalar(out, src, 1.0, None, ALU.mult)


def flat(ap):
    return ap.rearrange("o p n -> p (o n)")


def norm_stage(nc, a, c, x, hi, lo, mem, early):
    name = "norm"
    shift, scale, gain = 0, KT, VEC["mix_g"][0]
    n_ada = 2 * KT
    RING = 4
    with Stage(c) as ctx:
        sq = [mem(f"sq{i}", [P, NT]) for i in range(2)]
        rs = mem("rs", [P, NT])
        y = [mem(f"y{i}", [P, NT]) for i in range(2)]
        ps = ctx.enter_context(nc.psum_tensor(f"{name}_ms", [P, NP, 512], F32))
        S = lambda n, **k: Sig(ctx, nc, f"{name}_{n}", **k)
        x_in = [S(f"x_in{k}", step=16) for k in range(KT)]
        squared, used, summed, lnd, rstd = S("squared"), S("sq_used"), S("ms_summed"), S("ln"), S("rstd")
        normed, high, low = S("normed"), S("hi_done"), S("lo_done")
        aw = [mem(f"ada_w{i}", [P, KT * P]) for i in range(RING)]
        cx = mem("cx", [P, KT, CS])
        tmp = mem("tmp", [P, 2, DH])
        lw = mem("lw", [P, 6, H])
        pa = ctx.enter_context(nc.psum_tensor(f"{name}_ada", [P, RING, 512], F32))
        kept, cond, ada_in = S("kept_in", step=16), S("c_in", step=16), [S(f"ada_in{i}", step=16) for i in range(RING)]
        ada_done, ada_read, silu_e, csil = S("ada_done"), S("ada_read"), S("silu_e"), S("csil")
        lam_s, lam_e, lb_s, lb_e = S("lam_s"), S("lam_e"), S("lb_s"), S("lb_e")
        vec_in = S("vec_in", step=16)
        w_in, w_hi, w_lo = [S(f"w_in{n}", step=16) for n in range(2)], S("w_hi"), S("w_lo")
        mods, mean_in, mean = S("mods_ready"), S("mean_in", step=16), mem("mean", [P, P])
        block = ctx.enter_context(nc.Block())

        def ada_tile(t):
            return t // 2 + (shift, scale)[t % 2]

        @block.sync
        def _(sp):
            sp.dma_start(mean[:, :], a["ones1024"]).then_inc(mean_in.sem, 16)
            sp.dma_start(cx[:, :, :], a["cT"]).then_inc(cond.sem, 16)
            sp.dma_start(c["vec"][:, :], a["vec"]).then_inc(vec_in.sem, 16)
            for t in range(n_ada):
                if t < KT:
                    sp.dma_start(x[:, t, :], a["xT"][:, t, :]).then_inc(x_in[t].sem, 16)
                if t >= RING:
                    sp.wait_ge(ada_done.sem, ada_done.before(t - RING + 1))
                n = ada_tile(t)
                sp.dma_start(aw[t % RING][:, :], flat(a["w_ada"][n:n + 1])).then_inc(ada_in[t % RING].sem, 16)
                if t == KT + 1:
                    for n in range(2):
                        sp.dma_start(early["raw"][n][:, :], flat(a["w_in"][n:n + 1])).then_inc(w_in[n].sem, 16)
            for n in ("ident", "ones128", "ones"):
                sp.dma_start(c[n][:, :], a[n]).then_inc(kept.sem, 16)
            for n in ("cos", "sin", "rot", "blk", "causal", "lmask"):
                sp.dma_start(early[n][:, :], a[n]).then_inc(kept.sem, 16)
            sp.wait_ge(w_hi.sem, 1)
            sp.wait_ge(w_lo.sem, 1)
            sp.dma_start(early["raw"][0][:, :], flat(a["w_in"][2:3])).then_inc(kept.sem, 16)
            sp.wait_ge(kept.sem, kept.before(3 + 6 + 1))

        @block.scalar
        def _(act):
            act.preload_act_table_set(TABLES)
            act.wait_ge(cond.sem, cond.before(1))
            act.activation(c["csil"][:, :, :], cx[:, :, :], ACT.Exp, scale=-1.0).then_inc(silu_e.sem, 1)
            act.wait_ge(lam_s.sem, 1)
            act.activation(c["lam"][:, 0:2], c["lam"][:, 4:6], ACT.Exp).then_inc(lam_e.sem, 1)
            act.wait_ge(lb_s.sem, 1)
            act.activation(lw[:, 3:5, :], lw[:, 1:3, :], ACT.Exp).then_inc(lb_e.sem, 1)
            for k in range(KT):
                act.wait_ge(x_in[k].sem, x_in[k].before(1))
                if k >= 2:
                    act.wait_ge(used.sem, used.before(k - 1))
                act.activation(sq[k % 2][:, :], x[:, k, :], ACT.Square).then_inc(squared.sem, 1)
            act.wait_ge(summed.sem, 1)
            act.wait_ge(mods.sem, 1)
            for j in range(NP):
                act.activation(rs[:, cols(j)], ps[:, j, 0:TH], ACT.Ln, bias=c["eps"][:, 0:1]).then_inc(lnd.sem, 1)
            act.wait_ge(lnd.sem, NP)
            act.activation(rs[:, :], rs[:, :], ACT.Exp, scale=-0.5).then_inc(rstd.sem, 1)
            for n in range(2):
                act.wait_ge(w_in[n].sem, 16)
                act.activation(early["hi"][n][:, :], early["raw"][n][:, :], ACT.Copy).then_inc(w_hi.sem, 1)
            for k in range(KT):
                act.wait_ge(normed.sem, k + 1)
                act.activation(hi[:, k, :], y[k % 2][:, :], ACT.Copy).then_inc(high.sem, 1)

        @block.tensor
        def _(pe):
            pe.wait_ge(mean_in.sem, 16)
            pe.wait_ge(csil.sem, 1)
            for t in range(n_ada):
                k = t
                if k < KT:
                    pe.wait_ge(squared.sem, k + 1)
                    for j in range(NP):
                        ins = pe.matmul(ps[:, j, 0:TH], mean[:, :], sq[k % 2][:, cols(j)], start=(k == 0), stop=(k == KT - 1))
                    ins.then_inc(used.sem if k < KT - 1 else summed.sem, 1)
                pe.wait_ge(ada_in[t % RING].sem, ada_in[t % RING].before(t // RING + 1))
                if t >= RING:
                    pe.wait_ge(ada_read.sem, t - RING + 1)
                for k in range(KT):
                    ins = pe.matmul(pa[:, t % RING, 0:CS], aw[t % RING][:, k * P:(k + 1) * P], c["csil"][:, k, :],
                                    start=(k == 0), stop=(k == KT - 1))
                ins.then_inc(ada_done.sem, 1)

        @block.gpsimd
        def _(pool):
            ctx.clear_last(pool)
            for n in range(2):
                pool.wait_ge(w_hi.sem, n + 1)
                pool.wait_ge(w_in[n].sem, 16)
                pool.tensor_tensor(early["lo"][n][:, :], early["raw"][n][:, :], early["hi"][n][:, :].bitcast(F32), ALU.subtract)\
                    .then_inc(w_lo.sem, 1)
            for k in range(KT):
                pool.wait_ge(normed.sem, k + 1)
                pool.wait_ge(high.sem, k + 1)
                pool.tensor_tensor(lo[:, k, :], y[k % 2][:, :], hi[:, k, :].bitcast(F32), ALU.subtract).then_inc(low.sem, 1)

        @block.vector
        def _(dve):
            ch = Chain(ctx, nc, dve, f"{name}_dve_chain")
            mod, vec = c["mod"], c["vec"]
            ch(dve.memset(c["eps"][:, :], EPS))
            dve.wait_ge(silu_e.sem, 1)
            cs = c["csil"][:, :, :]
            ch(dve.tensor_scalar(cs, cs, 1.0, None, ALU.add))
            ch.sync()
            ch(dve.reciprocal(cs, cs))
            ch.sync()
            dve.tensor_tensor(cs, cs, cx[:, :, :], ALU.mult).then_inc(csil.sem, 1)
            dve.wait_ge(vec_in.sem, 16)
            lv = vec[:, VEC["lam"][0]:VEC["lam"][0] + 4 * DH].rearrange("p (c s n) -> p c s n", c=2, s=2)
            ch(dve.tensor_tensor(tmp[:, :, :], lv[:, :, 0, :], lv[:, :, 1, :], ALU.mult))
            ch.sync()
            dve.tensor_reduce(c["lam"][:, 4:6], tmp[:, :, :], AX.X, ALU.add).then_inc(lam_s.sem, 1)
            lb0 = VEC["lb"][0]
            l0, l1 = vec[:, lb0:lb0 + H], vec[:, lb0 + H:lb0 + 2 * H]
            ch(dve.tensor_tensor(lw[:, 0, :], l0, l1, ALU.max))
            ch.sync()
            ch(dve.tensor_tensor(lw[:, 1, :], l0, lw[:, 0, :], ALU.subtract))
            dve.tensor_tensor(lw[:, 2, :], l1, lw[:, 0, :], ALU.subtract).then_inc(lb_s.sem, 1)
            dve.wait_ge(lam_e.sem, 1)
            ch(dve.tensor_tensor(c["lam"][:, 2:3], c["lam"][:, 0:1], c["lam"][:, 1:2], ALU.subtract))
            ch.sync()
            ch(dve.tensor_scalar(c["lam"][:, 2:3], c["lam"][:, 2:3], LAM_INIT, None, ALU.add))
            ch.sync()
            ch(dve.tensor_scalar(c["lam"][:, 3:4], c["lam"][:, 2:3], -1.0, None, ALU.mult))
            dve.wait_ge(lb_e.sem, 1)
            ch(dve.tensor_tensor(lw[:, 5, :], lw[:, 3, :], lw[:, 4, :], ALU.add))
            ch.sync()
            ch(dve.reciprocal(lw[:, 5, :], lw[:, 5, :]))
            ch.sync()
            ch(dve.tensor_tensor(c["lb"][:, 0, :], lw[:, 3, :], lw[:, 5, :], ALU.mult))
            ch.sync()
            ch(dve.tensor_scalar(c["lb"][:, 1, :], c["lb"][:, 0, :], -1.0, 1.0, ALU.mult, ALU.add))
            ch.sync()
            dve.sem_inc(mods.sem, 1)

            def whole_scale(k):
                m = mod[:, scale + k, :]
                ch(dve.tensor_scalar(m, m, 1.0, vec[:, gain + k:gain + k + 1], ALU.add, ALU.mult))

            def add_bias(t):
                n = ada_tile(t)
                dve.wait_ge(ada_done.sem, t + 1)
                dve.tensor_scalar(mod[:, n, :], pa[:, t % RING, 0:CS], vec[:, n:n + 1], None, ALU.add).then_inc(ada_read.sem, 1)

            for t in range(KT):
                add_bias(t)
            dve.wait_ge(rstd.sem, 1)
            for k in range(KT):
                for t in (2 * k, 2 * k + 1):
                    if t >= KT:
                        add_bias(t)
                dve.wait_ge(ada_read.sem, 2 * k + 2)
                whole_scale(k)
                if k >= 2:
                    dve.wait_ge(high.sem, k - 1)
                    dve.wait_ge(low.sem, k - 1)
                yk = y[k % 2]
                ch(dve.tensor_tensor(yk[:, :], x[:, k, :], rs[:, :], ALU.mult))
                ch.sync()
                ch(dve.tensor_tensor(yk[:, T:NT], yk[:, T:NT], mod[:, scale + k, 1:CS], ALU.mult))
                ch(dve.tensor_scalar(yk[:, 0:T], yk[:, 0:T], mod[:, scale + k, 0:1], mod[:, shift + k, 0:1], ALU.mult, ALU.add))
                ch.sync()
                dve.tensor_tensor(yk[:, T:NT], yk[:, T:NT], mod[:, shift + k, 1:CS], ALU.add).then_inc(normed.sem, 1)


TILES = ("f", "qh", "ib", "og", "q", "k", "v")
NTL = len(TILES)
ADA_COL = 384
SLOT = (0, 1, 0, 1, 0, 1, 2)
BACK = (3, 3, 2, 2, 2, 2, 7)
PIECES = [(t, j) for t in range(NTL) for j in range(NP)]
ATT_PIECES = ([0], [1], [2], [3], [4, 5], [6, 7], [8, 9], [10, 11])
REC_PIECES = ([12], [13], [14], [15], [16], [17], [18], [19, 20])
SIGMOID = [n for n, (t, j) in enumerate(PIECES) if TILES[t] in ("f", "qh", "og")]
ADA_AT = {12: 0, 14: 1, 16: 2, 18: 3}
SPLIT_AT = {1: 1, 4: 2, 7: 3, 10: 4, 13: 5, 16: 6, 19: 7}


def level_view(ap, lv):
    return ap.rearrange("p (n two b) -> p n two b", two=2, b=1 << lv)


def early_tensors(nc):
    mem = Memory(nc, "h", R2)
    t = {"mem": mem, "raw": [mem(f"w_raw{s}", [P, KT * P]) for s in range(2)],
         "hi": [mem(f"w_hi{s}", [P, KT * P], F32R) for s in range(2)],
         "lo": [mem(f"w_lo{s}", [P, KT * P], F32R) for s in range(2)]}
    for n in ("hi", "lo"):
        t[n].append(mem(f"w_{n}2", [P, KT * P], F32R))
    t.update({n: mem(n, [P, NT]) for n in ("cos", "sin")})
    t.update({n: mem(n, [P, P]) for n in ("rot", "blk", "causal")})
    t["lmask"] = mem("lmask", [P, LEVELS * HALF], U32)
    return t


def heads_stage(nc, a, o, c, d, xh, xl, early):
    with Stage(c) as ctx:
        mem, raw, whi, wlo = early["mem"], early["raw"], early["hi"], early["lo"]
        cos, sin, rot, blk, causal, lmask = (early[n] for n in ("cos", "sin", "rot", "blk", "causal", "lmask"))
        qT, kT, vT = (mem(n, [P, NT]) for n in ("qT", "kT", "vT"))
        vtok = mem("vtok", [P, T])
        kk, fc, qh, ib, og = (mem(n, [P, NT]) for n in ("kk", "fc", "qh", "ib", "og"))
        ibtok = mem("ibtok", [P, T])
        E = mem("E", [P, 2, T])
        PT = mem("PT", [P, T])
        LV = [mem(f"LV{i}", [P, LEVELS + 2, P]) for i in range(2)]
        QL = [mem(f"QL{i}", [P, LEVELS * HALF + P]) for i in range(2)]
        AT = mem("AT", [P, P])
        kht = mem("kht", [P, P])
        St = mem("St", [P, P])
        oraw, braw = mem("oraw", [P, T]), mem("braw", [P, T])
        ex = [mem(f"ex{i}", [P, TH]) for i in range(2)]
        sq = [mem(f"sq{i}", [P, TH]) for i in range(2)]
        rg = [mem(f"rg{i}", [P, TH]) for i in range(2)]
        rb, rr = mem("rb", [P, TH]), mem("rr", [P, TH])
        aw, av = [mem(f"ada_w{i}", [P, KT * P]) for i in range(2)], [mem(f"ada{i}", [P, CS]) for i in range(2)]
        sm = mem("sm", [P, 16])
        dec = mem("dec", [P, NB])
        subg = mem("subg", [P, 1])
        G = ctx.enter_context(nc.psum_tensor("h_G", [P, 2, 512], F32))
        SP_ = ctx.enter_context(nc.psum_tensor("h_S", [P, 4, 512], F32))
        X = ctx.enter_context(nc.psum_tensor("h_X", [P, 2, 512], F32))
        dest = {"f": fc, "qh": qh, "ib": ib, "og": og, "v": vT, "q": qT, "k": kT}
        Xf = X[:, :, :].rearrange("p a b -> p (a b)")

        def S(n, per, **k):
            return Sig(ctx, nc, f"h_{n}", per=per, **k)

        loaded = [S("w_loaded0", 4, pre=3, step=16), S("w_loaded1", 3, pre=1, step=16)]
        hi_done, lo_done = S("w_hi_done", 7, pre=4), S("w_lo_done", 7, pre=4)
        piece_done = S("piece_done", 21, pre=9)
        piece_read = S("piece_read", 21, pre=9)
        ex_ready, ex_cut, sig_ready = (S(n, 9) for n in ("ex_ready", "ex_cut", "sig_ready"))
        sig_used = S("sig_used", 9, init=2)
        qk_squared = S("qk_squared", 6, pre=6)
        qk_summed = S("qk_summed", 6, pre=6)
        qk_rstd = S("qk_rstd", 6, pre=6)
        qk_ready = S("qk_ready", 6, pre=6)
        kv_stored = S("kv_stored", 2, step=16)
        sample_qkv, sample_rec = S("sample_qkv_kept", 1), S("sample_rec_kept", 1, init=1)
        scores, row_max, exped, weighed = S("scores", 8), S("row_max", 8), S("exped", 8), S("weighed", 8)
        turned, pt_ready, pv_done, pv_read = S("turned", 8), S("pt_ready", 8), S("pv_done", 8), S("pv_read", 8)
        v_turned, v_tok = S("v_turned", 1), S("v_tok", 1)
        ib_turned, ib_tok = S("ib_turned", 1, init=1), S("ib_tok", 1)
        log_f, cum_ready, dec_ready = S("log_f", 1), S("cum_ready", 1), S("chunk_decay", 1)
        lv_diff, lv_exp, lv_k = S("lv_diff", 8), S("lv_exp", 8), S("lv_ready", 8, init=2)
        rec_done, at_ready, kht_ready = S("rec_products", 8, init=1), S("at_ready", 8), S("kht_ready", 8)
        os_done, o_read, st_ready = S("rec_out_done", 8, init=1), S("rec_out_read", 8, init=1), S("state_ready", 8, init=1)
        st_stored = S("state_stored", 1, step=16, init=1)
        o_squared, o_summed, o_rstd, o_normed = S("o_squared", 4), S("o_summed", 4), S("o_rstd", 4, init=1), S("o_normed", 4, init=1)
        o_stored = S("o_stored", 4, step=16, init=1)
        ada_in = [S(f"ada_in{i}", 2, step=16) for i in range(2)]
        ada_read, ada_added = S("ada_read", 4), S("ada_added", 4, init=2)
        block = ctx.enter_context(nc.Block())
        wt = a["w_in"]

        def score_bank(i, m):
            return 2 * (i % 2) + m if i < NB // 2 else 2 * m

        def slot(t):
            return SLOT[t] if t >= 0 else (0, 1, 2)[t + 3]

        @block.sync
        def _(sp):
            sp.sem_inc(loaded[0].sem, 32)
            sp.sem_inc(loaded[1].sem, 16)
            sp.dma_start(raw[1][:, :], flat(wt[4:5])).then_inc(loaded[1].sem, 16)
            sp.wait_ge(hi_done.sem, hi_done.before(3))
            sp.wait_ge(lo_done.sem, lo_done.before(3))
            sp.dma_start(raw[0][:, :], flat(wt[3:4])).then_inc(loaded[0].sem, 16)
            o_stored.start(sp)
            st_stored.start(sp)

            def store_branch(h, u):
                branch, s = "oa" if u < 2 else "ob", slice((u % 2) * 512, (u % 2) * 512 + 512)
                sp.wait_ge(o_normed.sem, o_normed.at(h, u + 1))
                sp.dma_start(flat(d[branch][bass.ds(h, 1), :, s]), E[:, 1, s]).then_inc(o_stored.sem, 16)

            def load_ada(h, q, pieces):
                sp.wait_ge(piece_done.sem, piece_done.at(h, pieces))
                sp.dma_start(aw[q % 2][:, :], flat(a["w_ada"][bass.ds(h * 4 + (2 * KT + q), 1)])).then_inc(ada_in[q % 2].sem, 16)

            with sp.Fori(0, H) as h:
                sp.wait_ge(qk_ready.sem, qk_ready.at(h, 0))
                sp.dma_start(flat(o["k"][bass.ds(h, 1)]), kT[:, :]).then_inc(kv_stored.sem, 16)
                sp.wait_ge(piece_read.sem, piece_read.at(h, 0))
                sp.dma_start(flat(o["v"][bass.ds(h, 1)]), vT[:, :]).then_inc(kv_stored.sem, 16)
                for t in range(2, NTL + 2):
                    behind, r = {NTL: (1, 0), NTL + 1: (3, 1)}.get(t, (2, t % 2))
                    if t == 3:
                        load_ada(h, 0, 0)
                        load_ada(h, 1, 0)
                    if t == NTL:
                        store_branch(h, 0)
                        store_branch(h, 1)
                        load_ada(h, 2, 13)
                        load_ada(h, 3, 15)
                    sp.wait_ge(hi_done.sem, hi_done.at(h, t - behind))
                    sp.wait_ge(lo_done.sem, lo_done.at(h, t - behind))
                    sp.dma_start(raw[r][:, :], flat(wt[bass.ds(h * NTL + (3 + t), 1)])).then_inc(loaded[r].sem, 16)
                sp.wait_ge(st_ready.sem, st_ready.at(h, NB))
                sp.dma_start(flat(o["state"][bass.ds(h, 1)]), St[:, :]).then_inc(st_stored.sem, 16)
                store_branch(h, 2)
                store_branch(h, 3)
            sp.wait_ge(kv_stored.sem, kv_stored.at(H, 0))
            sp.wait_ge(o_stored.sem, o_stored.at(H, 0))
            sp.wait_ge(st_stored.sem, st_stored.at(H, 0))
            for s in range(2):
                sp.wait_ge(loaded[s].sem, loaded[s].at(H, 1 if s else 0))

        def raw_loaded(eng, h, t):
            if t == NTL:
                eng.wait_ge(loaded[0].sem, loaded[0].at(h, 4))
            elif t % 2 == 0:
                eng.wait_ge(loaded[0].sem, loaded[0].at(h, t // 2))
            else:
                eng.wait_ge(loaded[1].sem, loaded[1].at(h, t // 2 + 1))

        def used_wait(eng, h, t):
            tile = t if t < NTL else 0
            back = BACK[tile]
            eng.wait_ge(piece_done.sem, piece_done.at(h, NP * (t - back + 1)))

        @block.scalar
        def _(act):
            act.preload_act_table_set(TABLES)
            ch = Chain(ctx, nc, act, "h_act_chain")
            act.sem_inc(hi_done.sem, 2)
            vec = c["vec"]
            gq, gk = (vec[:, VEC[n][0]:VEC[n][0] + 1] for n in ("q_g", "k_g"))

            def split(w, r):
                act.activation(whi[w][:, :], raw[r][:, :], ACT.Copy).then_inc(hi_done.sem, 1)

            def qk_piece(g, bank, u):
                act.activation(sq[u][:, :], G[:, bank, 0:TH], ACT.Square).then_inc(qk_squared.sem, 1)
                act.activation(rg[u][:, :], G[:, bank, 0:TH], ACT.Copy, scale=g).then_inc(piece_read.sem, 1)

            def qk_norm(value):
                act.wait_ge(qk_summed.sem, value)
                ch(act.activation(rr[:, :], X[:, 1, 0:TH], ACT.Ln, bias=c["eps"][:, 0:1]))
                ch.sync()
                act.activation(rr[:, :], rr[:, :], ACT.Exp, scale=-0.5).then_inc(qk_rstd.sem, 1)

            for n in range(9):
                if n == 0:
                    act.wait_ge(loaded[0].sem, 32)
                    split(2, 0)
                if n == 6:
                    act.wait_ge(loaded[0].sem, 16 * 3)
                    act.wait_ge(piece_done.sem, 3)
                    split(0, 0)
                act.wait_ge(piece_done.sem, n + 1)
                if n < 6:
                    if n >= 2:
                        act.wait_ge(qk_ready.sem, n - 1)
                    qk_piece(gq if n < 3 else gk, n % 2, n % 2)
                    if n >= 1:
                        qk_norm(n)
                else:
                    if n == 6:
                        qk_norm(6)
                    act.activation(vT[:, cols(n - 6)], G[:, n % 2, 0:TH], ACT.Copy).then_inc(piece_read.sem, 1)
            o_read.start(act)
            o_rstd.start(act)
            ch.reset()

            def piece(h, n):
                t, j = PIECES[n]
                kind = TILES[t]
                bank = G[:, n % 2, 0:TH]
                act.wait_ge(piece_done.sem, piece_done.at(h, n + 1))
                if n in ADA_AT:
                    q = ADA_AT[n]
                    act.wait_ge(ada_added.sem, ada_added.at(h, q - 1))
                    act.activation(av[q % 2][:, :], G[:, n % 2, ADA_COL:ADA_COL + CS], ACT.Copy).then_inc(ada_read.sem, 1)
                if kind in ("f", "qh", "og"):
                    s = SIGMOID.index(n)
                    if s >= 1:
                        sigmoid(h, s - 1)
                    act.wait_ge(sig_used.sem, sig_used.at(h, s - 1))
                    if j == 0 and kind != "f":
                        last = rec_done if kind == "qh" else o_normed
                        act.wait_ge(last.sem, last.at(h, 0))
                        act.wait_ge(sample_rec.sem, sample_rec.at(h, 0))
                    ins = act.activation(ex[s % 2][:, :], bank, ACT.Exp, scale=-1.0)
                    ins.then_inc(ex_ready.sem, 1)
                    if kind == "f":
                        act.wait_ge(ex_ready.sem, ex_ready.at(h, s + 1))
                        act.sem_inc(piece_read.sem, 1)
                    else:
                        act.activation(dest[kind][:, cols(j)], bank, ACT.Copy).then_inc(piece_read.sem, 1)
                elif kind in ("ib", "v"):
                    if kind == "v" and j == 0:
                        act.wait_ge(kv_stored.sem, kv_stored.at(h, 2))
                        act.wait_ge(sample_qkv.sem, sample_qkv.at(h, 1))
                    if kind == "ib" and j == 0:
                        act.wait_ge(ib_turned.sem, ib_turned.at(h, 0))
                        act.wait_ge(sample_rec.sem, sample_rec.at(h, 0))
                    act.activation(dest[kind][:, cols(j)], bank, ACT.Copy).then_inc(piece_read.sem, 1)
                else:
                    u = n - 12
                    act.wait_ge(qk_ready.sem, qk_ready.at(h, u - 1))
                    qk_piece(gq if kind == "q" else gk, n % 2, u % 2)

            def sigmoid(h, s):
                act.wait_ge(ex_cut.sem, ex_cut.at(h, s + 1))
                ch(act.activation(ex[s % 2][:, :], ex[s % 2][:, :], ACT.Ln))
                ch.sync()
                act.activation(ex[s % 2][:, :], ex[s % 2][:, :], ACT.Exp, scale=-1.0).then_inc(sig_ready.sem, 1)

            def split_next(h, n):
                if n in SPLIT_AT:
                    t = SPLIT_AT[n]
                    raw_loaded(act, h, t)
                    used_wait(act, h, t)
                    split(slot(t % NTL), 0 if t == NTL else t % 2)

            def levels(h, k):
                act.wait_ge(lv_diff.sem, lv_diff.at(h, k + 1))
                act.activation(LV[k % 2][:, :, :], LV[k % 2][:, :, :], ACT.Exp, scale=-1.0).then_inc(lv_exp.sem, 1)

            def o_norm(h, u):
                act.wait_ge(o_summed.sem, o_summed.at(h, u + 1))
                r = E[:, 0, (u % 2) * 512:(u % 2) * 512 + 512]
                if u >= 2:
                    act.wait_ge(o_stored.sem, o_stored.at(h, 2))
                ch(act.activation(r, X[:, u % 2, :], ACT.Ln, bias=c["eps"][:, 0:1]))
                ch.sync()
                act.activation(r, r, ACT.Exp, scale=-0.5).then_inc(o_rstd.sem, 1)

            with act.Fori(0, H) as h:
                def read_values(i):
                    act.wait_ge(pv_done.sem, pv_done.at(h, i + 1))
                    act.activation(oraw[:, i * P:(i + 1) * P], X[:, 0, 0:P], ACT.Copy).then_inc(pv_read.sem, 1)

                for i in range(NB):
                    nk = (i + 1) * P
                    act.wait_ge(row_max.sem, row_max.at(h, i + 1))
                    if i == 0:
                        act.wait_ge(o_stored.sem, o_stored.at(h, 0))
                    for m in range(2):
                        ins = act.activation(E[:, m, 0:nk],
                                             SP_[:, :, :].rearrange("p a b -> p (a b)")[:, 512 * score_bank(i, m):512 * score_bank(i, m) + nk],
                                             ACT.Exp, bias=sm[:, 2 + m:3 + m], scale=SCALE, accum_out=sm[:, 4 + m:5 + m])
                        if m == 0:
                            ch(ins)
                    ins.then_inc(exped.sem, 1)
                    if i == 0:
                        act.wait_ge(v_turned.sem, v_turned.at(h, 1))
                        act.activation(vtok[:, :], Xf, ACT.Copy).then_inc(v_tok.sem, 1)
                    if 0 < i:
                        read_values(i - 1)
                    for n in ATT_PIECES[i]:
                        split_next(h, n)
                        piece(h, n)
                    if i == 4:
                        act.wait_ge(sig_used.sem, sig_used.at(h, 3))
                        act.activation(fc[:, 0:T], fc[:, 0:T], ACT.Ln).then_inc(log_f.sem, 1)
                    act.wait_ge(turned.sem, turned.at(h, i + 1))
                    act.activation(PT[:, 0:nk], Xf[:, 0:nk], ACT.Copy).then_inc(pt_ready.sem, 1)
                    if i == 6:
                        act.wait_ge(cum_ready.sem, cum_ready.at(h, 1))
                        act.activation(dec[:, :], fc[:, P - 1:T:P], ACT.Exp).then_inc(dec_ready.sem, 1)
                        levels(h, 0)
                read_values(NB - 1)
                act.wait_ge(ib_turned.sem, ib_turned.at(h, 1))
                act.activation(ibtok[:, :], Xf, ACT.Copy).then_inc(ib_tok.sem, 1)
                sigmoid(h, len(SIGMOID) - 1)
                for k in range(NB):
                    act.wait_ge(rec_done.sem, rec_done.at(h, k + 1))
                    act.activation(kht[:, :], SP_[:, 2, 0:P], ACT.Copy).then_inc(kht_ready.sem, 1)
                    if k + 1 < NB:
                        levels(h, k + 1)
                    if k == 0:
                        o_norm(h, 0)
                        o_norm(h, 1)
                    for n in REC_PIECES[k]:
                        split_next(h, n)
                        piece(h, n)
                    if 1 <= k <= 6:
                        qk_norm(qk_summed.at(h, k))
                    act.wait_ge(os_done.sem, os_done.at(h, k + 1))
                    act.activation(braw[:, k * P:(k + 1) * P], SP_[:, 3, 0:P], ACT.Copy).then_inc(o_read.sem, 1)
                o_norm(h, 2)
                o_norm(h, 3)
                ch.reset()

        @block.tensor
        def _(pe):
            ident, ones = c["ident"], c["ones128"]
            for sig in (rec_done, os_done, ib_turned):
                sig.start(pe)

            def qk_sums(u):
                pe.matmul(X[:, 1, 0:TH], blk[:, :], sq[u][:, :], start=True, stop=True)
                pe.matmul(X[:, 0, 0:TH], rot[:, :], rg[u][:, :], start=True, stop=True).then_inc(qk_summed.sem, 1)

            for n in range(9):
                t = n // NP
                if n % NP == 0:
                    pe.wait_ge(hi_done.sem, t + 1)
                    pe.wait_ge(lo_done.sem, t + 1)
                if n >= 2:
                    pe.wait_ge(piece_read.sem, n - 1)
                product(pe, G[:, n % 2, 0:TH], whi[t], wlo[t], xh, xl, KT, cols(n % NP)).then_inc(piece_done.sem, 1)
                if 1 <= n <= 6:
                    pe.wait_ge(qk_squared.sem, n)
                    pe.wait_ge(piece_read.sem, n)
                    if n >= 2:
                        pe.wait_ge(qk_ready.sem, n - 1)
                    qk_sums((n - 1) % 2)

            def piece(h, n):
                t, j = PIECES[n]
                if j == 0:
                    pe.wait_ge(hi_done.sem, hi_done.at(h, t))
                    pe.wait_ge(lo_done.sem, lo_done.at(h, t))
                pe.wait_ge(piece_read.sem, piece_read.at(h, n - 1 if n else 0))
                w = SLOT[t]
                ins = product(pe, G[:, n % 2, 0:TH], whi[w], wlo[w], xh, xl, KT, cols(j))
                if n in ADA_AT:
                    q = ADA_AT[n]
                    pe.wait_ge(ada_in[q % 2].sem, ada_in[q % 2].at(h, q // 2 + 1))
                    for k in range(KT):
                        ins = pe.matmul(G[:, n % 2, ADA_COL:ADA_COL + CS], aw[q % 2][:, k * P:(k + 1) * P], c["csil"][:, k, :],
                                        start=(k == 0), stop=(k == KT - 1))
                ins.then_inc(piece_done.sem, 1)

            def scores_of(h, i):
                nk = (i + 1) * P
                for m in range(2):
                    rows = slice(DH * m, DH * (m + 1))
                    for b in range(0, nk, 512):
                        w = min(512, nk - b)
                        ins = pe.matmul(SP_[:, score_bank(i, m) + b // 512, 0:w], qT[rows, i * P:(i + 1) * P], kT[rows, b:b + w],
                                        start=True, stop=True)
                ins.then_inc(scores.sem, 1)

            def turn8(src):
                for b in range(NB):
                    ins = pe.transpose(Xf[:, b * P:(b + 1) * P], src[:, b * P:(b + 1) * P], ident[:, :])
                return ins

            def o_sum(h, u):
                pe.wait_ge(o_squared.sem, o_squared.at(h, u + 1))
                pe.matmul(X[:, u % 2, :], ones[:, :], PT[:, (u % 2) * 512:(u % 2) * 512 + 512],
                          start=True, stop=True).then_inc(o_summed.sem, 1)

            with pe.Fori(0, H) as h:
                pe.wait_ge(qk_ready.sem, qk_ready.at(h, 0))
                pe.wait_ge(o_read.sem, o_read.at(h, 0))
                pe.wait_ge(st_ready.sem, st_ready.at(h, 0))
                scores_of(h, 0)
                pe.wait_ge(piece_read.sem, piece_read.at(h, 0))
                pe.wait_ge(o_rstd.sem, o_rstd.at(h, 0))
                turn8(vT).then_inc(v_turned.sem, 1)
                def values(i):
                    pe.wait_ge(pt_ready.sem, pt_ready.at(h, i + 1))
                    for b in range(i + 1):
                        ins = pe.matmul(X[:, 0, 0:P], vtok[:, b * P:(b + 1) * P], PT[:, b * P:(b + 1) * P],
                                        start=(b == 0), stop=(b == i))
                    ins.then_inc(pv_done.sem, 1)

                for i in range(NB):
                    if i + 1 < NB // 2:
                        scores_of(h, i + 1)
                    if 0 < i:
                        values(i - 1)
                    for n in ATT_PIECES[i]:
                        piece(h, n)
                    pe.wait_ge(weighed.sem, weighed.at(h, i + 1))
                    if i == 0:
                        pe.wait_ge(v_tok.sem, v_tok.at(h, 1))
                    else:
                        pe.wait_ge(pv_read.sem, pv_read.at(h, i))
                    for b in range(i + 1):
                        ins = pe.transpose(Xf[:, b * P:(b + 1) * P], E[:, 0, b * P:(b + 1) * P], ident[:, :])
                    ins.then_inc(turned.sem, 1)
                    if NB // 2 <= i + 1 < NB:
                        scores_of(h, i + 1)
                values(NB - 1)
                pe.wait_ge(piece_read.sem, piece_read.at(h, 9))
                pe.wait_ge(pv_read.sem, pv_read.at(h, NB))
                turn8(ib).then_inc(ib_turned.sem, 1)
                for k in range(NB):
                    ck = slice(k * P, (k + 1) * P)
                    pe.wait_ge(lv_k.sem, lv_k.at(h, k + 1))
                    if k:
                        pe.wait_ge(at_ready.sem, at_ready.at(h, k))
                        pe.wait_ge(kht_ready.sem, kht_ready.at(h, k))
                    pe.matmul(SP_[:, 0, 0:P], kk[:, ck], qh[:, ck], start=True, stop=True)
                    for lv in range(LEVELS):
                        pe.matmul(SP_[:, 1, lv * HALF:(lv + 1) * HALF], LV[k % 2][:, lv, :],
                                  QL[k % 2][:, lv * HALF:(lv + 1) * HALF], start=True, stop=True)
                    pe.transpose(SP_[:, 2, 0:P], LV[k % 2][:, LEVELS, :], ident[:, :]).then_inc(rec_done.sem, 1)
                    for n in REC_PIECES[k]:
                        piece(h, n)
                    if k == 0:
                        pe.wait_ge(ib_tok.sem, ib_tok.at(h, 1))
                        o_sum(h, 0)
                        o_sum(h, 1)
                    if k == NB - 1:
                        pe.wait_ge(qk_ready.sem, qk_ready.at(h, 6))
                        o_sum(h, 2)
                    if 1 <= k <= 6:
                        u = k - 1
                        pe.wait_ge(qk_squared.sem, qk_squared.at(h, u + 1))
                        pe.wait_ge(piece_read.sem, piece_read.at(h, 12 + u + 1))
                        if u:
                            pe.wait_ge(qk_ready.sem, qk_ready.at(h, u))
                        else:
                            pe.wait_ge(o_rstd.sem, o_rstd.at(h, 2))
                        qk_sums(u % 2)
                    pe.wait_ge(at_ready.sem, at_ready.at(h, k + 1))
                    if k:
                        pe.wait_ge(o_read.sem, o_read.at(h, k))
                        pe.wait_ge(st_ready.sem, st_ready.at(h, k))
                    pe.matmul(SP_[:, 3, 0:P], ibtok[:, ck], AT[:, :], start=True, stop=(k == 0))
                    if k:
                        pe.matmul(SP_[:, 3, 0:P], St[:, :], QL[k % 2][:, LEVELS * HALF:], start=False, stop=True)
                    pe.wait_ge(kht_ready.sem, kht_ready.at(h, k + 1))
                    pe.matmul(SP_[:, 3, P:2 * P], kht[:, :], ibtok[:, ck], start=True, stop=True).then_inc(os_done.sem, 1)
                o_sum(h, 3)

        @block.gpsimd
        def _(pool):
            ctx.clear_last(pool)
            ch = Chain(ctx, nc, pool, "h_pool_chain")

            def lo_of(w, r):
                pool.tensor_tensor(wlo[w][:, :], raw[r][:, :], whi[w][:, :].bitcast(F32), ALU.subtract).then_inc(lo_done.sem, 1)

            pool.sem_inc(lo_done.sem, 2)
            for t in (2, 3):
                pool.wait_ge(loaded[0].sem, 16 * t)
                pool.wait_ge(hi_done.sem, t + 1)
                if t == 3:
                    pool.wait_ge(piece_done.sem, 3)
                lo_of((0, 1, 2, 0)[t], (0, 1, 0, 0)[t])
            sample_rec.start(pool)

            def split_next(h, n):
                if n in SPLIT_AT:
                    t = SPLIT_AT[n]
                    raw_loaded(pool, h, t)
                    pool.wait_ge(hi_done.sem, hi_done.at(h, t))
                    used_wait(pool, h, t)
                    lo_of(slot(t % NTL), 0 if t == NTL else t % 2)

            def kept(name, src, h):
                return pool.tensor_copy(c["s_" + name][:, bass.ds(h, 1), :].rearrange("p o n -> p (o n)"), src[:, T:NT])

            def differences(h, k):
                if k == 0:
                    pool.wait_ge(cum_ready.sem, cum_ready.at(h, 1))
                pool.wait_ge(rec_done.sem, rec_done.at(h, max(k - 1, 0)))
                pool.wait_ge(lv_k.sem, lv_k.at(h, k - 1))
                cu, L = fc[:, k * P:(k + 1) * P], LV[k % 2]
                for lv in range(LEVELS):
                    b = 1 << lv
                    v, w = level_view(cu, lv), level_view(L[:, lv, :], lv)
                    mid = v[:, :, 0, b - 1:b].broadcast_to([P, HALF // b, b])
                    ch(pool.tensor_tensor(w[:, :, 0, :], v[:, :, 0, :], mid, ALU.subtract))
                    ch(pool.tensor_tensor(w[:, :, 1, :], mid, v[:, :, 1, :], ALU.subtract))
                ch(pool.tensor_tensor(L[:, LEVELS, :], cu, cu[:, P - 1:P].broadcast_to([P, P]), ALU.subtract))
                ch(pool.tensor_scalar(L[:, LEVELS + 1, :], cu, -1.0, 0.0, ALU.mult, ALU.add))
                ch.sync()
                pool.sem_inc(lv_diff.sem, 1)

            def squares(h, src, u):
                if u == 2:
                    pool.wait_ge(o_summed.sem, o_summed.at(h, 2))
                s = slice((u % 2) * 512, (u % 2) * 512 + 512)
                pool.tensor_tensor(PT[:, s], src[:, s], src[:, s], ALU.mult).then_inc(o_squared.sem, 1)

            with pool.Fori(0, H) as h:
                pool.wait_ge(qk_ready.sem, qk_ready.at(h, 0))
                pool.wait_ge(piece_read.sem, piece_read.at(h, 0))
                ch(kept("q", qT, h))
                ch(kept("k", kT, h))
                ch(kept("v", vT, h))
                ch.sync()
                pool.sem_inc(sample_qkv.sem, 1)
                for i in range(NB):
                    for n in ATT_PIECES[i]:
                        split_next(h, n)
                    if i in (5, 6):
                        differences(h, i - 5)
                pool.wait_ge(sig_used.sem, sig_used.at(h, 9))
                pool.wait_ge(piece_read.sem, piece_read.at(h, 9))
                for n, src in (("f", fc), ("kk", kk), ("qh", qh), ("ib", ib), ("og", og)):
                    ch(kept(n, src, h))
                ch.sync()
                pool.sem_inc(sample_rec.sem, 1)
                pool.wait_ge(pv_read.sem, pv_read.at(h, NB))
                squares(h, oraw, 0)
                squares(h, oraw, 1)
                for k in range(NB):
                    if 0 < k < NB - 1:
                        differences(h, k + 1)
                    for n in REC_PIECES[k]:
                        split_next(h, n)
                    if k == NB - 2:
                        pool.wait_ge(o_read.sem, o_read.at(h, NB // 2))
                        squares(h, braw, 2)
                pool.wait_ge(o_read.sem, o_read.at(h, NB - 1))
                pool.wait_ge(o_summed.sem, o_summed.at(h, 2))
                most, rest = slice(512, T - P), slice(T - P, T)
                pool.tensor_tensor(PT[:, most], braw[:, most], braw[:, most], ALU.mult)
                pool.wait_ge(o_read.sem, o_read.at(h, NB))
                pool.tensor_tensor(PT[:, rest], braw[:, rest], braw[:, rest], ALU.mult).then_inc(o_squared.sem, 1)
                ch.reset()

        @block.vector
        def _(dve):
            ch = Chain(ctx, nc, dve, "h_dve_chain")
            vec, lam, lb = c["vec"], c["lam"], c["lb"]
            ones_row = c["ones"]
            ch(dve.tensor_scalar(subg[:, :], vec[:, VEC["sub_g"][0]:VEC["sub_g"][0] + 1], 1.0 - LAM_INIT, None, ALU.mult))
            for sig in (lv_k, st_ready, sig_used, o_normed, ada_added):
                sig.start(dve)

            def rope(j, u):
                ch(dve.tensor_tensor(rb[:, :], X[:, 0, 0:TH], sin[:, cols(j)], ALU.mult))
                ch(dve.tensor_tensor(rg[u][:, :], rg[u][:, :], cos[:, cols(j)], ALU.mult))
                ch.sync()
                ch(dve.tensor_tensor(rb[:, :], rb[:, :], rg[u][:, :], ALU.add))
                ch.sync()

            def rope_end(j, dst):
                dve.tensor_tensor(dst[:, cols(j)], rb[:, :], rr[:, :], ALU.mult).then_inc(qk_ready.sem, 1)

            for n in range(6):
                dve.wait_ge(qk_summed.sem, n + 1)
                rope(n % NP, n % 2)
                dve.wait_ge(qk_rstd.sem, n + 1)
                rope_end(n % NP, qT if n < 3 else kT)
            ch.reset()

            def maxima(h, i):
                nk = (i + 1) * P
                dve.wait_ge(scores.sem, scores.at(h, i + 1))
                b0 = score_bank(i, 0)
                both = SP_[:, b0:b0 + 2, :] if i < NB // 2 else SP_[:, :, :].rearrange("p (m a) b -> p m (a b)", m=2)
                diag = both[:, :, i * P:nk]
                ch(dve.tensor_tensor(diag, diag, causal[:, :].unsqueeze(1).broadcast_to([P, 2, P]), ALU.add))
                ch.sync()
                ch(dve.tensor_reduce(sm[:, 0:2], both[:, :, 0:nk], AX.X, ALU.max))
                ch.sync()
                dve.tensor_scalar(sm[:, 2:4], sm[:, 0:2], -SCALE, None, ALU.mult).then_inc(row_max.sem, 1)

            def weigh(h, i):
                nk = (i + 1) * P
                dve.wait_ge(exped.sem, exped.at(h, i + 1))
                ch(dve.reciprocal(sm[:, 6:8], sm[:, 4:6]))
                ch.sync()
                ch(dve.tensor_tensor(sm[:, 7:8], sm[:, 7:8], lam[:, 3:4], ALU.mult))
                ch(dve.tensor_scalar(E[:, 0, 0:nk], E[:, 0, 0:nk], sm[:, 6:7], None, ALU.mult))
                ch.sync()
                dve.scalar_tensor_tensor(out=E[:, 0, 0:nk], in0=E[:, 1, 0:nk], scalar=sm[:, 7:8], in1=E[:, 0, 0:nk],
                                         op0=ALU.mult, op1=ALU.add).then_inc(weighed.sem, 1)

            def cut(h, s):
                dve.wait_ge(ex_ready.sem, ex_ready.at(h, s + 1))
                dve.tensor_scalar(ex[s % 2][:, :], ex[s % 2][:, :], BIG, 1.0, ALU.min, ALU.add).then_inc(ex_cut.sem, 1)

            def use_sigmoid(h, s):
                t, j = PIECES[SIGMOID[s]]
                kind = TILES[t]
                dve.wait_ge(sig_ready.sem, sig_ready.at(h, s + 1))
                e = ex[s % 2][:, :]
                if kind == "f":
                    one_lb, low = (lb[:, n, bass.ds(h, 1)] for n in (1, 0))
                    ch(dve.tensor_scalar(fc[:, cols(j)], e, one_lb, low, ALU.mult, ALU.add))
                    ch.sync()
                    dve.tensor_scalar(kk[:, cols(j)], fc[:, cols(j)], -1.0, 1.0, ALU.mult, ALU.add).then_inc(sig_used.sem, 1)
                else:
                    dve.wait_ge(piece_read.sem, piece_read.at(h, SIGMOID[s] + 1))
                    dve.tensor_tensor(dest[kind][:, cols(j)], dest[kind][:, cols(j)], e, ALU.mult).then_inc(sig_used.sem, 1)

            def cumulate(h):
                dve.wait_ge(log_f.sem, log_f.at(h, 1))
                for k in range(NB):
                    g = fc[:, k * P:(k + 1) * P]
                    ch(dve.tensor_tensor_scan(g, ones_row[:, :], g, 0.0, ALU.mult, ALU.add))
                ch.sync()
                dve.sem_inc(cum_ready.sem, 1)

            def operands(h, k):
                L, Q, ck = LV[k % 2], QL[k % 2], slice(k * P, (k + 1) * P)
                dve.wait_ge(lv_exp.sem, lv_exp.at(h, k + 1))
                dve.wait_ge(os_done.sem, os_done.at(h, k - 1 if k >= 2 else 0))
                for lv in range(LEVELS):
                    b = 1 << lv
                    q2 = level_view(qh[:, ck], lv)[:, :, 1, :]
                    e2 = level_view(L[:, lv, :], lv)[:, :, 1, :]
                    ch(dve.tensor_tensor(Q[:, lv * HALF:(lv + 1) * HALF].rearrange("p (n b) -> p n b", b=b), q2, e2, ALU.mult))
                ch(dve.tensor_tensor(Q[:, LEVELS * HALF:], qh[:, ck], L[:, LEVELS + 1, :], ALU.mult))
                ch.sync()
                kl = L[:, 0:LEVELS + 1, :]
                dve.tensor_tensor(kl, kl, kk[:, ck].unsqueeze(1).broadcast_to([P, LEVELS + 1, P]), ALU.mult).then_inc(lv_k.sem, 1)

            def assemble(h, k):
                dve.wait_ge(rec_done.sem, rec_done.at(h, k + 1))
                dve.wait_ge(os_done.sem, os_done.at(h, k))
                ch(dve.tensor_tensor(AT[:, :], SP_[:, 0, 0:P], c["ident"][:, :], ALU.mult))
                ch.sync()
                for lv in range(LEVELS):
                    b = 1 << lv
                    s = slice(lv * HALF, (lv + 1) * HALF)
                    ins = dve.copy_predicated(level_view(AT[:, :], lv)[:, :, 1, :],
                                              lmask[:, s].rearrange("p (n b) -> p n b", b=b),
                                              SP_[:, 1, s].rearrange("p (n b) -> p n b", b=b))
                    if lv < LEVELS - 1:
                        ch(ins)
                        ch.sync()
                ins.then_inc(at_ready.sem, 1)

            def state(h, k):
                dve.wait_ge(os_done.sem, os_done.at(h, k + 1))
                dve.wait_ge(o_read.sem, o_read.at(h, k + 1))
                if k == 0:
                    dve.wait_ge(dec_ready.sem, dec_ready.at(h, 1))
                    dve.wait_ge(st_stored.sem, st_stored.at(h, 0))
                    dve.tensor_copy(St[:, :], SP_[:, 3, P:2 * P]).then_inc(st_ready.sem, 1)
                else:
                    dve.wait_ge(st_ready.sem, st_ready.at(h, k))
                    dve.scalar_tensor_tensor(out=St[:, :], in0=St[:, :], scalar=dec[:, k:k + 1], in1=SP_[:, 3, P:2 * P],
                                             op0=ALU.mult, op1=ALU.add).then_inc(st_ready.sem, 1)

            def o_norm(h, u):
                src, g = (oraw, subg[:, 0:1]) if u < 2 else (braw, vec[:, VEC["hgrn_g"][0]:VEC["hgrn_g"][0] + 1])
                s = slice((u % 2) * 512, (u % 2) * 512 + 512)
                dve.wait_ge(o_rstd.sem, o_rstd.at(h, u + 1))
                if u >= 2:
                    dve.wait_ge(o_stored.sem, o_stored.at(h, 2))
                if u < 2:
                    dve.scalar_tensor_tensor(out=E[:, 1, s], in0=src[:, s], scalar=g, in1=E[:, 0, s], op0=ALU.mult,
                                             op1=ALU.mult).then_inc(o_normed.sem, 1)
                else:
                    ch(dve.scalar_tensor_tensor(out=E[:, 1, s], in0=src[:, s], scalar=g, in1=E[:, 0, s], op0=ALU.mult, op1=ALU.mult))
                    ch.sync()
                    dve.tensor_tensor(E[:, 1, s], E[:, 1, s], og[:, s], ALU.mult).then_inc(o_normed.sem, 1)

            with dve.Fori(0, H) as h:
                done = 0
                for i in range(NB):
                    maxima(h, i)
                    weigh(h, i)
                    if i == 5:
                        cumulate(h)
                    for n in ATT_PIECES[i]:
                        if n in SIGMOID:
                            s = SIGMOID.index(n)
                            if s == 0:
                                dve.wait_ge(rec_done.sem, rec_done.at(h, 0))
                                dve.wait_ge(sample_rec.sem, sample_rec.at(h, 0))
                            cut(h, s)
                            if s:
                                use_sigmoid(h, s - 1)
                operands(h, 0)
                use_sigmoid(h, len(SIGMOID) - 1)
                for k in range(NB):
                    assemble(h, k)
                    if k + 1 < NB:
                        operands(h, k + 1)
                    if k == 0:
                        o_norm(h, 0)
                        o_norm(h, 1)
                    if 1 <= k <= 6:
                        u = k - 1
                        j = u % NP
                        dve.wait_ge(qk_summed.sem, qk_summed.at(h, u + 1))
                        rope(j, u % 2)
                        dve.wait_ge(qk_rstd.sem, qk_rstd.at(h, u + 1))
                        if u == 0:
                            dve.wait_ge(sample_qkv.sem, sample_qkv.at(h, 1))
                            dve.wait_ge(kv_stored.sem, kv_stored.at(h, 2))
                        rope_end(j, qT if u < 3 else kT)
                    if k % 2 == 0:
                        q = k // 2
                        dve.wait_ge(ada_read.sem, ada_read.at(h, q + 1))
                        dve.tensor_scalar(c["mod"][:, bass.ds(h * 4 + (2 * KT + q), 1), :].rearrange("p o n -> p (o n)"), av[q % 2][:, :],
                                          vec[:, bass.ds(h * 4 + (2 * KT + q), 1)], None, ALU.add).then_inc(ada_added.sem, 1)
                    state(h, k)
                o_norm(h, 2)
                o_norm(h, 3)
                ch.reset()


def gates_stage(nc, a, o, c, d, xh, xl, gate, slots):
    with Stage(c) as ctx:
        mem = Memory(nc, "g", R_X, R3)
        W = Stream(ctx, nc, slots, "g")
        kp = [mem(f"kp{i}", [P, D]) for i in range(PAGES)]
        vp = mem("vp", [P, PAGES, D])
        qB, vB, st = mem("qB", [P, D]), mem("vB", [P, D]), mem("st", [P, D])
        rows = mem("rows", [H * NS, 2, P])
        prow = mem("prow", [H, D])
        s_tok = mem("s_tok", [P, PAGES, 2 * H])
        pd = mem("pd", [P, 2 * H])
        sc = mem("sc", [2 * H, PAST + 1])
        sv = mem("sv", [2 * H, 8])
        ge = mem("ge", [P, NT])
        pn = mem("pn", [2 * H, P])
        pt = mem("pt", [P, (PAGES + 1) * H])
        vn = mem("vn", [P, H])
        comb, coef = mem("comb", [2 * H, H]), mem("coef", [2 * H, 3])
        blk2 = mem("blk2", [P, 2])
        pages = mem("pages", [1, NS * PAGES], I32)
        subg = mem("subg", [P, 1])
        nsq, nrs = mem("nsq", [P, 2, H * NS]), mem("nrs", [P, 2, H * NS])
        Y = ctx.enter_context(nc.psum_tensor("g_Y", [P, 2, 512], F32))
        Yf = Y[:, :, :].rearrange("p a b -> p (a b)")

        def S(n, per=1, **k):
            return Sig(ctx, nc, f"g_{n}", per=per, **k)

        consts, page_in = S("consts_in", 0, step=16), S("pages_in", 0, step=16)
        k_in = [S(f"k_in{i}", pre=1, step=16) for i in range(PAGES)]
        v_in, st_in, st_out = S("v_in", 4, step=16), S("st_in", pre=1, step=16), S("st_out", step=16, init=1)
        rows_turned, rows_ready, rows_out = S("rows_turned", 0), S("rows_ready", 0), S("rows_out", 0, step=16)
        q_in, vb_in = S("q_in", pre=1, step=16), S("v_rows_in", pre=1, step=16)
        k_scaled, k_summed = S("k_scaled", 2), S("k_summed", 4)
        st_new, rec_out, rec_read = S("st_new"), S("rec_out"), S("rec_read", init=1)
        s_turned, s_max, s_exp, s_norm = S("s_turned"), S("s_max"), S("s_exp"), S("s_norm")
        p_turned, p_read, pv, pv_read = S("p_turned"), S("p_read"), S("pv", init=1), S("pv_read", init=1)
        pv_row, pv_turned = S("pv_row"), S("pv_turned")
        gate_e, gate_cut = S("gate_e", 2), S("gate_cut", 2)
        n_sq, n_sum, n_rs, n_norm, n_st = (S("n_" + n) for n in ("sq", "sum", "rs", "norm", "st"))
        block = ctx.enter_context(nc.Block())
        wt = a["w_in"]
        N_CONST = 3

        def pair(ap, i):
            return ap[:, :, bass.ds(i, 1)]

        @block.sync
        def _(sp):
            def page_of(i, j):
                return sp.value_load(pages[0:1, bass.ds(i * PAGES + j, 1)], min_val=0, max_val=POOL_PAGES - 1)

            def load_keys(i, j):
                sp.dma_start(kp[j][:, :], flat(a["cache_k"][bass.ds(page_of(i, j), 1)])).then_inc(k_in[j].sem, 16)

            def load_state(i):
                sp.dma_start(st[:, :], flat(a["state"][bass.ds(i, 1)])).then_inc(st_in.sem, 16)

            def load_spread(i):
                sp.dma_start(qB[:, :], d["q_rows"][bass.ds(i, 1), :].broadcast_to([P, D])).then_inc(q_in.sem, 16)

            def load_values(i):
                sp.dma_start(vB[:, :], d["v_rows"][bass.ds(i, 1), :].broadcast_to([P, D])).then_inc(vb_in.sem, 16)

            def load_weights(i, s):
                W.load(sp, i, s, flat(wt[bass.ds(i * 2 + (s + 3 + NTL * H), 1)]))

            W.take_over(sp, None, None)
            for t, n in ((comb, "comb"), (blk2, "blk2"), (coef, "coef")):
                sp.dma_start(t[:, :], a[n]).then_inc(consts.sem, 16)
            sp.dma_start(pages[:, :], a["pages"]).then_inc(page_in.sem, 16)
            sp.wait_ge(page_in.sem, 16)
            sp.wait_ge(rows_ready.sem, 1)
            sp.dma_start(d["q_rows"].rearrange("n (h m) -> h n m", h=H), rows[:, 0, :]).then_inc(rows_out.sem, 16)
            sp.dma_start(d["v_rows"].rearrange("h (n m) -> (h n) m", m=P), rows[:, 1, :]).then_inc(rows_out.sem, 16)
            load_keys(0, 0)
            sp.wait_ge(rows_out.sem, 32)
            load_spread(0)
            for j in range(1, PAGES):
                load_keys(0, j)
            load_state(0)
            load_values(0)

            def body(i, last):
                if last:
                    W.load(sp, i + 1, 0, flat(a["w_mix"][0:1]))
                    W.load(sp, i + 1, 1, flat(a["w_mix"][1:2]))
                else:
                    load_weights(i + 1, 0)
                sp.wait_ge(pv.sem, pv.at(i, 0))
                for j in range(PAGES):
                    sp.dma_start(vp[:, j, :], flat(a["cache_v"][bass.ds(page_of(i, j), 1)])).then_inc(v_in.sem, 16)
                if not last:
                    load_weights(i + 1, 1)
                    for j in range(PAGES):
                        sp.wait_ge(k_summed.sem, k_summed.at(i, j + 1))
                        load_keys(i + 1, j)
                    load_spread(i + 1)
                    sp.wait_ge(st_new.sem, st_new.at(i, 1))
                    load_values(i + 1)
                    sp.wait_ge(st_out.sem, st_out.at(i, 1))
                    sp.wait_ge(rec_out.sem, rec_out.at(i, 1))
                    load_state(i + 1)
            turns(sp, NS, body)
            sp.wait_ge(W.loaded[1].sem, W.loaded[1].at(NS, 1))

        @block.scalar
        def _(act):
            act.preload_act_table_set(TABLES)
            W.head_start(act=act)
            W.free.start(act)
            st_out.start(act)
            ch = Chain(ctx, nc, act, "g_act_chain")

            act.wait_ge(rows_turned.sem, 1)
            act.activation(rows[:, :, :], Y[0:H * NS, 0, 0:2 * P].rearrange("p (a b) -> p a b", a=2), ACT.Copy).then_inc(rows_ready.sem, 1)
            W.take_over(None, act, None)

            def body(i, last):
                for s in range(2):
                    W.split_hi(act, i + s, 1 - s)
                    for j in range(NP):
                        ch.sync()
                        W.wait_piece(act, i, s, j)
                        act.activation(ge[:, cols(j)], W.out(s, j), ACT.Exp, scale=-1.0).then_inc(W.free.sem, 1)
                        if (s, j) == (0, 2):
                            act.wait_ge(s_max.sem, s_max.at(i, 1))
                            act.activation(sc[:, :], sc[:, :], ACT.Exp, bias=sv[:, 1:2], scale=SCALE,
                                           accum_out=sv[:, 2:3]).then_inc(s_exp.sem, 1)
                        if (s, j) == (1, 0):
                            act.wait_ge(pv.sem, pv.at(i, 1))
                            act.activation(prow[:, :], Yf[0:H, :], ACT.Copy).then_inc(pv_row.sem, 1)
                            act.wait_ge(st_new.sem, st_new.at(i, 1))
                            act.dma_start(flat(o["s_state"][bass.ds(i, 1)]), st[:, :]).then_inc(st_out.sem, 16)
                    act.wait_ge(gate_cut.sem, gate_cut.at(i, s + 1))
                    ch(act.activation(ge[:, :], ge[:, :], ACT.Ln))
                    ch.sync()
                    ch(act.activation(gate[s][:, bass.ds(i, 1), :].rearrange("p o n -> p (o n)"), ge[:, :], ACT.Exp, scale=-1.0))
                ch.reset()
            turns(act, NS, body)
            act.wait_ge(n_sum.sem, 1)
            ch(act.activation(nrs[:, :, :], Y[:, 0, 0:2 * H * NS].rearrange("p (a b) -> p a b", a=2), ACT.Ln, bias=c["eps"][:, 0:1]))
            ch.sync()
            act.activation(nrs[:, :, :], nrs[:, :, :], ACT.Exp, scale=-0.5).then_inc(n_rs.sem, 1)
            act.wait_ge(n_norm.sem, 1)
            for b, name in enumerate(("oa", "ob")):
                act.dma_start(d[name][:, :, T:NT].rearrange("h p n -> p h n"),
                              nsq[:, b, :].rearrange("p (h n) -> p h n", h=H)).then_inc(n_st.sem, 16)
            act.wait_ge(n_st.sem, 32)
            act.wait_ge(st_out.sem, st_out.at(NS, 0))

        @block.tensor
        def _(pe):
            W.head_start(pe=pe)
            pv.start(pe)
            ones, ident = c["ones"], c["ident"]
            for n, src in enumerate((c["s_q"], c["s_ib"])):
                ins = pe.transpose(Y[0:H * NS, 0, n * P:(n + 1) * P], src[:, :, :].rearrange("p h n -> p (h n)"), ident[:, :])
            ins.then_inc(rows_turned.sem, 1)
            pe.wait_ge(consts.sem, 16 * N_CONST)

            def body(i, last):
                for s in range(2):
                    for j in range(NP):
                        W.piece(pe, i, s, j, xh, xl)
                        if (s, j) == (0, 2):
                            pe.wait_ge(k_summed.sem, k_summed.at(i, PAGES))
                            pe.wait_ge(rec_read.sem, rec_read.at(i, 0))
                            pe.wait_ge(pv_read.sem, pv_read.at(i, 0))
                            for b in range(PAGES):
                                pe.transpose(Y[0:2 * H, 0, b * P:(b + 1) * P], s_tok[:, b, :], ident[:, :])
                            pe.matmul(Y[0:2 * H, 1, 0:1], pd[:, :], ones[:, 0:1], start=True, stop=True).then_inc(s_turned.sem, 1)
                        if (s, j) == (1, 0):
                            pe.wait_ge(s_norm.sem, s_norm.at(i, 1))
                            for b in range(PAGES):
                                pe.matmul(Y[:, 0, b * H:(b + 1) * H], sc[:, b * P:(b + 1) * P], comb[:, :], start=True, stop=True)
                            pe.matmul(Y[:, 0, PAGES * H:(PAGES + 1) * H], pn[:, :], comb[:, :], start=True, stop=True)\
                              .then_inc(p_turned.sem, 1)
                            pe.wait_ge(p_read.sem, p_read.at(i, 1))
                            pe.wait_ge(v_in.sem, v_in.at(i, PAGES))
                            for half in range(2):
                                for b in range(PAGES):
                                    ins = pe.matmul(Y[0:H, half, :], pt[:, b * H:(b + 1) * H], vp[:, b, half * 512:(half + 1) * 512],
                                                    start=(b == 0), stop=(b == PAGES - 1))
                            ins.then_inc(pv.sem, 1)
                        if (s, j) == (1, 1):
                            pe.wait_ge(pv_row.sem, pv_row.at(i, 1))
                            for h in range(H):
                                ins = pe.matmul(Y[:, 1, h:h + 1], prow[:, h * P:(h + 1) * P], ident[0:H, h:h + 1], start=True, stop=True)
                            ins.then_inc(pv_turned.sem, 1)
                        if (s, j) == (1, 2):
                            pe.wait_ge(st_new.sem, st_new.at(i, 1))
                            for b in range(NS):
                                ins = pe.matmul(Y[:, 0, b:b + 1], st[:, b * P:(b + 1) * P],
                                                c["s_qh"][:, bass.ds(i, 1), b:b + 1].rearrange("p o n -> p (o n)"),
                                                start=True, stop=True)
                            ins.then_inc(rec_out.sem, 1)
            turns(pe, NS, body)
            pe.wait_ge(n_sq.sem, 1)
            pe.matmul(Y[:, 0, 0:2 * H * NS], c["ones128"][:, :], nsq[:, :, :].rearrange("p a b -> p (a b)"),
                      start=True, stop=True).then_inc(n_sum.sem, 1)

        @block.gpsimd
        def _(pool):
            ctx.clear_last(pool)
            W.head_start(pool=pool)

            W.take_over(None, None, pool)

            def body(i, last):
                for j in (2, 3):
                    pool.wait_ge(q_in.sem, q_in.at(i, 0))
                    pool.wait_ge(k_in[j].sem, k_in[j].at(i, 0))
                    pool.tensor_tensor(kp[j][:, :], kp[j][:, :], qB[:, :], ALU.mult).then_inc(k_scaled.sem, 1)
                W.split_lo(pool, i, 1)
                W.split_lo(pool, i + 1, 0)
            turns(pool, NS, body)

        @block.vector
        def _(dve):
            pv_read.start(dve)
            rec_read.start(dve)
            ch = Chain(ctx, nc, dve, "g_dve_chain")
            dve.wait_ge(consts.sem, 16 * N_CONST)
            ch(dve.tensor_scalar(subg[:, :], c["vec"][:, VEC["sub_g"][0]:VEC["sub_g"][0] + 1], 1.0 - LAM_INIT, None, ALU.mult))
            ch(dve.tensor_tensor(coef[:, 2:3], coef[:, 1:2], c["lam"][0:2 * H, 3:4], ALU.mult))
            ch.sync()
            ch(dve.tensor_tensor(coef[:, 2:3], coef[:, 2:3], coef[:, 0:1], ALU.add))
            ch.sync()
            ch.reset()

            def sum_page(i, j):
                ch(dve.tensor_reduce(s_tok[:, j, :], kp[j][:, :].rearrange("p (h n) -> p h n", n=DH), AX.X, ALU.add))
                ch.sync()
                dve.sem_inc(k_summed.sem, 1)

            def cut(i, s):
                W.wait_piece(dve, i, s, 2)
                dve.wait_ge(W.free.sem, W.free.at(i, 3 * s + 3))
                dve.tensor_scalar(ge[:, :], ge[:, :], BIG, 1.0, ALU.min, ALU.add).then_inc(gate_cut.sem, 1)

            def body(i, last):
                sq, sk, sv_, skk, sf, sob, soa = (c["s_" + n] for n in ("q", "k", "v", "kk", "f", "ob", "oa"))

                def head(t):
                    return t[:, bass.ds(i, 1), :].rearrange("p o n -> p (o n)").unsqueeze(2)
                dve.wait_ge(pv_read.sem, pv_read.at(i, 0))
                ch(dve.tensor_tensor(vn[:, :].unsqueeze(2), pair(sq, i), pair(sk, i), ALU.mult))
                ch.sync()
                ch(dve.tensor_tensor(pd[:, :].rearrange("p (h n) -> p h n", n=2), vn[:, :].unsqueeze(2).broadcast_to([P, H, 2]),
                                     blk2[:, :].unsqueeze(1).broadcast_to([P, H, 2]), ALU.mult))
                for j in range(2):
                    dve.wait_ge(k_in[j].sem, k_in[j].at(i, 0))
                    dve.wait_ge(q_in.sem, q_in.at(i, 0))
                    ch(dve.tensor_tensor(kp[j][:, :], kp[j][:, :], qB[:, :], ALU.mult))
                    ch.sync()
                    sum_page(i, j)
                for j in (2, 3):
                    dve.wait_ge(k_scaled.sem, k_scaled.at(i, j - 1))
                    sum_page(i, j)
                st3 = st[:, :].rearrange("p (b v) -> p b v", b=NS)
                dve.wait_ge(st_in.sem, st_in.at(i, 0))
                ch(dve.tensor_tensor(st3, st3, head(sf).broadcast_to([P, NS, P]), ALU.mult))
                dve.wait_ge(s_turned.sem, s_turned.at(i, 1))
                ch(dve.tensor_copy(sc[:, 0:PAST], Y[0:2 * H, 0, :]))
                ch(dve.tensor_copy(sc[:, PAST:PAST + 1], Y[0:2 * H, 1, 0:1]))
                ch.sync()
                ch(dve.tensor_reduce(sv[:, 0:1], sc[:, :], AX.X, ALU.max))
                ch.sync()
                dve.tensor_scalar(sv[:, 1:2], sv[:, 0:1], -SCALE, None, ALU.mult).then_inc(s_max.sem, 1)
                dve.wait_ge(vb_in.sem, vb_in.at(i, 0))
                vB3 = vB[:, :].rearrange("p (b v) -> p b v", b=NS)
                ch(dve.tensor_tensor(vB3, vB3, head(skk).broadcast_to([P, NS, P]), ALU.mult))
                dve.wait_ge(s_exp.sem, s_exp.at(i, 1))
                ch(dve.reciprocal(sv[:, 3:4], sv[:, 2:3]))
                ch.sync()
                ch(dve.tensor_tensor(sv[:, 3:4], sv[:, 3:4], coef[:, 2:3], ALU.mult))
                ch.sync()
                ch(dve.tensor_scalar(sc[:, :], sc[:, :], sv[:, 3:4], None, ALU.mult))
                ch.sync()
                dve.tensor_scalar(pn[:, :], c["ones"][0:2 * H, :], sc[:, PAST:PAST + 1], None, ALU.mult).then_inc(s_norm.sem, 1)
                ch.sync()
                dve.tensor_tensor(st[:, :], st[:, :], vB[:, :], ALU.add).then_inc(st_new.sem, 1)
                cut(i, 0)
                dve.wait_ge(p_turned.sem, p_turned.at(i, 1))
                dve.tensor_copy(pt[:, :], Y[:, 0, 0:(PAGES + 1) * H]).then_inc(p_read.sem, 1)
                dve.wait_ge(p_read.sem, p_read.at(i, 1))
                ch(dve.tensor_tensor(vn[:, :].unsqueeze(2), pair(sv_, i), pt[:, PAGES * H:].unsqueeze(2), ALU.mult))
                ch.sync()
                dve.wait_ge(pv_turned.sem, pv_turned.at(i, 1))
                dve.tensor_tensor(pair(soa, i), Y[:, 1, 0:H].unsqueeze(2), vn[:, :].unsqueeze(2), ALU.add).then_inc(pv_read.sem, 1)
                dve.wait_ge(rec_out.sem, rec_out.at(i, 1))
                copy(dve, head(sob).rearrange("p n o -> p (n o)"), Y[:, 0, 0:NS]).then_inc(rec_read.sem, 1)
                cut(i, 1)
                ch.reset()
            turns(dve, NS, body)
            dve.wait_ge(rec_read.sem, rec_read.at(NS, 0))
            srcs = [c["s_oa"][:, :, :].rearrange("p a b -> p (a b)"), c["s_ob"][:, :, :].rearrange("p a b -> p (a b)")]
            dve.wait_ge(pv_read.sem, pv_read.at(NS, 0))
            ch(dve.tensor_tensor(nsq[:, 0, :], srcs[0], srcs[0], ALU.mult))
            dve.tensor_tensor(nsq[:, 1, :], srcs[1], srcs[1], ALU.mult).then_inc(n_sq.sem, 1)
            dve.wait_ge(n_rs.sem, 1)
            ch(dve.scalar_tensor_tensor(out=nsq[:, 0, :], in0=srcs[0], scalar=subg[:, 0:1], in1=nrs[:, 0, :], op0=ALU.mult, op1=ALU.mult))
            hg = c["vec"][:, VEC["hgrn_g"][0]:VEC["hgrn_g"][0] + 1]
            ch(dve.scalar_tensor_tensor(out=nsq[:, 1, :], in0=srcs[1], scalar=hg, in1=nrs[:, 1, :], op0=ALU.mult, op1=ALU.mult))
            ch.sync()
            dve.tensor_tensor(nsq[:, 1, :], nsq[:, 1, :], c["s_og"][:, :, :].rearrange("p a b -> p (a b)"), ALU.mult).then_inc(n_norm.sem, 1)


BRANCH_TURNS = KT // 2
MIX_TURNS = 3 * BRANCH_TURNS


def mix_stage(nc, a, c, d, x, oh, ol, gate, mh, ml, acc, slots):
    with Stage(c) as ctx:
        W = Stream(ctx, nc, slots, "m")
        mem = Memory(nc, "m", R_SQ + WIDE // KT, R3)
        m = [mem(f"m{i}", [P, TH]) for i in range(2)]
        sq = [mem(f"sq{i}", [P, NT]) for i in range(2)]
        t8 = mem("t8", [P, NS])

        def S(n, per=0, **k):
            return Sig(ctx, nc, f"m_{n}", per=per, **k)

        x_in = [S(f"x_in{k}", step=16) for k in range(KT)]
        o_hi, o_lo, o_used = S("o_hi"), S("o_lo"), S("o_used")
        merged, m_hi, m_lo = S("merged", 6), S("m_hi", 6), S("m_lo", 6, init=2)
        squared, added = S("squared", 2, init=2), S("squares_added", 2, init=2)
        cleared = S("acc_cleared")
        block = ctx.enter_context(nc.Block())
        wt = a["w_mix"]
        A_END, B_END = BRANCH_TURNS, 2 * BRANCH_TURNS

        def turns_of(eng, body):
            body(0, "a")
            with eng.Fori(1, A_END - 1) as i:
                body(i, "a")
            body(A_END - 1, "a")
            body(A_END, "b")
            with eng.Fori(A_END + 1, B_END) as i:
                body(i, "b")
            with eng.Fori(B_END, MIX_TURNS - 1) as i:
                body(i, "out")
            body(MIX_TURNS - 1, "out")

        def is_at(turn, n):
            return isinstance(turn, int) and turn == n

        def tile_of(t, turn, first, s):
            return t[:, bass.ds(turn * 2 + (s - 2 * first), 1), :].rearrange("p o n -> p (o n)")

        @block.sync
        def _(sp):
            W.take_over(sp, None, None)
            for k in range(KT):
                sp.dma_start(x[:, k, :], flat(d["oa"][k:k + 1])).then_inc(x_in[k].sem, 16)

            def body(i, phase):
                for s in range(2):
                    W.load(sp, i + 1, s, flat(a["w_ffn"][s:s + 1] if is_at(i, MIX_TURNS - 1) else wt[bass.ds(i * 2 + (s + 2), 1)]))
                if is_at(i, 0) or is_at(i, A_END):
                    n, src = (0, d["ob"]) if i == 0 else (1, None)
                    for k in range(KT):
                        sp.wait_ge(o_hi.sem, n * KT + k + 1)
                        sp.wait_ge(o_lo.sem, n * KT + k + 1)
                        sp.dma_start(x[:, k, :], flat(src[k:k + 1]) if src is not None else a["xT"][:, k, :]).then_inc(x_in[k].sem, 16)
            turns_of(sp, body)
            sp.wait_ge(W.loaded[1].sem, W.loaded[1].at(MIX_TURNS, 1))

        def o_ready(eng, n, k):
            eng.wait_ge(x_in[k].sem, 16 * (n + 1))
            if n:
                if k < KT - 1:
                    eng.wait_ge(o_used.sem, k + 1)
                else:
                    eng.wait_ge(W.done.sem, W.done.at(A_END, 0))

        @block.scalar
        def _(act):
            W.head_start(act=act)
            squared.start(act)

            def high(n):
                for k in range(KT):
                    o_ready(act, n, k)
                    act.activation(oh[:, k, :], x[:, k, :], ACT.Copy).then_inc(o_hi.sem, 1)

            W.take_over(None, act, None)
            high(0)

            def square(i, s):
                act.wait_ge(W.free.sem, W.free.at(i, 3 * s + 3))
                act.wait_ge(added.sem, added.at(i - B_END, s - 1))
                act.activation(sq[s][:, :], tile_of(x, i, B_END, s), ACT.Square).then_inc(squared.sem, 1)

            def body(i, phase):
                W.split_hi(act, i, 1)
                W.split_hi(act, i + 1, 0)
                if is_at(i, A_END - 1):
                    high(1)
                if phase == "out":
                    square(i, 0)
                    square(i, 1)
            turns_of(act, body)

        @block.tensor
        def _(pe):
            W.head_start(pe=pe)

            def by_tiles(i, s, n=None, mark=False):
                pe.wait_ge(W.hi_done.sem, W.hi_done.at(i, s + 1))
                pe.wait_ge(W.lo_done.sem, W.lo_done.at(i, s + 1))
                pe.wait_ge(W.free.sem, W.free.at(i, 3 * s - 3))
                for k in range(KT):
                    if n is not None:
                        pe.wait_ge(o_hi.sem, n * KT + k + 1)
                        pe.wait_ge(o_lo.sem, n * KT + k + 1)
                    for j in range(NP):
                        w = slice(k * P, (k + 1) * P)
                        for q, (wp, xp) in enumerate(((W.hi, oh), (W.hi, ol), (W.lo, oh))):
                            ins = pe.matmul(W.out(s, j), wp[s][:, w], xp[:, k, cols(j)], start=(k == 0 and q == 0),
                                            stop=(k == KT - 1 and q == 2))
                        if k == KT - 1:
                            ins.then_inc(W.done.sem, 1)
                    if mark and k < KT - 1:
                        ins.then_inc(o_used.sem, 1)

            def body(i, phase):
                if is_at(i, A_END - 1):
                    for j in range(NP):
                        W.piece(pe, i, 0, j, oh, ol)
                    by_tiles(i, 1, mark=True)
                elif is_at(i, 0) or is_at(i, A_END):
                    by_tiles(i, 0, n=0 if i == 0 else 1)
                    for j in range(NP):
                        W.piece(pe, i, 1, j, oh, ol)
                else:
                    if phase == "out":
                        pe.wait_ge(m_lo.sem, m_lo.at(BRANCH_TURNS, 0))
                    for s in range(2):
                        for j in range(NP):
                            W.piece(pe, i, s, j, *((mh, ml) if phase == "out" else (oh, ol)))
            turns_of(pe, body)

        @block.gpsimd
        def _(pool):
            ctx.clear_last(pool)
            W.head_start(pool=pool)
            m_lo.start(pool)
            added.start(pool)
            pool.memset(acc[:, :], 0.0).then_inc(cleared.sem, 1)
            pool.wait_ge(cleared.sem, 1)
            W.take_over(None, None, pool)

            def body(i, phase):
                for s in range(2):
                    W.split_lo(pool, i + s, 1 - s)
                    if phase == "b":
                        for j in range(NP):
                            n = 3 * s + j
                            pool.wait_ge(m_hi.sem, m_hi.at(i - A_END, n + 1))
                            hi, lo = (tile_of(t, i, A_END, s)[:, cols(j)] for t in (mh, ml))
                            pool.tensor_tensor(lo, m[n % 2][:, :], hi.bitcast(F32), ALU.subtract).then_inc(m_lo.sem, 1)
                    if phase == "out":
                        pool.wait_ge(squared.sem, squared.at(i - B_END, s + 1))
                        pool.wait_ge(added.sem, added.at(i - B_END, s))
                        pool.tensor_tensor(acc[:, :], acc[:, :], sq[s][:, :], ALU.add).then_inc(added.sem, 1)
            turns_of(pool, body)

        @block.vector
        def _(dve):
            W.free.start(dve)
            ch = Chain(ctx, nc, dve, "m_dve_chain")

            def low(n):
                for k in range(KT):
                    dve.wait_ge(o_hi.sem, n * KT + k + 1)
                    o_ready(dve, n, k)
                    dve.tensor_tensor(ol[:, k, :], x[:, k, :], oh[:, k, :].bitcast(F32), ALU.subtract).then_inc(o_lo.sem, 1)

            low(0)

            def body(i, phase):
                if phase == "out":
                    for k in range(KT):
                        dve.wait_ge(x_in[k].sem, 16 * 3)
                for s in range(2):
                    for j in range(NP):
                        n = 3 * s + j
                        W.wait_piece(dve, i, s, j)
                        if phase == "a":
                            g0 = tile_of(gate[0], i, 0, s)[:, cols(j)]
                            dve.tensor_tensor(g0, W.out(s, j), g0, ALU.mult).then_inc(W.free.sem, 1)
                        elif phase == "b":
                            g0, g1 = (tile_of(g, i, A_END, s)[:, cols(j)] for g in gate)
                            dve.wait_ge(m_lo.sem, m_lo.at(i - A_END, n - 1))
                            dve.tensor_tensor(m[n % 2][:, :], W.out(s, j), g1, ALU.mult).then_inc(W.free.sem, 1)
                            dve.wait_ge(W.free.sem, W.free.at(i, n + 1))
                            dve.tensor_tensor(m[n % 2][:, :], m[n % 2][:, :], g0, ALU.add).then_inc(merged.sem, 1)
                            dve.wait_ge(merged.sem, merged.at(i - A_END, n + 1))
                            copy(dve, tile_of(mh, i, A_END, s)[:, cols(j)], m[n % 2][:, :]).then_inc(m_hi.sem, 1)
                        else:
                            add_residual(dve, ch, W, i, s, j, tile_of(x, i, B_END, s), c["mod"], i * 2 + (s + 2 * KT - 2 * B_END), t8)
                if is_at(i, A_END - 1):
                    low(1)
                if phase == "out":
                    ch.reset()
            turns_of(dve, body)


def add_residual(dve, ch, W, turn, s, j, x, mod, tile, t8):
    ps = W.out(s, j)
    a0, n = j * TH, (TH if j < NP - 1 else T - 2 * TH)
    f0 = mod[:, bass.ds(tile, 1), 0:1].rearrange("p o n -> p (o n)")
    ins = dve.scalar_tensor_tensor(out=x[:, a0:a0 + n], in0=ps[:, 0:n], scalar=f0, in1=x[:, a0:a0 + n], op0=ALU.mult, op1=ALU.add)
    if j == NP - 1:
        ch(ins)
        dve.wait_ge(W.free.sem, W.free.at(turn, 3 * s))
        ch(dve.tensor_tensor(t8[:, :], ps[:, n:TH], mod[:, bass.ds(tile, 1), 1:CS].rearrange("p o n -> p (o n)"), ALU.mult))
        ch.sync()
        ins = dve.tensor_tensor(x[:, T:NT], x[:, T:NT], t8[:, :], ALU.add)
    ins.then_inc(W.free.sem, 1)


GROUP = 2
N_GROUPS = FT // GROUP
FFN_TURNS = (N_GROUPS - 1) // 2
HALF_TILES = ("up", "up", "down", "up", "up", "down")
DOWN_OUT = KT // 2
UP_PIECES, DOWN_PIECES = NP, NP * DOWN_OUT
TILE_PIECES = [UP_PIECES if t == "up" else DOWN_PIECES for t in HALF_TILES]
FIRST_PIECE = [sum(TILE_PIECES[:t]) for t in range(len(HALF_TILES) + 1)]
HALF_PIECES = FIRST_PIECE[-1]
PIECE_KIND = [HALF_TILES[t] for t in range(len(HALF_TILES)) for _ in range(TILE_PIECES[t])] * 2
BEFORE_UP = 2 * GROUP * UP_PIECES
BANKS = 8
assert N_GROUPS == 2 * FFN_TURNS + 1 and (2 * HALF_PIECES) % BANKS == 0


class Span:

    def __init__(self, turn, half=0):
        self.turn, self.half = turn, half

    def __call__(self, sig, k):
        return sig.before(k) if self.turn is None else sig.at(self.turn, self.half * (sig.per // 2) + k)

    def first(self, t):
        return UP_PIECES * t if self.turn is None else FIRST_PIECE[t]

    def bank(self, n):
        return (n if self.turn is None else BEFORE_UP + self.half * HALF_PIECES + n) % BANKS

    def bank_free(self, eng, n, up_free, down_free):
        if self.turn is None:
            return eng.wait_ge(up_free.sem, up_free.before(n - BANKS + 1))
        m = self.half * HALF_PIECES + n - BANKS
        kind = PIECE_KIND[m]
        sig = up_free if kind == "up" else down_free
        count = PIECE_KIND[:m % len(PIECE_KIND) + 1].count(kind)
        eng.wait_ge(sig.sem, sig.at(self.turn, count if m >= 0 else count - sig.per))


class LastSpan(Span):

    def first(self, t):
        return DOWN_PIECES * t

    def bank_free(self, eng, n, up_free, down_free):
        if n < BANKS:
            return super().bank_free(eng, n, up_free, down_free)
        eng.wait_ge(down_free.sem, self(down_free, n - BANKS + 1))


def ffn_stage(nc, a, o, c, x, hh, hl, acc, slots):
    with Stage(c) as ctx:
        raw, whi, wlo = slots
        mem = Memory(nc, "f", R_SQ + WIDE // KT)
        ah, al = ([mem(f"{n}{b}", [P, GROUP, NT], F32R) for b in range(2)] for n in ("act_hi", "act_lo"))
        u = [mem(f"u{s}", [P, 2 + NT]) for s in range(2)]
        y = [mem(f"y{s}", [P, NT]) for s in range(2)]
        e = mem("e", [P, NT])
        old = mem("old", [P, 2 * FT, 2, NS])
        new = mem("new", [P, 2 * FT, 2 + NS])
        cv = mem("cv", [P, 4 * 2 * FT])
        t8 = mem("t8", [P, NS])
        ps = ctx.enter_context(nc.psum_tensor("f_ps", [P, BANKS, 512], F32))

        def S(n, per, **k):
            return Sig(ctx, nc, f"f_{n}", per=per, **k)

        loaded = [S(f"w_loaded{s}", 6, pre=2, step=16) for s in range(2)]
        hi_done, lo_done = S("w_hi_done", 12, pre=4, init=2), S("w_lo_done", 12, pre=4, init=2)
        done = S("piece_done", 2 * HALF_PIECES, pre=BEFORE_UP, init=4)
        up_free = S("up_piece_free", 24, pre=BEFORE_UP, init=BANKS)
        down_free = S("down_piece_free", 48, init=BANKS)
        conved = S("conved", 8, pre=4, init=2)
        e_raw, e_cut, e_sig = S("e_raw", 4, pre=2), S("e_cut", 4, pre=2), S("e_sig", 4, pre=2)
        act_f, act_hi, act_lo = S("act", 4, pre=2, init=1), S("act_hi", 4, pre=2, init=1), S("act_lo", 4, pre=2, init=1)
        old_in, stored = S("old_in", 0, step=16), S("stored", 0, step=16)
        mean, mean_in = mem("mean", [P, P]), S("mean_in", 0, step=16)
        ms_summed, ln_done, rstd = (S(n, 0) for n in ("ms_summed", "ln", "rstd"))
        normed, norm_hi, norm_lo = S("normed", 0), S("norm_hi", 0), S("norm_lo", 0)
        block = ctx.enter_context(nc.Block())
        wt = a["w_ffn"]

        def loaded_at(at, t):
            return at(loaded[t % 2], t // 2 + 1)

        def load(sp, at, t, src):
            sp.wait_ge(hi_done.sem, at(hi_done, t - 1))
            sp.wait_ge(lo_done.sem, at(lo_done, t - 1))
            sp.dma_start(raw[t % 2][:, :], flat(src)).then_inc(loaded[t % 2].sem, 16)

        first, last = Span(None), LastSpan(FFN_TURNS)

        def turns_of(eng, half):
            with eng.Fori(0, FFN_TURNS) as i:
                for h in range(2):
                    half(Span(i, h))

        @block.sync
        def _(sp):
            sp.dma_start(mean[:, :], a["ones1024"]).then_inc(mean_in.sem, 16)
            for s in range(2):
                sp.sem_inc(loaded[s].sem, 16)
            for t in range(2, 4):
                load(sp, first, t, wt[t:t + 1])
            sp.dma_start(old[:, :, :, :], a["sconv"]).then_inc(old_in.sem, 16)

            def half(at):
                for t in range(6):
                    load(sp, at, t, wt[bass.ds(at.turn * 12 + (4 + at.half * 6 + t), 1)])
            turns_of(sp, half)
            for t in range(2):
                load(sp, last, t, wt[4 + 12 * FFN_TURNS + t:5 + 12 * FFN_TURNS + t])
            sp.wait_ge(conved.sem, last(conved, 0))
            sp.wait_ge(old_in.sem, 16)
            sp.dma_start(o["conv"], new[:, :, :]).then_inc(stored.sem, 16)
            sp.dma_start(o["conv_old"], old[:, :, 1, :]).then_inc(stored.sem, 16)
            for n in range(KT):
                sp.wait_ge(down_free.sem, last(down_free, NP * (n + 1)))
                sp.dma_start(flat(o["y"][n:n + 1]), x[:, n, :]).then_inc(stored.sem, 16)
            sp.wait_ge(stored.sem, 16 * (2 + KT))

        @block.scalar
        def _(act):
            act.preload_act_table_set(TABLES)
            for sig in (hi_done, up_free):
                sig.start(act)
            ch = Chain(ctx, nc, act, "f_act_chain")

            def split(at, t):
                act.wait_ge(loaded[t % 2].sem, loaded_at(at, t))
                before = at.first(t - 1) if t else -1
                act.wait_ge(done.sem, at(done, before))
                act.activation(whi[t % 2][:, :], raw[t % 2][:, :], ACT.Copy).then_inc(hi_done.sem, 1)

            def read(at, pair, s, piece):
                act.wait_ge(conved.sem, at(conved, 2 * pair + s - 1))
                for j in range(NP):
                    act.wait_ge(done.sem, at(done, piece + j + 1))
                    act.activation(u[s][:, 2 + j * TH:2 + (j + 1) * TH], ps[:, at.bank(piece + j), 0:TH], ACT.Copy).then_inc(up_free.sem, 1)

            def silu(at, pair):
                act.wait_ge(conved.sem, at(conved, 2 * pair + 1))
                act.wait_ge(act_f.sem, at(act_f, pair))
                act.activation(e[:, :], y[0][:, :], ACT.Exp, scale=-1.0).then_inc(e_raw.sem, 1)
                act.wait_ge(e_cut.sem, at(e_cut, pair + 1))
                ch(act.activation(e[:, :], e[:, :], ACT.Ln))
                ch.sync()
                act.activation(e[:, :], e[:, :], ACT.Exp, scale=-1.0).then_inc(e_sig.sem, 1)

            act.sem_inc(hi_done.sem, 1)
            split(first, 1)
            act.wait_ge(ms_summed.sem, 1)
            for j in range(NP):
                ins = act.activation(e[:, cols(j)], ps[:, j, 0:TH], ACT.Ln, bias=c["eps"][:, 0:1])
                ins.then_inc(ln_done.sem, 1)
            act.wait_ge(ln_done.sem, NP)
            act.activation(e[:, :], e[:, :], ACT.Exp, scale=-0.5).then_inc(rstd.sem, 1)
            for k in range(KT):
                act.wait_ge(normed.sem, k + 1)
                act.activation(hh[:, k, :], y[k % 2][:, :], ACT.Copy).then_inc(norm_hi.sem, 1)
            split(first, 2)
            read(first, 0, 0, first.first(0))
            split(first, 3)
            read(first, 0, 1, first.first(1))
            silu(first, 0)
            read(first, 1, 0, first.first(2))
            split(first, 4)
            read(first, 1, 1, first.first(3))
            silu(first, 1)
            ch.reset()

            def half(at):
                for pair in range(2):
                    t = 3 * pair
                    split(at, t + 1)
                    read(at, pair, 0, at.first(t))
                    split(at, t + 2)
                    read(at, pair, 1, at.first(t + 1))
                    split(at, t + 3)
                    silu(at, pair)
                if at.half:
                    ch.reset()
            turns_of(act, half)
            split(last, 1)

        @block.tensor
        def _(pe):
            done.start(pe)

            def up(at, t):
                for j in range(NP):
                    n = at.first(t) + j
                    if j == 0:
                        pe.wait_ge(hi_done.sem, at(hi_done, t + 1))
                        pe.wait_ge(lo_done.sem, at(lo_done, t + 1))
                    at.bank_free(pe, n, up_free, down_free)
                    product(pe, ps[:, at.bank(n), 0:TH], whi[t % 2], wlo[t % 2], hh, hl, KT, cols(j)).then_inc(done.sem, 1)

            def down(at, t, buf):
                pe.wait_ge(hi_done.sem, at(hi_done, t + 1))
                pe.wait_ge(lo_done.sem, at(lo_done, t + 1))
                if t < 3:
                    pe.wait_ge(act_hi.sem, at(act_hi, 0))
                    pe.wait_ge(act_lo.sem, at(act_lo, 0))
                for q in range(DOWN_OUT):
                    w = slice(q * GROUP * P, (q + 1) * GROUP * P)
                    for j in range(NP):
                        n = at.first(t) + q * NP + j
                        at.bank_free(pe, n, up_free, down_free)
                        product(pe, ps[:, at.bank(n), 0:TH], whi[t % 2][:, w], wlo[t % 2][:, w], ah[buf], al[buf], GROUP, cols(j))\
                            .then_inc(done.sem, 1)

            pe.wait_ge(mean_in.sem, 16)
            for j in range(NP):
                ins = pe.matmul(ps[:, j, 0:TH], mean[:, :], acc[:, cols(j)], start=True, stop=True)
            ins.then_inc(ms_summed.sem, 1)
            pe.wait_ge(ln_done.sem, NP)
            pe.wait_ge(hi_done.sem, first(hi_done, 2))
            pe.wait_ge(lo_done.sem, first(lo_done, 2))
            for k in range(KT):
                pe.wait_ge(norm_hi.sem, k + 1)
                pe.wait_ge(norm_lo.sem, k + 1)
                w = slice(k * P, (k + 1) * P)
                for t in range(2):
                    for j in range(NP):
                        for q, (wp, xp) in enumerate(((whi, hh), (whi, hl), (wlo, hh))):
                            ins = pe.matmul(ps[:, t * NP + j, 0:TH], wp[t][:, w], xp[:, k, cols(j)], start=(k == 0 and q == 0),
                                            stop=(k == KT - 1 and q == 2))
                        if k == KT - 1:
                            ins.then_inc(done.sem, 1)
            for t in range(2, 4):
                up(first, t)
            pe.wait_ge(up_free.sem, first(up_free, BEFORE_UP))

            def half(at):
                for t, kind in enumerate(HALF_TILES):
                    up(at, t) if kind == "up" else down(at, t, at.half)
            turns_of(pe, half)
            for t in range(2):
                down(last, t, 0)

        @block.gpsimd
        def _(pool):
            ctx.clear_last(pool)
            lo_done.start(pool)
            act_lo.start(pool)

            def split(at, t):
                pool.wait_ge(loaded[t % 2].sem, loaded_at(at, t))
                pool.wait_ge(hi_done.sem, at(hi_done, t + 1))
                pool.wait_ge(done.sem, at(done, at.first(t - 1) if t else -1))
                pool.tensor_tensor(wlo[t % 2][:, :], raw[t % 2][:, :], whi[t % 2][:, :].bitcast(F32), ALU.subtract)\
                    .then_inc(lo_done.sem, 1)

            def act_low(at, pair, buf):
                pool.wait_ge(act_hi.sem, at(act_hi, pair + 1))
                pool.tensor_tensor(al[buf][:, pair, :], y[0][:, :], ah[buf][:, pair, :].bitcast(F32), ALU.subtract).then_inc(act_lo.sem, 1)

            pool.sem_inc(lo_done.sem, 1)
            split(first, 1)
            for k in range(KT):
                pool.wait_ge(normed.sem, k + 1)
                pool.wait_ge(norm_hi.sem, k + 1)
                pool.tensor_tensor(hl[:, k, :], y[k % 2][:, :], hh[:, k, :].bitcast(F32), ALU.subtract).then_inc(norm_lo.sem, 1)
            split(first, 2)
            split(first, 3)
            act_low(first, 0, 0)
            split(first, 4)
            act_low(first, 1, 0)

            def half(at):
                for t in range(len(HALF_TILES)):
                    split(at, t + 1)
                    if HALF_TILES[t] == "down":
                        act_low(at, t // 3, 1 - at.half)
            turns_of(pool, half)
            split(last, 1)

        @block.vector
        def _(dve):
            for sig in (down_free, conved, act_f, act_hi):
                sig.start(dve)
            ch = Chain(ctx, nc, dve, "f_dve_chain")
            for s in range(2):
                ch(dve.memset(u[s][:, 0:2], 0.0))
            n_cv, at0 = 2 * FT, VEC["conv_w"][0]
            ch(dve.tensor_copy(cv[:, :], c["vec"][:, at0:at0 + 4 * n_cv]))
            mod, vec, shift, scale = c["mod"], c["vec"], 3 * KT, 4 * KT
            for k in range(KT):
                g = VEC["ffn_g"][0] + k
                ch(dve.tensor_scalar(mod[:, scale + k, :], mod[:, scale + k, :], 1.0, vec[:, g:g + 1], ALU.add, ALU.mult))
            ch.sync()
            dve.wait_ge(rstd.sem, 1)
            for k in range(KT):
                if k >= 2:
                    dve.wait_ge(norm_hi.sem, k - 1)
                    dve.wait_ge(norm_lo.sem, k - 1)
                yk = y[k % 2]
                ch(dve.tensor_tensor(yk[:, :], x[:, k, :], e[:, :], ALU.mult))
                ch.sync()
                ch(dve.tensor_tensor(yk[:, T:NT], yk[:, T:NT], mod[:, scale + k, 1:CS], ALU.mult))
                ch(dve.tensor_scalar(yk[:, 0:T], yk[:, 0:T], mod[:, scale + k, 0:1], mod[:, shift + k, 0:1], ALU.mult, ALU.add))
                ch.sync()
                dve.tensor_tensor(yk[:, T:NT], yk[:, T:NT], mod[:, shift + k, 1:CS], ALU.add).then_inc(normed.sem, 1)
            dve.wait_ge(old_in.sem, 16)
            dve.wait_ge(norm_hi.sem, KT)
            dve.wait_ge(norm_lo.sem, KT)
            ch.sync()

            def conv(at, tile, pair, s):
                w = [cv[:, bass.ds(tile + r * n_cv, 1)] for r in range(4)]
                us, ys = u[s], y[s]
                st = [old[:, bass.ds(tile, 1), r, :].rearrange("p o n -> p (o n)") for r in range(2)]
                dve.wait_ge(up_free.sem, at(up_free, NP * (2 * pair + s + 1)))
                dve.wait_ge(act_hi.sem, at(act_hi, pair))
                dve.wait_ge(act_lo.sem, at(act_lo, pair))
                ch(dve.tensor_scalar(ys[:, 0:T], us[:, 0:T], w[0], w[3], ALU.mult, ALU.add))
                ch(dve.tensor_scalar(ys[:, T:NT], st[0], w[0], w[3], ALU.mult, ALU.add))
                ch.sync()
                ch(dve.scalar_tensor_tensor(out=ys[:, 0:T], in0=us[:, 1:1 + T], scalar=w[1], in1=ys[:, 0:T], op0=ALU.mult, op1=ALU.add))
                ch(dve.scalar_tensor_tensor(out=ys[:, T:NT], in0=st[1], scalar=w[1], in1=ys[:, T:NT], op0=ALU.mult, op1=ALU.add))
                ch(copy(dve, new[:, bass.ds(tile, 1), :].rearrange("p o n -> p (o n)"), us[:, T:T + 2 + NS]))
                ch.sync()
                dve.scalar_tensor_tensor(out=ys[:, :], in0=us[:, 2:2 + NT], scalar=w[2], in1=ys[:, :], op0=ALU.mult,
                                         op1=ALU.add).then_inc(conved.sem, 1)

            def cut(at, pair):
                dve.wait_ge(e_raw.sem, at(e_raw, pair + 1))
                dve.tensor_scalar(e[:, :], e[:, :], BIG, 1.0, ALU.min, ALU.add).then_inc(e_cut.sem, 1)

            def gate(at, pair, buf):
                dve.wait_ge(e_sig.sem, at(e_sig, pair + 1))
                dve.wait_ge(conved.sem, at(conved, 2 * pair + 2))
                ch(dve.tensor_tensor(y[0][:, :], y[0][:, :], e[:, :], ALU.mult))
                ch.sync()
                dve.tensor_tensor(y[0][:, :], y[0][:, :], y[1][:, :], ALU.mult).then_inc(act_f.sem, 1)
                dve.wait_ge(act_f.sem, at(act_f, pair + 1))
                copy(dve, ah[buf][:, pair, :], y[0][:, :]).then_inc(act_hi.sem, 1)

            def residual(at, t, q):
                n_out = (t // 3 if at is not last else t) * DOWN_OUT + q
                xt, m = x[:, n_out, :], c["mod"][:, 5 * KT + n_out, :]
                for j in range(NP):
                    n, k = at.first(t) + q * NP + j, n_out * NP + j
                    dve.wait_ge(done.sem, at(done, n + 1))
                    dve.wait_ge(down_free.sem, at(down_free, k))
                    b, a0, w = ps[:, at.bank(n), :], j * TH, (TH if j < NP - 1 else T - 2 * TH)
                    ins = dve.scalar_tensor_tensor(out=xt[:, a0:a0 + w], in0=b[:, 0:w], scalar=m[:, 0:1], in1=xt[:, a0:a0 + w],
                                                   op0=ALU.mult, op1=ALU.add)
                    if j == NP - 1:
                        ch(ins)
                        ch(dve.tensor_tensor(t8[:, :], b[:, w:TH], m[:, 1:CS], ALU.mult))
                        ch.sync()
                        ins = dve.tensor_tensor(xt[:, T:NT], xt[:, T:NT], t8[:, :], ALU.add)
                    ins.then_inc(down_free.sem, 1)

            for pair in range(2):
                conv(first, 2 * pair, pair, 0)
                conv(first, 2 * pair + 1, pair, 1)
                cut(first, pair)
                gate(first, pair, 0)
            ch.reset()

            def half(at):
                for pair in range(2):
                    for s in range(2):
                        conv(at, at.turn * 8 + (4 * (1 + at.half) + 2 * pair + s), pair, s)
                    cut(at, pair)
                    t = 2 + 3 * pair
                    residual(at, t, 0)
                    residual(at, t, 1)
                    if pair == 0:
                        dve.wait_ge(done.sem, at(done, 0))
                    gate(at, pair, 1 - at.half)
                    for q in range(2, DOWN_OUT):
                        residual(at, t, q)
                if at.half:
                    ch.reset()
            turns_of(dve, half)
            for t in range(2):
                for q in range(DOWN_OUT):
                    residual(last, t, q)


def program(nc, a, o):
    keep = Memory(nc, "keep", BASE, R1)
    c = {n: keep(n, [P, P]) for n in ("ident", "ones128", "ones")}
    c.update(vec=keep("vec", [P, VEC_W]), mod=keep("mod", [P, 6 * KT, CS]), csil=keep("csil", [P, KT, CS]),
             lam=keep("lam", [P, 8]), lb=keep("lb", [P, 2, H]), eps=keep("eps", [P, 1]))
    for n in ("q", "k", "v", "qh", "kk", "f", "ib", "og", "oa", "ob"):
        c["s_" + n] = keep("s_" + n, [P, H, NS])

    def scratch(name, dt):
        return nc.dram_tensor(name, (KT, P, NT), dt, kind="Internal").ap()

    d = {b: scratch(b, F32) for b in ("oa", "ob")}
    d["q_rows"], d["v_rows"] = (nc.dram_tensor(n, (NS, D), F32, kind="Internal").ap() for n in ("q_rows", "v_rows"))

    def wide(name, at, dt=F32, n=KT):
        return nc.alloc_sbuf_tensor_at(name, [P, n, NT], dt, offset=at)

    xh, xl = wide("xn_hi", R1, F32R), wide("xn_lo", R1 + WIDE, F32R)
    early = early_tensors(nc)
    x = wide("x", early["mem"].off)
    norm_stage(nc, a, c, x, xh, xl, Memory(nc, "n1", early["mem"].off + WIDE), early)
    heads_stage(nc, a, o, c, d, xh, xl, early)
    gate = [wide("gate_a", R3), wide("gate_b", R3 + WIDE)]
    slots = [early[n][:2] for n in ("raw", "hi", "lo")]
    gates_stage(nc, a, o, c, d, xh, xl, gate, slots)
    mh, ml = wide("merged_hi", R3, F32R), wide("merged_lo", R3 + WIDE, F32R)
    oh, ol = wide("branch_hi", R1, F32R), wide("branch_lo", R1 + WIDE, F32R)
    x1, acc = wide("x1", R_X), nc.alloc_sbuf_tensor_at("squares", [P, NT], F32, offset=R_SQ)
    mix_stage(nc, a, c, d, x1, oh, ol, gate, mh, ml, acc, slots)
    hh, hl = wide("hn_hi", R1, F32R), wide("hn_lo", R1 + WIDE, F32R)
    ffn_stage(nc, a, o, c, x1, hh, hl, acc, slots)


def constants():
    f32 = np.float32
    k = {"ident": np.eye(P, dtype=f32), "ones": np.ones((P, P), f32), "ones128": np.full((P, P), 1 / P, f32),
         "ones1024": np.full((P, P), 1 / D, f32)}
    r = np.arange(P)
    k["blk"] = ((r[:, None] // DH) == (r[None, :] // DH)).astype(f32) / DH
    rot = np.zeros((P, P), f32)
    half = DH // 2
    for m in range(P):
        if m % DH < half:
            rot[m + half, m] = -1.0
        else:
            rot[m - half, m] = 1.0
    k["rot"] = rot
    inv = (10000.0 ** (-np.arange(half) / half)).astype(f32)
    pos = np.concatenate([np.arange(T), np.full(NS, PAST)]).astype(f32)
    ang = (pos[:, None] * inv[None, :]).astype(f32).astype(np.float64)
    k["cos"] = np.ascontiguousarray(np.cos(ang).astype(f32).T[r % half])
    k["sin"] = np.ascontiguousarray(np.sin(ang).astype(f32).T[r % half])
    k["causal"] = np.where(r[None, :] <= r[:, None], 0.0, -1e30).astype(f32)
    m = np.zeros((P, LEVELS * HALF), np.uint32)
    for lv in range(LEVELS):
        b = 1 << lv
        for j in range(HALF):
            first = (j // b) * 2 * b
            m[first:first + b, lv * HALF + j] = 1
    k["lmask"] = m
    hc = np.arange(2 * H)
    k["comb"] = (hc[:, None] // 2 == np.arange(H)[None, :]).astype(f32)
    k["coef"] = np.stack([hc % 2 == 0, hc % 2 == 1, 0 * hc], 1).astype(f32)
    k["blk2"] = (r[:, None] // DH == np.arange(2)[None, :]).astype(f32)
    return k


def kernel(**inputs):
    import concourse.bacc as bacc
    from concourse.bass_utils import run_bass_kernel_spmd

    x = {n: np.asarray(v) for n, v in inputs.items()}
    f32 = np.float32

    def rows(v):
        return v.reshape(-1, P).T

    def tiles(w, order=None):
        kt, mt = w.shape[0] // P, w.shape[1] // P
        t = w.reshape(kt, P, mt, P).transpose(2, 1, 0, 3)
        return np.ascontiguousarray(t if order is None else t[order]).reshape(-1, P, kt * P)

    a = constants()
    tokens = np.concatenate([x["x_prompt"].reshape(T, D), x["x_sample"].reshape(NS, D)])
    a["xT"] = tokens.T.reshape(KT, P, NT).transpose(1, 0, 2)
    a["cT"] = np.concatenate([x["c_prompt"], x["c_sample"]]).T.reshape(KT, P, CS).transpose(1, 0, 2)
    a["w_ada"] = tiles(x["w_ada"][0])
    at = dict(zip(("q", "k", "v", "qh", "f", "ib", "og", "ga", "gb"), range(0, 9 * H, H)))
    order = [at[n] for n in ("q", "k", "v")]
    for h in range(H):
        order += [at[n] + h for n in ("f", "qh", "ib", "og")]
        if h + 1 < H:
            order += [at[n] + h + 1 for n in ("q", "k", "v")]
    gates = [at[n] + h for h in range(H) for n in ("ga", "gb")]
    a["w_in"] = tiles(x["w_in"][0], order + order[:3] + gates)
    a["w_mix"] = np.concatenate([tiles(x[n][0]) for n in ("w_branch_a", "w_branch_b", "w_out")])
    pairs = [s * FT + f for f in range(FT) for s in range(2)]
    up = tiles(x["w_up"][0], pairs)
    down = x["w_down"][0].reshape(N_GROUPS, GROUP, P, 2, KT // 2, P).transpose(0, 3, 2, 4, 1, 5).reshape(N_GROUPS, 2, P, KT * P)
    ffn = [up[0:4]]
    for g in range(1, N_GROUPS):
        ffn += [up[4 * g:4 * g + 2], down[g - 1, 0:1], up[4 * g + 2:4 * g + 4], down[g - 1, 1:2]]
    a["w_ffn"] = np.concatenate(ffn + [down[-1]])
    conv_w = [rows(x["conv_w"][0, r])[:, pairs] for r in range(3)]
    lams = np.concatenate([x[n][0] for n in ("lambda_q1", "lambda_k1", "lambda_q2", "lambda_k2")])
    a["vec"] = np.concatenate(
        [rows(x["b_ada"][0]), rows(x["rms_mix_g"][0]), rows(x["rms_ffn_g"][0]), np.tile(x["q_norm_g"][0], 2)[:, None],
         np.tile(x["k_norm_g"][0], 2)[:, None], x["subln_g"][0][:, None], x["hgrn_norm_g"][0][:, None],
         rows(x["lb_logits"][0]), rows(x["lb_logits"][1])] + conv_w
        + [rows(x["conv_b"][0])[:, pairs], np.broadcast_to(lams, (P, 4 * DH))], axis=1)
    a["sconv"] = x["state_conv"][0].reshape(NS, 2, 2 * FT, P)[:, :, pairs].transpose(3, 2, 1, 0)
    a["state"] = x["state_hgrn"][0].transpose(1, 2, 0, 3).reshape(H, P, NS * P)
    a["cache_k"] = x["cache_k"][0].reshape(POOL_PAGES, P, D)
    a["cache_v"] = x["cache_v"][0].reshape(POOL_PAGES, P, D)
    a["pages"] = x["page_table"].reshape(1, NS * PAGES)
    outs = {"y": (KT, P, NT), "k": (H, P, NT), "v": (H, P, NT), "state": (H, P, P), "s_state": (H, P, NS * P),
            "conv": (P, 2 * FT, 2 + NS), "conv_old": (P, 2 * FT, NS)}

    nc = bacc.Bacc("TRN2", target_bir_lowering=False, num_devices=1, dynamic_dma_scratch_size=DMA_SCRATCH)
    arrays, ins, res = {}, {}, {}
    for n, v in a.items():
        v = np.ascontiguousarray(v)
        arrays[f"in_{n}"] = v
        ins[n] = nc.dram_tensor(f"in_{n}", v.shape, mybir.dt.from_np(v.dtype), kind="ExternalInput").ap()
    for n, shape in outs.items():
        res[n] = nc.dram_tensor(f"out_{n}", shape, F32, kind="ExternalOutput").ap()
    program(nc, ins, res)
    r = run_bass_kernel_spmd(nc, [arrays], core_ids=[0]).results[0]
    r = {n: np.asarray(r[f"out_{n}"]) for n in outs}

    def per_token(v):
        return v.transpose(2, 0, 1).reshape(NT, -1)

    y, k, v = per_token(r["y"]), per_token(r["k"]), per_token(r["v"])
    back = np.argsort(pairs)
    conv = r["conv"][:, back].transpose(2, 1, 0).reshape(2 + NS, 2 * FF)
    old = r["conv_old"][:, back].transpose(2, 1, 0).reshape(NS, 2 * FF)
    C = np.ascontiguousarray
    return (C(y[:T].reshape(1, T, D)), C(y[T:].reshape(NS, 1, D)),
            C(k[:T].reshape(1, 1, T, H, 2, DH)), C(v[:T].reshape(1, 1, T, H, P)),
            C(r["state"].reshape(1, 1, H, P, P)), C(conv[:2].reshape(1, 1, 2, 2 * FF)),
            C(k[T:].reshape(1, NS, 1, H, 2, DH)), C(v[T:].reshape(1, NS, 1, H, P)),
            C(r["s_state"].reshape(H, P, NS, P).transpose(2, 0, 1, 3)[None]),
            C(np.stack([old, conv[2:]], 1)[None]))
```
